# Optimizing a Trainium2 kernel written in Bass

```python
import math
import jax
import jax.numpy as jnp
from jax import lax
import numpy as np

D_MODEL = 1024
BATCH = 1
SEQ = 512
DEPTH = 2

N_A_LAYERS = DEPTH // 2
N_B_LAYERS = DEPTH - N_A_LAYERS
D_FF = 2816
NORM_EPS = 1e-6
FFN_RES_WEIGHT = 0.5

GDN_DK = 128
GDN_DV = 128
GDN_HEADS = D_MODEL // GDN_DV
GDN_CONV = 4
GDN_CHUNK = 64

DIFF_DK = 64
DIFF_DV = 2 * DIFF_DK
DIFF_HEADS = D_MODEL // DIFF_DV
ROPE_THETA = 500000.0
ROPE_DIM = DIFF_DK // 4
Q_BLOCK = 128
POS_OFFSET_MAX = 1024

kernel_name = "yoco_gdn_diffattn_macaron"

def rmsnorm(x, g):
    xf = x.astype(jnp.float32)
    y = xf * lax.rsqrt(jnp.mean(xf * xf, axis=-1, keepdims=True) + NORM_EPS)
    return (y * g.astype(jnp.float32)).astype(x.dtype)

def swiglu(h, w_gate_up, w_down):
    gate, up = jnp.split(h @ w_gate_up, 2, axis=-1)
    return (jax.nn.silu(gate) * up) @ w_down

def causal_depthwise_conv(x, w):
    k_size, ch = w.shape
    return lax.conv_general_dilated(
        x, w[:, None, :].astype(x.dtype), window_strides=(1,),
        padding=((k_size - 1, 0),), dimension_numbers=("NWC", "WIO", "NWC"),
        feature_group_count=ch)

def l2norm(x):
    xf = x.astype(jnp.float32)
    return xf * lax.rsqrt(jnp.sum(xf * xf, axis=-1, keepdims=True) + NORM_EPS)

def gated_delta_rule(q, k, v, g, beta):
    f32 = jnp.float32
    q, k, v, g, beta = (a.astype(f32) for a in (q, k, v, g, beta))
    bsz, t_len, n_h, dk = q.shape
    dv = v.shape[-1]
    c = GDN_CHUNK
    n_c = t_len // c

    def chunks(a):
        return jnp.moveaxis(a.reshape((bsz, n_c, c) + a.shape[2:]), 2, 3)

    q = chunks(q) * (dk ** -0.5)
    k, v, g, beta = chunks(k), chunks(v), chunks(g), chunks(beta)
    G = jnp.cumsum(g, axis=-1)
    tri_incl = jnp.tril(jnp.ones((c, c), bool))
    tri_strict = jnp.tril(jnp.ones((c, c), bool), -1)
    diff = G[..., :, None] - G[..., None, :]
    decay = jnp.where(tri_incl, jnp.exp(jnp.where(tri_incl, diff, 0.0)), 0.0)

    kb = k * beta[..., None]
    A = jnp.where(tri_strict, jnp.einsum('bnhcd,bnhsd->bnhcs', kb, k) * decay, 0.0)
    L = A + jnp.eye(c, dtype=f32)
    rhs = jnp.concatenate([v * beta[..., None], kb * jnp.exp(G)[..., None]], axis=-1)
    sol = lax.linalg.triangular_solve(L, rhs, left_side=True, lower=True, unit_diagonal=True)
    u_base, w = sol[..., :dv], sol[..., dv:]
    qk = jnp.einsum('bnhcd,bnhsd->bnhcs', q, k) * decay
    q_dec = q * jnp.exp(G)[..., None]
    k_dec = k * jnp.exp(G[..., -1:] - G)[..., None]
    g_last = jnp.exp(G[..., -1])

    def step(S, xs):
        qd, kd, u0, w_c, qk_c, gl = xs
        u = u0 - jnp.einsum('bhcd,bhde->bhce', w_c, S)
        o = jnp.einsum('bhcd,bhde->bhce', qd, S) + jnp.einsum('bhcs,bhse->bhce', qk_c, u)
        S = S * gl[..., None, None] + jnp.einsum('bhcd,bhce->bhde', kd, u)
        return S, o

    xs = tuple(jnp.moveaxis(a, 1, 0) for a in (q_dec, k_dec, u_base, w, qk, g_last))
    S0 = jnp.zeros((bsz, n_h, dk, dv), f32)
    _, o = lax.scan(step, S0, xs)
    o = jnp.moveaxis(jnp.moveaxis(o, 0, 1), 3, 2)
    return o.reshape(bsz, t_len, n_h, dv)

def gdn_mixer(h, w_in, conv_w, a_log, dt_bias, out_norm, w_out):
    bsz, t_len, _ = h.shape
    hk = GDN_HEADS * GDN_DK
    hv = GDN_HEADS * GDN_DV
    proj = h @ w_in
    qkv = jax.nn.silu(causal_depthwise_conv(proj[..., :2 * hk + hv], conv_w))
    z = proj[..., 2 * hk + hv:2 * hk + 2 * hv]
    b = proj[..., 2 * hk + 2 * hv:2 * hk + 2 * hv + GDN_HEADS]
    a = proj[..., 2 * hk + 2 * hv + GDN_HEADS:]
    q = l2norm(qkv[..., :hk].reshape(bsz, t_len, GDN_HEADS, GDN_DK))
    k = l2norm(qkv[..., hk:2 * hk].reshape(bsz, t_len, GDN_HEADS, GDN_DK))
    v = qkv[..., 2 * hk:].reshape(bsz, t_len, GDN_HEADS, GDN_DV)
    beta = jax.nn.sigmoid(b.astype(jnp.float32))
    g = -jnp.exp(a_log.astype(jnp.float32)) * jax.nn.softplus(a.astype(jnp.float32) + dt_bias.astype(jnp.float32))
    o = gated_delta_rule(q, k, v, g, beta)
    zf = z.reshape(bsz, t_len, GDN_HEADS, GDN_DV).astype(jnp.float32)
    o = rmsnorm(o, out_norm) * jax.nn.silu(zf)
    return o.reshape(bsz, t_len, hv).astype(h.dtype) @ w_out

def rope_partial(x, pos):
    half = ROPE_DIM // 2
    inv_freq = 1.0 / (ROPE_THETA ** (jnp.arange(half, dtype=jnp.float32) / half))
    ang = pos.astype(jnp.float32)[..., None] * inv_freq
    cos = jnp.cos(ang)[:, :, None, :]
    sin = jnp.sin(ang)[:, :, None, :]
    xr = x[..., :ROPE_DIM].astype(jnp.float32)
    x1, x2 = xr[..., :half], xr[..., half:]
    rot = jnp.concatenate([x1 * cos - x2 * sin, x2 * cos + x1 * sin], axis=-1)
    return jnp.concatenate([rot.astype(x.dtype), x[..., ROPE_DIM:]], axis=-1)

def shared_kv(h, w_kv, pos):
    bsz, t_len, _ = h.shape
    kv = h @ w_kv
    k = kv[..., :2 * DIFF_HEADS * DIFF_DK].reshape(bsz, t_len, 2 * DIFF_HEADS, DIFF_DK)
    k = rope_partial(k, pos).reshape(bsz, t_len, DIFF_HEADS, 2, DIFF_DK)
    v = kv[..., 2 * DIFF_HEADS * DIFF_DK:].reshape(bsz, t_len, DIFF_HEADS, DIFF_DV)
    return k, v

def diff_attention(q, k, v, lam):
    bsz, t_len, n_h, _, dk = q.shape
    n_q = t_len // Q_BLOCK
    qb = jnp.moveaxis(q.reshape(bsz, n_q, Q_BLOCK, n_h, 2, dk), 1, 0)
    key_idx = jnp.arange(t_len)
    scale = dk ** -0.5

    def block(args):
        qi, i = args
        s = jnp.einsum('bqhmd,bkhmd->bhmqk', qi, k).astype(jnp.float32) * scale
        q_idx = i * Q_BLOCK + jnp.arange(Q_BLOCK)
        s = jnp.where(key_idx[None, :] <= q_idx[:, None], s, -jnp.inf)
        p = jax.nn.softmax(s, axis=-1)
        p = p[:, :, 0] - lam * p[:, :, 1]
        return jnp.einsum('bhqk,bkhe->bqhe', p.astype(v.dtype), v)

    o = lax.map(block, (qb, jnp.arange(n_q)))
    return jnp.moveaxis(o, 0, 1).reshape(bsz, t_len, n_h, v.shape[-1])

def diff_mixer(h, pos, k_sh, v_sh, w_q, lam_params, subln, w_out, lam_init):
    bsz, t_len, _ = h.shape
    q = (h @ w_q).reshape(bsz, t_len, 2 * DIFF_HEADS, DIFF_DK)
    q = rope_partial(q, pos).reshape(bsz, t_len, DIFF_HEADS, 2, DIFF_DK)
    lp = lam_params.astype(jnp.float32)
    lam = jnp.exp(jnp.sum(lp[0] * lp[1])) - jnp.exp(jnp.sum(lp[2] * lp[3])) + lam_init
    o = diff_attention(q, k_sh, v_sh, lam)
    o = rmsnorm(o, subln) * (1.0 - lam_init)
    return o.reshape(bsz, t_len, DIFF_HEADS * DIFF_DV) @ w_out

def setup_inputs(seed: int = 0) -> dict:
    key = jax.random.key(seed)
    ks = jax.random.split(key, 24)
    f32 = jnp.float32

    def dense(k, shape, fan_in):
        return jax.random.normal(k, shape, f32) * fan_in ** -0.5

    def gain(k, shape):
        return 1.0 + 0.02 * jax.random.normal(k, shape, f32)

    x = jax.random.normal(ks[0], (BATCH, SEQ, D_MODEL), f32)
    offset = jax.random.randint(ks[1], (BATCH, 1), 0, POS_OFFSET_MAX, dtype=jnp.int32)
    positions = offset + jnp.arange(SEQ, dtype=jnp.int32)[None, :]
    gdn_in_w = 2 * GDN_HEADS * GDN_DK + 2 * GDN_HEADS * GDN_DV + 2 * GDN_HEADS
    gdn_conv_ch = 2 * GDN_HEADS * GDN_DK + GDN_HEADS * GDN_DV
    dt = jnp.exp(jax.random.uniform(ks[2], (N_A_LAYERS, GDN_HEADS), f32, math.log(1e-3), math.log(1e-1)))
    return {
        "x": x,
        "positions": positions,
        "ffn1_norm": gain(ks[3], (DEPTH, D_MODEL)),
        "ffn1_w_gate_up": dense(ks[4], (DEPTH, D_MODEL, 2 * D_FF), D_MODEL),
        "ffn1_w_down": dense(ks[5], (DEPTH, D_FF, D_MODEL), D_FF),
        "mix_norm": gain(ks[6], (DEPTH, D_MODEL)),
        "ffn2_norm": gain(ks[7], (DEPTH, D_MODEL)),
        "ffn2_w_gate_up": dense(ks[8], (DEPTH, D_MODEL, 2 * D_FF), D_MODEL),
        "ffn2_w_down": dense(ks[9], (DEPTH, D_FF, D_MODEL), D_FF),
        "gdn_w_in": dense(ks[10], (N_A_LAYERS, D_MODEL, gdn_in_w), D_MODEL),
        "gdn_conv": dense(ks[11], (N_A_LAYERS, GDN_CONV, gdn_conv_ch), GDN_CONV),
        "gdn_a_log": jnp.log(jax.random.uniform(ks[12], (N_A_LAYERS, GDN_HEADS), f32, 1.0, 16.0)),
        "gdn_dt_bias": dt + jnp.log(-jnp.expm1(-dt)),
        "gdn_out_norm": gain(ks[13], (N_A_LAYERS, GDN_DV)),
        "gdn_w_out": dense(ks[14], (N_A_LAYERS, GDN_HEADS * GDN_DV, D_MODEL), GDN_HEADS * GDN_DV),
        "kv_norm": gain(ks[15], (D_MODEL,)),
        "kv_w": dense(ks[16], (D_MODEL, 2 * DIFF_HEADS * DIFF_DK + DIFF_HEADS * DIFF_DV), D_MODEL),
        "diff_w_q": dense(ks[17], (N_B_LAYERS, D_MODEL, 2 * DIFF_HEADS * DIFF_DK), D_MODEL),
        "diff_lambda": 0.1 * jax.random.normal(ks[18], (N_B_LAYERS, 4, DIFF_DK), f32),
        "diff_subln": gain(ks[19], (N_B_LAYERS, DIFF_DV)),
        "diff_w_out": dense(ks[20], (N_B_LAYERS, DIFF_HEADS * DIFF_DV, D_MODEL), DIFF_HEADS * DIFF_DV),
        "final_norm": gain(ks[21], (D_MODEL,)),
    }

def reference(x, positions, ffn1_norm, ffn1_w_gate_up, ffn1_w_down, mix_norm, ffn2_norm,
              ffn2_w_gate_up, ffn2_w_down, gdn_w_in, gdn_conv, gdn_a_log, gdn_dt_bias,
              gdn_out_norm, gdn_w_out, kv_norm, kv_w, diff_w_q, diff_lambda, diff_subln,
              diff_w_out, final_norm):
    h = x
    k_sh = None
    v_sh = None
    for layer in range(DEPTH):
        h = h + FFN_RES_WEIGHT * swiglu(rmsnorm(h, ffn1_norm[layer]), ffn1_w_gate_up[layer], ffn1_w_down[layer])
        hn = rmsnorm(h, mix_norm[layer])
        if layer < N_A_LAYERS:
            i = layer
            h = h + gdn_mixer(hn, gdn_w_in[i], gdn_conv[i], gdn_a_log[i], gdn_dt_bias[i],
                              gdn_out_norm[i], gdn_w_out[i])
        else:
            i = layer - N_A_LAYERS
            lam_init = 0.8 - 0.6 * math.exp(-0.3 * layer)
            h = h + diff_mixer(hn, positions, k_sh, v_sh, diff_w_q[i], diff_lambda[i],
                               diff_subln[i], diff_w_out[i], lam_init)
        h = h + FFN_RES_WEIGHT * swiglu(rmsnorm(h, ffn2_norm[layer]), ffn2_w_gate_up[layer], ffn2_w_down[layer])
        if layer == N_A_LAYERS - 1:
            k_sh, v_sh = shared_kv(rmsnorm(h, kv_norm), kv_w, positions)
    return rmsnorm(h, final_norm)


_drawn_inputs = setup_inputs


def setup_inputs(seed=0):
    import zlib

    import numpy as np

    out = dict(_drawn_inputs(seed))
    spreads = {}
    factors = {'ffn1_norm': 4.109,
     'ffn2_norm': 5.43,
     'gdn_out_norm': 13.708,
     'kv_norm': 14.339,
     'diff_subln': 50.04,
     'final_norm': 7.525}
    for name, (base, spread) in spreads.items():
        noise = np.random.default_rng([zlib.crc32(name.encode()), seed]).standard_normal(out[name].shape)
        drawn = base * np.exp(spread * noise) if base else spread * noise
        out[name] = jnp.asarray(drawn.astype(out[name].dtype))
    for name, factor in factors.items():
        out[name] = (out[name] * factor).astype(out[name].dtype)
    return out
```

```python
import math
from contextlib import ExitStack

import concourse.bass as bass
from concourse import mybir

ALU = mybir.AluOpType
ACT = mybir.ActivationFunctionType
AX = mybir.AxisListType
F32 = mybir.dt.float32
F32R = mybir.dt.float32r
I32 = mybir.dt.int32

P = 128
D = 1024
T = 512
KD = D // P
TT = T // P
FF = 2816
FT = FF // P
FJ = FT // 2
H = 8
EPS = 1e-6
UNIT = 2048
LAM_INIT = 0.8 - 0.6 * math.exp(-0.3 * 1)
ROPE_THETA = 500000.0
ROPE_DIM = 16

U_FFN = 2 * FJ + FJ
U_IN, U_OUT, U_KV, U_Q = 2 * H, D * D // (P * UNIT), 8, 4
BASE = {}
_at = 0
for _name, _n in (("ffn0", U_FFN), ("gdn_in", U_IN), ("gdn_out", U_OUT), ("ffn1", U_FFN), ("kv", U_KV),
                  ("ffn2", U_FFN), ("q", U_Q), ("attn_out", U_OUT), ("ffn3", U_FFN)):
    BASE[_name] = _at
    _at += _n
N_UNITS = _at

C_IDENT, C_ONES, C_UPPER, C_ROPE, C_CAUSAL = (P * n for n in range(5))
C_GAIN = 5 * P
C_CONV = C_GAIN + 8 * KD
C_ALOG = C_CONV + H * 12
C_DTB = C_ALOG + H
C_ONORM = C_DTB + H
C_SUBLN = C_ONORM + 1
C_FREQ = C_SUBLN + 1
N_CST = C_FREQ + 1

A_ACT, A_SILU, A_KT, A_V = 0, FT * T, FT * T + 2 * T, FT * T + 2 * T + KD * T
N_ARENA = A_V + KD * T
A_EARLY = A_KT
A_GMASK = N_ARENA - 5 * P

HEAD_COLS = 7
K_G, K_CUM, K_BETA, K_NBETA, K_BEXPG, K_KDEC, K_LAST = range(HEAD_COLS)


def trunk_kernel(nc, weights, cst_in, masks_in, early_in, xT_in, pos_in, out):
    ctx = ExitStack()
    with ctx:
        def sb(name, shape, dt=F32):
            return ctx.enter_context(nc.sbuf_tensor(name, shape, dt))

        h = sb("h", [P, KD, T])
        xh = sb("xh", [P, KD, T], F32R)
        xl = sb("xl", [P, KD, T], F32R)
        raw = [sb(f"raw{n}", [P, UNIT]) for n in range(2)]
        whi = [sb(f"whi{n}", [P, UNIT], F32R) for n in range(2)]
        wlo = [sb(f"wlo{n}", [P, UNIT], F32R) for n in range(2)]
        ahi = [sb(f"ahi{n}", [P, 2, T], F32R) for n in range(2)]
        alo = [sb(f"alo{n}", [P, 2, T], F32R) for n in range(2)]
        arena = sb("arena", [P, N_ARENA])
        sq = sb("sq", [P, 2, T])
        acc = sb("acc", [P, T])
        xn = sb("xn", [P, 2, T])
        cst = sb("cst", [P, N_CST])
        bahi = sb("bahi", [P, KD, 16], F32R)
        balo = sb("balo", [P, KD, 16], F32R)
        hc = sb("hc", [P, HEAD_COLS, TT, H])
        hcur = sb("hcur", [P, HEAD_COLS, TT])
        cwh = sb("cwh", [P, 3, 4])
        gcur = sb("gcur", [P, 2, TT])
        st = sb("st", [P, 84])
        neglam = sb("neglam", [P, 4])
        bank = ctx.enter_context(nc.psum_tensor("bank", [P, 8, T], F32))

        ident = cst[:, C_IDENT:C_IDENT + P]
        ones = cst[:, C_ONES:C_ONES + P]
        upper = cst[:, C_UPPER:C_UPPER + P]
        rope_rot = cst[:, C_ROPE:C_ROPE + P]
        causal = cst[:, C_CAUSAL:C_CAUSAL + P]

        def slot(n, w=1):
            return arena[:, n * T:(n + w) * T]

        def c4(ap):
            return ap.rearrange("p (c t) -> p c t", c=TT)

        def over_t(cols):
            return cols.unsqueeze(2).to_broadcast([P, TT, P])

        def over_c(mask):
            return mask.unsqueeze(1).to_broadcast([P, TT, P])

        (G_QS, G_KS, G_Q, G_K, G_V, G_Z, G_DL, G_DU, G_D, G_EG, G_QD, G_QK, G_NA, G_N0, G_N0T, G_NAT,
         G_B1, G_B2, G_B3, G_N2, G_N2T, G_N4, G_TA, G_TB, G_KBG, G_KD, G_VB) = range(8, 35)
        PRE0 = 35 * T
        S0 = PRE0 + 3 * (T + 4)
        assert S0 + P <= A_GMASK
        pre3 = arena[:, PRE0:S0].rearrange("p (q t) -> p q t", q=3)
        pre_pad = pre3[:, :, 0:3]
        state = arena[:, S0:S0 + P]
        gm_lower, gm_diag, gm_b1, gm_b2, gm_b3 = (arena[:, A_GMASK + n * P:A_GMASK + (n + 1) * P] for n in range(5))

        sems = {}

        def S(name):
            if name not in sems:
                sems[name] = ctx.enter_context(nc.semaphore(name))
            return sems[name]

        block = ctx.enter_context(nc.Block())

        def past(count):
            return not isinstance(count, int) or count > 0

        def supply_hi(act, n, s):
            act.wait_ge(S(f"raw_landed{s}"), (n - s) * 8 + 16)
            if past(n - 1):
                act.wait_ge(S("unit_used"), n - 1)
            act.activation(whi[s][:, :], raw[s][:, :], ACT.Copy).then_inc(S("w_hi"), 1)

        def supply_lo(dve, n, s):
            dve.wait_ge(S("w_hi"), n + 1)
            dve.tensor_tensor(wlo[s][:, :], raw[s][:, :], whi[s][:, :].bitcast(F32), ALU.subtract)\
               .then_inc(S("w_lo"), 1)

        def mm3(pe, o, ah, al, bh, bl, start, stop):
            pe.matmul(o, ah, bh, start=start, stop=False)
            pe.matmul(o, ah, bl, start=False, stop=False)
            return pe.matmul(o, al, bh, start=False, stop=stop)

        def w_block(s, lo, width=P):
            return whi[s][:, lo:lo + width], wlo[s][:, lo:lo + width]

        def project_unit(pe, s, banks, x_build=None, part=None):
            a, b = part or (0, 2 * KD)
            for n in range(a, b):
                k, f = n // 2, n % 2
                if x_build is not None and f == 0:
                    pe.wait_ge(S("x_lo"), 8 * x_build + k + 1)
                last = mm3(pe, bank[:, banks[f], :], *w_block(s, k * 256 + f * P), xh[:, k, :], xl[:, k, :],
                           k == 0, k == KD - 1)
            return last

        def norm_act(act, r):
            for d in range(KD):
                if r == 0:
                    if d == 0:
                        act.wait_ge(S("x_landed"), 16)
                else:
                    act.wait_ge(S("h_ready"), 8 * (r - 1) + d + 1)
                if d == 0:
                    if past(6 * r):
                        act.wait_ge(S("sq_summed"), 6 * r)
                elif d == 1:
                    if past(r):
                        act.wait_ge(S("ss_done"), r)
                else:
                    act.wait_ge(S("sq_summed"), 6 * r + max(d - 2, 1))
                act.activation(sq[:, d % 2, :], h[:, d, :], ACT.Square).then_inc(S("sq_ready"), 1)
            act.wait_ge(S("var_ready"), r + 1)
            act.activation(st[:, 0:4], st[:, 4:8], ACT.Sqrt).then_inc(S("std_ready"), 1)

        def norm_pool(pool, r):
            if past(r):
                pool.wait_ge(S("ss_done"), r)
            if r == 4:
                pool.wait_ge(S("xn_ready"), 40)
            for d in range(1, KD - 1):
                pool.wait_ge(S("sq_ready"), 8 * r + d + 1)
                if d == 1:
                    ins = pool.tensor_tensor(acc[:, :], sq[:, 0, :], sq[:, 1, :], ALU.add)
                else:
                    pool.wait_ge(S("sq_summed"), 6 * r + d - 1)
                    ins = pool.tensor_tensor(acc[:, :], acc[:, :], sq[:, d % 2, :], ALU.add)
                ins.then_inc(S("sq_summed"), 1)

        def norm_pe(pe, r):
            pe.wait_ge(S("sq_summed"), 6 * (r + 1))
            pe.wait_ge(S("sq_ready"), 8 * (r + 1))
            if r:
                pe.wait_ge(S("h_ready"), 8 * (r - 1) + 2)
            for t in range(TT):
                pe.matmul(bank[:, 4, t:t + 1], acc[:, t * P:(t + 1) * P], ones[:, 0:1], start=True, stop=False)
                last = pe.matmul(bank[:, 4, t:t + 1], sq[:, 1, t * P:(t + 1) * P], ones[:, 0:1],
                                 start=False, stop=True)
            last.then_inc(S("ss_done"), 1)
            pe.wait_ge(S("rstd_ready"), r + 1)
            spread(pe, bank[:, 5, :], st[:, 16:20]).then_inc(S("rbc_done"), 1)

        def spread(pe, o, cols):
            for t in range(TT):
                last = pe.matmul(o[:, t * P:(t + 1) * P], cols[:, t:t + 1].to_broadcast([P, P]), ident,
                                 start=True, stop=True)
            return last

        class Steps:

            def __init__(self, eng, name, base=0):
                self.eng, self.name, self.base, self.n = eng, name, base, 0

            def link(self, ins):
                self.n += 1
                ins.then_inc(S(self.name), 1)
                self.eng.wait_ge(S(self.name), self.base + self.n)

        def newton(dve, steps, v, r0, tmp, o):
            steps.link(dve.tensor_tensor(tmp, r0, r0, ALU.mult))
            steps.link(dve.tensor_tensor(tmp, tmp, v, ALU.mult))
            steps.link(dve.tensor_scalar(tmp, tmp, -0.5, 1.5, ALU.mult, ALU.add))
            return dve.tensor_tensor(o, r0, tmp, ALU.mult)

        def norm_dve(dve, r):
            dve.wait_ge(S("ss_done"), r + 1)
            steps = Steps(dve, "small_step", 4 * r)
            dve.tensor_scalar(st[:, 4:8], bank[:, 4, 0:4], 1.0 / D, EPS, ALU.mult, ALU.add).then_inc(S("var_ready"), 1)
            dve.wait_ge(S("std_ready"), r + 1)
            steps.link(dve.reciprocal(st[:, 8:12], st[:, 0:4]))
            if past(r):
                dve.wait_ge(S("rbc_done"), r)
            newton(dve, steps, st[:, 4:8], st[:, 8:12], st[:, 12:16], st[:, 16:20]).then_inc(S("rstd_ready"), 1)

        def build_dve(dve, r, b, g):
            kept = b == 4
            rbc = acc[:, :] if kept else bank[:, 5, :]
            dve.wait_ge(S("rbc_done"), r + 1)
            if kept:
                dve.wait_ge(S("rbc_kept"), 1)
            for k in range(KD + 1):
                if k < KD:
                    if k >= 2:
                        dve.wait_ge(S("x_lo"), 8 * b + k - 1)
                    elif b:
                        dve.wait_ge(S("x_lo"), 8 * b)
                    dve.scalar_tensor_tensor(xn[:, k % 2, :], h[:, k, :], cst[:, C_GAIN + g * KD + k:C_GAIN + g * KD + k + 1],
                                             rbc, ALU.mult, ALU.mult).then_inc(S("xn_ready"), 1)
                if k:
                    dve.wait_ge(S("x_hi"), 8 * b + k)
                    dve.tensor_tensor(xl[:, k - 1, :], xn[:, (k - 1) % 2, :], xh[:, k - 1, :].bitcast(F32),
                                      ALU.subtract).then_inc(S("x_lo"), 1)

        def build_act(act, b, n_used):
            if past(n_used):
                act.wait_ge(S("unit_used"), n_used)
            for k in range(KD):
                act.wait_ge(S("xn_ready"), 8 * b + k + 1)
                act.activation(xh[:, k, :], xn[:, k % 2, :], ACT.Copy).then_inc(S("x_hi"), 1)

        def ffn_pe(pe, f, b, U):
            s = U % 2

            def gate(j, first=False):
                pe.wait_ge(S("w_lo"), U + 2 * j + 1)
                if past(FJ * f + j):
                    pe.wait_ge(S("silu_ready"), FJ * f + j)
                project_unit(pe, s, (0, 1), b if first else None).then_inc(S("unit_used"), 1)

            def up(j):
                pe.wait_ge(S("w_lo"), U + 2 * j + 2)
                if past(FJ * f + j):
                    pe.wait_ge(S("act_ready"), FJ * f + j)
                project_unit(pe, 1 - s, (2, 3)).then_inc(S("unit_used"), 1)

            gate(0, True)
            up(0)
            with pe.Fori(1, FJ) as j:
                gate(j)
                up(j)

        def ffn_free(f):
            return {4: ("silu_ready", FJ * (f + 1)), 6: ("act_ready", FJ * (f + 1))}

        def ffn_act(act, f, U):
            s = U % 2

            def silu(j):
                act.wait_ge(S("unit_used"), U + 2 * j + 1)
                if past(FJ * f + j):
                    act.wait_ge(S("act_ready"), FJ * f + j)
                act.activation(arena[:, A_SILU:A_SILU + 2 * T].rearrange("p (a t) -> p a t", a=2), bank[:, 0:2, :],
                               ACT.Silu).then_inc(S("silu_ready"), 1)

            supply_hi(act, U + 2, s)
            silu(0)
            with act.Fori(1, FJ) as j:
                supply_hi(act, U + 2 * j + 1, 1 - s)
                supply_hi(act, U + 2 * j + 2, s)
                silu(j)

        def ffn_dve(dve, f, U, AU):
            s = U % 2

            def product(j):
                dve.wait_ge(S("unit_used"), U + 2 * j + 2)
                dve.wait_ge(S("silu_ready"), FJ * f + j + 1)
                dve.tensor_tensor(arena[:, bass.ds(A_ACT + j * (2 * T), 2 * T)].rearrange("p (a t) -> p a t", a=2),
                                  arena[:, A_SILU:A_SILU + 2 * T].rearrange("p (a t) -> p a t", a=2),
                                  bank[:, 2:4, :], ALU.mult).then_inc(S("act_ready"), 1)

            with dve.Fori(0, FJ - 1) as j:
                supply_lo(dve, U + 2 * j + 2, s)
                product(j)
                supply_lo(dve, U + 2 * j + 3, 1 - s)
            supply_lo(dve, U + 2 * FJ, s)
            split_a_lo(dve, 0, 0, AU)
            split_a_lo(dve, 1, 1, AU)
            product(FJ - 1)
            supply_lo(dve, U + 2 * FJ + 1, 1 - s)

        def a_pair(u):
            return arena[:, bass.ds(A_ACT + u * (2 * T), 2 * T)].rearrange("p (a t) -> p a t", a=2)

        def split_a_hi(act, u, s, AU):
            act.activation(ahi[s][:, :, :], a_pair(u), ACT.Copy).then_inc(S("a_hi"), 1)

        def split_a_lo(dve, u, s, AU):
            dve.wait_ge(S("a_hi"), AU + u + 1)
            dve.tensor_tensor(alo[s][:, :, :], a_pair(u), ahi[s][:, :, :].bitcast(F32), ALU.subtract)\
               .then_inc(S("a_lo"), 1)

        def down_pe(pe, t, n, U, AU, free):
            def unit(u, first=False, last=False):
                ws, xs = (U + u) % 2, u % 2
                if first:
                    pe.wait_ge(S("a_lo"), AU + 1)
                pe.wait_ge(S("w_lo"), U + u + 1)
                pe.wait_ge(S("a_lo"), AU + u + 1)
                order = [(d, kt) for d in range(KD) for kt in range(2)] if last else \
                    [(d, kt) for kt in range(2) for d in range(KD)]
                for d, kt in order:
                    if first and kt == 0 and d in free:
                        pe.wait_ge(S(free[d][0]), free[d][1])
                    ins = mm3(pe, bank[:, (d + 4) % 8, :], *w_block(ws, kt * D + d * P), ahi[xs][:, kt, :],
                              alo[xs][:, kt, :], first and kt == 0, last and kt == 1)
                    if last and kt == 1 and d < KD - 1:
                        ins.then_inc(S("down_done"), 1)
                ins.then_inc(S("unit_used"), 1)

            unit(0, first=True)
            pairs = max(0, (n - 2) // 2 - (n < 6))
            if pairs:
                with pe.Fori(0, pairs) as i:
                    for q in range(2):
                        loop_unit(pe, i, q, U, AU)
            for u in range(1 + 2 * pairs, n - 1):
                unit(u)
            unit(n - 1, last=True)

        def loop_unit(pe, i, q, U, AU):
            ws, xs = (U + 1 + q) % 2, (1 + q) % 2
            pe.wait_ge(S("w_lo"), U + 2 * i + q + 2)
            pe.wait_ge(S("a_lo"), AU + 2 * i + q + 2)
            for kt in range(2):
                for d in range(KD):
                    ins = mm3(pe, bank[:, (d + 4) % 8, :], *w_block(ws, kt * D + d * P), ahi[xs][:, kt, :],
                              alo[xs][:, kt, :], False, False)
            ins.then_inc(S("unit_used"), 1)

        def down_act(act, t, n, U, AU):
            def after(u, sw, sa, a):
                supply_hi(act, U + u + 2, sw)
                if a:
                    act.wait_ge(S("unit_used"), U + u + 1)
                    split_a_hi(act, u + 2, sa, AU)

            loops = (n - 3) // 2 if n > 4 else 0
            if loops:
                with act.Fori(0, loops) as i:
                    after(2 * i, U % 2, 0, True)
                    after(2 * i + 1, (U + 1) % 2, 1, True)
            for u in range(2 * loops, n - 1):
                if U + u + 2 < N_UNITS:
                    supply_hi(act, U + u + 2, (U + u) % 2)
                if u + 2 < n:
                    act.wait_ge(S("unit_used"), U + u + 1)
                    split_a_hi(act, u + 2, u % 2, AU)

        def down_dve(dve, t, n, U, AU, scale):
            loops = (n - 3) // 2 if n > 4 else 0
            if loops:
                with dve.Fori(0, loops) as i:
                    for q in range(2):
                        supply_lo(dve, U + 2 * i + q + 2, (U + q) % 2)
                        dve.wait_ge(S("a_hi"), AU + 2 * i + q + 3)
                        dve.tensor_tensor(alo[q][:, :, :], a_pair(2 * i + q + 2), ahi[q][:, :, :].bitcast(F32),
                                          ALU.subtract).then_inc(S("a_lo"), 1)
            for u in range(2 * loops, n - 1):
                if U + u + 2 < N_UNITS:
                    supply_lo(dve, U + u + 2, (U + u) % 2)
                if u + 2 < n:
                    split_a_lo(dve, u + 2, u % 2, AU)
            for d in range(KD):
                if d < KD - 1:
                    dve.wait_ge(S("down_done"), 7 * t + d + 1)
                else:
                    dve.wait_ge(S("unit_used"), U + n)
                dve.scalar_tensor_tensor(h[:, d, :], bank[:, (d + 4) % 8, :], scale, h[:, d, :], ALU.mult, ALU.add)\
                   .then_inc(S("h_ready"), 1)

        def gdn_pre_pe(pe):
            pe.wait_ge(S("x_lo"), 16)
            pe.wait_ge(S("ba_split"), 2)
            for t in range(TT):
                for k in range(KD):
                    last = mm3(pe, bank[:, 6, t * 16:(t + 1) * 16], xh[:, k, t * P:(t + 1) * P],
                               xl[:, k, t * P:(t + 1) * P], bahi[:, k, :], balo[:, k, :], k == 0, k == KD - 1)
            last.then_inc(S("ba_done"), 1)

        def gdn_cum_pe(pe):
            pe.wait_ge(S("pre_dve"), PRE_G)
            g = hc[:, K_G, :, :].rearrange("p a b -> p (a b)")
            pe.matmul(bank[:, 7, 0:32], upper, g, start=True, stop=True)
            pe.matmul(bank[:, 7, 32:64], ones, g, start=True, stop=True).then_inc(S("cum_done"), 1)

        PRE_G = 12
        small = [slot(0)[:, n * 32:(n + 1) * 32].rearrange("p (a b) -> p a b", a=TT) for n in range(16)]
        sm_x, sm_e1, sm_ax, sm_e2, sm_u, sm_ln, sm_t, sm_ru, sm_gl, sm_d, sm_eg = small[2:13]
        ba = slot(0)[:, 0:64].rearrange("p (a b) -> p a b", a=TT)
        alog_e = slot(0)[:, 480:488]

        def gdn_pre_act(act):
            act.wait_ge(S("pre_dve"), 2)
            act.activation(sm_e1, ba[:, :, 0:H], ACT.Exp, scale=-1.0).then_inc(S("pre_act"), 1)
            act.activation(sm_ax, sm_x, ACT.Abs).then_inc(S("pre_act"), 1)
            act.activation(alog_e, cst[:, C_ALOG:C_ALOG + H], ACT.Exp).then_inc(S("pre_act"), 1)
            act.wait_ge(S("pre_act"), 3)
            act.activation(sm_e2, sm_ax, ACT.Exp, scale=-1.0).then_inc(S("pre_act"), 1)
            act.wait_ge(S("pre_dve"), 3)
            act.activation(sm_ln, sm_u, ACT.Ln).then_inc(S("pre_act"), 1)
            act.wait_ge(S("pre_dve"), PRE_G + 3)
            act.activation(sm_eg, hc[:, K_CUM, :, :], ACT.Exp).then_inc(S("pre_act"), 1)
            act.activation(hc[:, K_KDEC, :, :], sm_d, ACT.Exp).then_inc(S("pre_act"), 1)
            act.activation(hc[:, K_LAST, :, :], sm_gl, ACT.Exp).then_inc(S("pre_act"), 1)

        def gdn_pre_dve(dve):
            dve.memset(pre_pad, 0.0).then_inc(S("pad_ready"), 1)
            st_ = Steps(dve, "pre_dve")
            dve.wait_ge(S("ba_done"), 1)
            st_.link(dve.tensor_copy(slot(0)[:, 0:64], bank[:, 6, 0:64]))
            dtb = cst[:, C_DTB:C_DTB + H].unsqueeze(1).to_broadcast([P, TT, H])
            st_.link(dve.tensor_tensor(sm_x, ba[:, :, H:2 * H], dtb, ALU.add))
            dve.wait_ge(S("pre_act"), 4)
            st_.link(dve.tensor_scalar(sm_u, sm_e2, 1.0, None, ALU.add))
            st_.link(dve.scalar_tensor_tensor(sm_t, sm_u, -1.0, sm_e2, ALU.add, ALU.subtract))
            st_.link(dve.reciprocal(sm_ru, sm_u))
            st_.link(dve.tensor_tensor(sm_t, sm_t, sm_ru, ALU.mult))
            dve.wait_ge(S("pre_act"), 5)
            st_.link(dve.tensor_tensor(sm_ln, sm_ln, sm_t, ALU.subtract))
            st_.link(dve.scalar_tensor_tensor(sm_x, sm_x, 0.0, sm_ln, ALU.max, ALU.add))
            st_.link(dve.scalar_tensor_tensor(hc[:, K_G, :, :], sm_x, -1.0,
                                              alog_e.unsqueeze(1).to_broadcast([P, TT, H]), ALU.mult, ALU.mult))
            st_.link(dve.tensor_scalar(sm_e1, sm_e1, 1.0, None, ALU.add))
            st_.link(dve.reciprocal(hc[:, K_BETA, :, :], sm_e1))
            st_.link(dve.tensor_scalar(hc[:, K_NBETA, :, :], hc[:, K_BETA, :, :], -1.0, None, ALU.mult))
            assert st_.n == PRE_G
            dve.wait_ge(S("cum_done"), 1)
            flat = "p a b -> p (a b)"
            st_.link(dve.tensor_copy(hc[:, K_CUM, :, :].rearrange(flat), bank[:, 7, 0:32]))
            st_.link(dve.tensor_copy(sm_gl.rearrange(flat), bank[:, 7, 32:64]))
            st_.link(dve.tensor_tensor(sm_d, sm_gl, hc[:, K_CUM, :, :], ALU.subtract))
            dve.wait_ge(S("pre_act"), 8)
            st_.link(dve.tensor_tensor(hc[:, K_BEXPG, :, :], hc[:, K_BETA, :, :], sm_eg, ALU.mult))

        def chunks(pe, b, lhs, rhs, start=True, stop=True):
            for n in range(TT):
                cs = slice(n * P, (n + 1) * P)
                last = pe.matmul(bank[:, b, cs], lhs[:, cs], rhs[:, cs], start=start, stop=stop)
            return last

        def turned(pe, b, src):
            for n in range(TT):
                cs = slice(n * P, (n + 1) * P)
                last = pe.transpose(bank[:, b, cs], src[:, cs], ident)
            return last

        def gdn_pe(pe, hp, c):
            U = BASE["gdn_in"]
            core, proj = c is not None, hp is not None
            UA = U + 2 * hp if proj else None

            def A(a, b):
                if not proj:
                    return
                if a == 0:
                    pe.wait_ge(S("w_lo"), UA + 1)
                    if past(hp):
                        pe.wait_ge(S("k_ready"), hp)
                last = project_unit(pe, U % 2, (0, 1), part=(a, b))
                if b == 16:
                    last.then_inc(S("unit_used"), 1)

            def B(a, b):
                if not proj:
                    return
                if a == 0:
                    pe.wait_ge(S("w_lo"), UA + 2)
                    if past(hp):
                        pe.wait_ge(S("expg_ready"), hp)
                    if past(hp):
                        pe.wait_ge(S("z_silu"), hp)
                last = project_unit(pe, 1 - U % 2, (2, 3), part=(a, b))
                if b == 16:
                    last.then_inc(S("unit_used"), 1)

            if core:
                pe.wait_ge(S("k_ready"), c + 1)
                chunks(pe, 4, slot(G_K), slot(G_K)).then_inc(S("kk_done"), 1)
                if past(c):
                    pe.wait_ge(S("on_ready"), c)
                turned(pe, 5, slot(G_K)).then_inc(S("ktr_done"), 1)
                pe.wait_ge(S("q_ready"), c + 1)
                chunks(pe, 7, slot(G_K), slot(G_Q)).then_inc(S("qk_done"), 1)
            A(0, 2)
            if core:
                pe.wait_ge(S("na_ready"), c + 1)
                turned(pe, 4, slot(G_NA)).then_inc(S("nat_done"), 1)
            A(2, 4)
            if core:
                pe.wait_ge(S("n0t_ready"), c + 1)
                pe.wait_ge(S("kd_ready"), c + 1)
                chunks(pe, 5, slot(G_N0T), slot(G_N0)).then_inc(S("n2_done"), 1)
                if past(c):
                    pe.wait_ge(S("y_ready"), c)
                chunks(pe, 6, slot(G_N0), slot(G_N0T)).then_inc(S("n2t_done"), 1)
            A(4, 5)
            if core:
                pe.wait_ge(S("n2_ready"), c + 1)
                pe.wait_ge(S("n2t_ready"), c + 1)
                pe.wait_ge(S("nat_ready"), c + 1)
                chunks(pe, 4, slot(G_N2), slot(G_N2T)).then_inc(S("n4t_done"), 1)
                pe.wait_ge(S("qkm_ready"), c + 1)
                chunks(pe, 7, slot(G_N2T), slot(G_N2)).then_inc(S("n4_done"), 1)
                pe.wait_ge(S("t1_ready"), c + 1)
                chunks(pe, 5, slot(G_N2T), slot(G_TA)).then_inc(S("p2_done"), 1)
            A(5, 6)
            if core:
                pe.wait_ge(S("n4t_ready"), c + 1)
                pe.wait_ge(S("n4_ready"), c + 1)
                chunks(pe, 6, slot(G_N4), slot(G_N0T)).then_inc(S("n8t_done"), 1)
                pe.wait_ge(S("t2_ready"), c + 1)
                chunks(pe, 7, slot(G_N0T), slot(G_TB)).then_inc(S("p4_done"), 1)
                pe.wait_ge(S("v_silu"), c + 1)
                turned(pe, 5, slot(G_V)).then_inc(S("vtr_done"), 1)
            A(6, 8)
            if core:
                pe.wait_ge(S("n8t_ready"), c + 1)
                pe.wait_ge(S("t4_ready"), c + 1)
                chunks(pe, 4, slot(G_NA), slot(G_TA)).then_inc(S("p8_done"), 1)
            A(8, 10)
            if core:
                pe.wait_ge(S("t8_ready"), c + 1)
                pe.wait_ge(S("vb_ready"), c + 1)
                turned(pe, 5, slot(G_TB)).then_inc(S("tt_done"), 1)
                pe.wait_ge(S("b_ready"), 3 * c + 1)
                chunks(pe, 6, slot(G_B1), slot(G_TB)).then_inc(S("w1_done"), 1)
            A(10, 12)
            if core:
                pe.wait_ge(S("tt_ready"), c + 1)
                pe.wait_ge(S("w1_ready"), c + 1)
                chunks(pe, 7, slot(G_N2), slot(G_N2T)).then_inc(S("ta_done"), 1)
                chunks(pe, 4, slot(G_N2T), slot(G_N2)).then_inc(S("tta_done"), 1)
            A(12, 14)
            if core:
                pe.wait_ge(S("ta_ready"), c + 1)
                pe.wait_ge(S("b_ready"), 3 * c + 2)
                chunks(pe, 5, slot(G_B2), slot(G_TA)).then_inc(S("w2_done"), 1)
            A(14, 16)
            if core:
                pe.wait_ge(S("tta_ready"), c + 1)
                pe.wait_ge(S("w2_ready"), c + 1)
                chunks(pe, 6, slot(G_N4), slot(G_N2T)).then_inc(S("tb_done"), 1)
                chunks(pe, 7, slot(G_N2T), slot(G_N4)).then_inc(S("ttb_done"), 1)
            B(0, 2)
            if core:
                pe.wait_ge(S("tb_ready"), c + 1)
                pe.wait_ge(S("b_ready"), 3 * c + 3)
                chunks(pe, 4, slot(G_B3), slot(G_TB)).then_inc(S("w3_done"), 1)
            B(2, 4)
            if core:
                pe.wait_ge(S("ttb_ready"), c + 1)
                pe.wait_ge(S("w3_ready"), c + 1)
                chunks(pe, 5, slot(G_N2T), slot(G_N2)).then_inc(S("ttc_done"), 1)
            B(4, 6)
            if core:
                pe.wait_ge(S("ttc_ready"), c + 1)
                chunks(pe, 6, slot(G_KBG), slot(G_N4)).then_inc(S("wt_done"), 1)
            fill = [(6, 7), (7, 8), (8, 9), (9, 10), (10, 11), (11, 12), (12, 13)]
            for n in range(TT):
                cs = slice(n * P, (n + 1) * P)
                if core:
                    ins = pe.matmul(bank[:, 7, cs], slot(G_N4)[:, cs], slot(G_VB)[:, cs], start=True, stop=n == 0)
                    if n == 0:
                        pe.wait_ge(S("wt_ready"), c + 1)
                    else:
                        pe.wait_ge(S("s_ready"), 3 * c + n)
                        ins = pe.matmul(bank[:, 7, cs], slot(G_N0)[:, cs], state, start=False, stop=True)
                    ins.then_inc(S("u_done"), 1)
                    if n == 0:
                        pe.wait_ge(S("qd_ready"), c + 1)
                    else:
                        pe.matmul(bank[:, 5, cs], slot(G_QD)[:, cs], state, start=True, stop=False)
                B(*fill[2 * n])
                if core:
                    pe.wait_ge(S("u_ready"), 4 * c + n + 1)
                    if n < TT - 1:
                        pe.matmul(bank[:, 4, 0:P], slot(G_KD)[:, cs], slot(G_N0T)[:, cs], start=True, stop=True)\
                          .then_inc(S("s_done"), 1)
                    ins = pe.matmul(bank[:, 5, cs], slot(G_QK)[:, cs], slot(G_N0T)[:, cs], start=n == 0, stop=True)
                    if n == TT - 1:
                        ins.then_inc(S("o_done"), 1)
                if n < TT - 1:
                    B(*fill[2 * n + 1])
                if proj and n == 1:
                    pe.wait_ge(S("qk_sq"), hp + 1)
                    for q in range(2):
                        for t in range(TT):
                            ins = pe.matmul(bank[:, 0, q * TT + t:q * TT + t + 1], sq[:, q, t * P:(t + 1) * P],
                                            ones[:, 0:1], start=True, stop=True)
                    ins.then_inc(S("qk_ss"), 1)
            B(13, 16)
            if proj:
                pe.wait_ge(S("qk_rn"), hp + 1)
                spread(pe, bank[:, 1, :], st[:, 44:48]).then_inc(S("q_bc"), 1)
                spread(pe, bank[:, 0, :], st[:, 48:52]).then_inc(S("k_bc"), 1)
                pe.wait_ge(S("gcur_ready"), hp + 1)
                pe.wait_ge(S("v_pre"), hp + 1)
                for t in range(TT):
                    ins = pe.matmul(bank[:, 2, t * P:(t + 1) * P], gcur[:, 0, t:t + 1].to_broadcast([P, P]), upper,
                                    start=True, stop=True)
                ins.then_inc(S("gbc_done"), 1)
            if core:
                pe.wait_ge(S("on_ready"), c + 1)
                pe.wait_ge(S("wt_ready"), c + 1)
                turned(pe, 6, xn[:, 1, :]).then_inc(S("otr_done"), 1)

        def gdn_act(act, hp, c):
            U = BASE["gdn_in"]
            core, proj = c is not None, hp is not None
            UA = U + 2 * hp if proj else None

            def keep(b, dst, need, name, scale=1.0):
                if core:
                    act.wait_ge(S(need), c + 1)
                    act.activation(slot(dst), bank[:, b, :], ACT.Copy, scale=scale).then_inc(S(name), 1)

            if core:
                act.wait_ge(S("n0t_ready"), c + 1)
            keep(4, G_NAT, "nat_done", "nat_ready")
            keep(5, G_N2, "n2_done", "n2_ready")
            keep(7, G_N4, "n4_done", "n4_ready")
            keep(6, G_NA, "n8t_done", "n8t_ready")
            keep(5, G_N2, "tt_done", "tt_ready")
            keep(5, G_N2T, "w2_done", "w2_ready")
            if proj:
                act.wait_ge(S("unit_used"), UA + 1)
                act.wait_ge(S("pad_ready"), 1)
                if past(8 * hp):
                    act.wait_ge(S("qk_conv"), 8 * hp)
                act.activation(pre3[:, 0:2, 3:3 + T], bank[:, 0:2, :], ACT.Copy).then_inc(S("qk_pre"), 1)
            keep(4, G_N2T, "w3_done", "w3_ready")
            if proj:
                supply_hi(act, UA + 2, U % 2)
            keep(6, G_N0, "wt_done", "wt_ready", -1.0)
            if proj:
                act.wait_ge(S("qk_conv"), 8 * hp + 8)
                act.activation(slot(G_QS, 2), slot(G_QS, 2), ACT.Silu).then_inc(S("qk_silu"), 1)
                act.wait_ge(S("qk_silu"), hp + 1)
                if past(hp):
                    act.wait_ge(S("qk_ss"), hp)
                act.activation(sq[:, :, :].rearrange("p a t -> p (a t)"), slot(G_QS, 2), ACT.Square)\
                   .then_inc(S("qk_sq"), 1)
            if core:
                act.wait_ge(S("o_done"), c + 1)
                act.activation(xn[:, 0, :], bank[:, 5, :], ACT.Square).then_inc(S("osq_ready"), 1)
            if proj:
                act.wait_ge(S("unit_used"), UA + 2)
                if past(4 * hp):
                    act.wait_ge(S("v_conv"), 4 * hp)
                act.activation(pre3[:, 2, 3:3 + T], bank[:, 2, :], ACT.Copy).then_inc(S("v_pre"), 1)
                rsqrt_act(act, "qk_var", hp + 1, "qk_est", 2 * hp, st[:, 20:28], st[:, 28:36], st[:, 36:44])
            if core:
                rsqrt_act(act, "o_var", c + 1, "o_est", 2 * c, st[:, 56:60], st[:, 60:64], st[:, 64:68])
            if proj:
                act.wait_ge(S("dabs_ready"), hp + 1)
                if past(hp):
                    act.wait_ge(S("du_ready"), hp)
                act.activation(slot(G_D), slot(G_D), ACT.Exp, scale=-1.0).then_inc(S("decay_ready"), 1)
                if past(hp):
                    act.wait_ge(S("qd_ready"), hp)
                act.activation(slot(G_EG), bank[:, 2, :], ACT.Exp).then_inc(S("expg_ready"), 1)
                act.wait_ge(S("v_conv"), 4 * hp + 4)
                act.activation(slot(G_V), slot(G_V), ACT.Silu).then_inc(S("v_silu"), 1)
                if core:
                    act.wait_ge(S("y_ready"), c + 1)
                act.activation(slot(G_Z), bank[:, 3, :], ACT.Silu).then_inc(S("z_silu"), 1)
                supply_hi(act, UA + 3, 1 - U % 2)

        def rsqrt_act(act, need, n, name, base, v, ln, est):
            act.wait_ge(S(need), n)
            act.activation(ln, v, ACT.Ln).then_inc(S(name), 1)
            act.wait_ge(S(name), base + 1)
            act.activation(est, ln, ACT.Exp, scale=-0.5).then_inc(S(name), 1)

        def gdn_dve(dve, hp, c):
            U = BASE["gdn_in"]
            core, proj = c is not None, hp is not None
            UA = U + 2 * hp if proj else None

            def add(b, a, o, need, name):
                if core:
                    dve.wait_ge(S(need), c + 1)
                    dve.tensor_tensor(slot(o), bank[:, b, :], slot(a), ALU.add).then_inc(S(name), 1)

            def keep(b, dst, need, name):
                if core:
                    dve.wait_ge(S(need), c + 1)
                    dve.tensor_copy(slot(dst), bank[:, b, :]).then_inc(S(name), 1)

            def conv(q, dst, name, base):
                if not proj:
                    return
                for j in range(4):
                    x, w = pre3[:, q, j:j + T], cwh[:, q, j:j + 1]
                    if j == 0:
                        ins = dve.tensor_scalar(slot(dst), x, w, None, ALU.mult)
                    else:
                        dve.wait_ge(S(name), base + j)
                        ins = dve.scalar_tensor_tensor(slot(dst), x, w, slot(dst), ALU.mult, ALU.add)
                    ins.then_inc(S(name), 1)

            if core:
                if past(3 * c):
                    dve.wait_ge(S("s_ready"), 3 * c)
                dve.tensor_copy(hcur[:, :, :], hc[:, :, :, bass.ds(c, 1)].rearrange("p a b c -> p a (b c)"))\
                   .then_inc(S("hcur_ready"), 1)
                dve.wait_ge(S("kk_done"), c + 1)
                dve.wait_ge(S("dl_ready"), c + 1)
                dve.wait_ge(S("hcur_ready"), c + 1)
                for n in range(TT):
                    cs = slice(n * P, (n + 1) * P)
                    ins = dve.scalar_tensor_tensor(slot(G_NA)[:, cs], bank[:, 4, cs], hcur[:, K_NBETA, n:n + 1],
                                                   slot(G_DL)[:, cs], ALU.mult, ALU.mult)
                ins.then_inc(S("na_ready"), 1)
                dve.wait_ge(S("na_ready"), c + 1)
                dve.tensor_tensor(c4(slot(G_N0)), c4(slot(G_NA)), over_c(gm_diag), ALU.mult)\
                   .then_inc(S("n0_ready"), 1)
                dve.wait_ge(S("nat_done"), c + 1)
                dve.tensor_tensor(c4(slot(G_N0T)), c4(bank[:, 4, :]), over_c(gm_diag), ALU.mult)\
                   .then_inc(S("n0t_ready"), 1)
                dve.wait_ge(S("ktr_done"), c + 1)
                dve.tensor_tensor(c4(slot(G_KBG)), c4(bank[:, 5, :]), over_t(hcur[:, K_BEXPG, :]), ALU.mult)\
                   .then_inc(S("kbg_ready"), 1)
                dve.tensor_tensor(c4(slot(G_KD)), c4(bank[:, 5, :]), over_t(hcur[:, K_KDEC, :]), ALU.mult)\
                   .then_inc(S("kd_ready"), 1)
            keep(6, G_N2T, "n2t_done", "n2t_ready")
            if core:
                dve.wait_ge(S("qk_done"), c + 1)
                dve.wait_ge(S("du_ready"), c + 1)
                dve.tensor_tensor(slot(G_QK), bank[:, 7, :], slot(G_DU), ALU.mult).then_inc(S("qkm_ready"), 1)
            keep(4, G_N0T, "n4t_done", "n4t_ready")
            add(5, G_TA, G_TB, "p2_done", "t2_ready")
            add(7, G_TB, G_TA, "p4_done", "t4_ready")
            if core:
                dve.wait_ge(S("vtr_done"), c + 1)
                dve.tensor_tensor(c4(slot(G_VB)), c4(bank[:, 5, :]), over_t(hcur[:, K_BETA, :]), ALU.mult)\
                   .then_inc(S("vb_ready"), 1)
            add(4, G_TA, G_TB, "p8_done", "t8_ready")
            keep(6, G_N2T, "w1_done", "w1_ready")
            add(7, G_TB, G_TA, "ta_done", "ta_ready")
            if core:
                dve.wait_ge(S("tt_ready"), c + 1)
            add(4, G_N2, G_N4, "tta_done", "tta_ready")
            if proj:
                dve.wait_ge(S("unit_used"), UA + 1)
                if past(4 * hp):
                    dve.wait_ge(S("v_conv"), 4 * hp)
                if past(hp):
                    dve.wait_ge(S("gbc_done"), hp)
                dve.tensor_copy(cwh[:, :, :].rearrange("p a b -> p (a b)"), cst[:, bass.ds(C_CONV + 12 * hp, 12)])\
                   .then_inc(S("gcur_ready"), 1)
                dve.tensor_copy(gcur[:, :, :], hc[:, 0:2, :, bass.ds(hp, 1)].rearrange("p a b c -> p a (b c)"))\
                   .then_inc(S("gcur_ready"), 1)
                dve.wait_ge(S("gcur_ready"), 2 * hp + 2)
                dve.wait_ge(S("qk_pre"), hp + 1)
                if past(hp):
                    dve.wait_ge(S("k_ready"), hp)
            conv(0, G_QS, "qk_conv", 8 * hp if proj else 0)
            add(6, G_TA, G_TB, "tb_done", "tb_ready")
            add(7, G_N4, G_N2, "ttb_done", "ttb_ready")
            conv(1, G_KS, "qk_conv", 8 * hp + 4 if proj else 0)
            add(5, G_N2, G_N4, "ttc_done", "ttc_ready")
            if proj:
                supply_lo(dve, UA + 2, U % 2)
            if core:
                for n in range(TT):
                    cs = slice(n * P, (n + 1) * P)
                    dve.wait_ge(S("u_done"), 4 * c + n + 1)
                    dve.tensor_copy(slot(G_N0T)[:, cs], bank[:, 7, cs]).then_inc(S("u_ready"), 1)
                    if n < TT - 1:
                        dve.wait_ge(S("s_done"), 3 * c + n + 1)
                        if n == 0:
                            ins = dve.tensor_copy(state, bank[:, 4, 0:P])
                        else:
                            dve.wait_ge(S("s_ready"), 3 * c + n)
                            ins = dve.scalar_tensor_tensor(state, state, hcur[:, K_LAST, n:n + 1], bank[:, 4, 0:P],
                                                           ALU.mult, ALU.add)
                        ins.then_inc(S("s_ready"), 1)
            if proj:
                dve.wait_ge(S("qk_ss"), hp + 1)
                dve.tensor_scalar(st[:, 20:28], bank[:, 0, 0:8], EPS, None, ALU.add).then_inc(S("qk_var"), 1)
            if core:
                dve.wait_ge(S("osq_ready"), c + 1)
                if past(c):
                    dve.wait_ge(S("o_var"), c)
                dve.tensor_reduce(st[:, 52:56], c4(xn[:, 0, :]), AX.X, ALU.add).then_inc(S("o_sum"), 1)
                dve.wait_ge(S("o_sum"), c + 1)
                dve.tensor_scalar(st[:, 56:60], st[:, 52:56], 1.0 / P, EPS, ALU.mult, ALU.add)\
                   .then_inc(S("o_var"), 1)
            if proj:
                dve.wait_ge(S("qk_est"), 2 * hp + 2)
                if past(hp):
                    dve.wait_ge(S("k_bc"), hp)
                steps = Steps(dve, "qk_step", 3 * hp)
                newton(dve, steps, st[:, 20:28], st[:, 36:44], st[:, 68:76], st[:, 44:52]).then_inc(S("qk_rn"), 1)
            if core:
                dve.wait_ge(S("o_est"), 2 * c + 2)
                steps = Steps(dve, "o_step", 4 * c)
                steps.link(newton(dve, steps, st[:, 56:60], st[:, 64:68], st[:, 76:80], st[:, 80:84]))
                if past(c):
                    dve.wait_ge(S("otr_done"), c)
                dve.tensor_tensor(c4(xn[:, 1, :]), c4(bank[:, 5, :]), over_t(st[:, 80:84]), ALU.mult)\
                   .then_inc(S("on_ready"), 1)
            if proj:
                dve.wait_ge(S("v_pre"), hp + 1)
            conv(2, G_V, "v_conv", 4 * hp if proj else 0)
            if proj:
                dve.wait_ge(S("q_bc"), hp + 1)
                if past(hp):
                    dve.wait_ge(S("qd_ready"), hp)
                dve.scalar_tensor_tensor(slot(G_Q), slot(G_QS), float(P) ** -0.5, bank[:, 1, :], ALU.mult, ALU.mult)\
                   .then_inc(S("q_ready"), 1)
                dve.wait_ge(S("k_bc"), hp + 1)
                dve.tensor_tensor(slot(G_K), slot(G_KS), bank[:, 0, :], ALU.mult).then_inc(S("k_ready"), 1)
                dve.wait_ge(S("gbc_done"), hp + 1)
                if past(hp):
                    dve.wait_ge(S("du_ready"), hp)
                dve.tensor_tensor(c4(slot(G_D)), c4(bank[:, 2, :]), over_t(gcur[:, 1, :]), ALU.subtract)\
                   .then_inc(S("diff_ready"), 1)
                dve.wait_ge(S("diff_ready"), hp + 1)
                dve.scalar_tensor_tensor(slot(G_D), slot(G_D), -1.0, slot(G_D), ALU.mult, ALU.max).then_inc(S("dabs_ready"), 1)
            if core:
                dve.wait_ge(S("otr_done"), c + 1)
                dve.wait_ge(S("z_silu"), c + 1)
                dve.scalar_tensor_tensor(arena[:, bass.ds(c * T, T)], bank[:, 6, :], cst[:, C_ONORM:C_ONORM + 1],
                                         slot(G_Z), ALU.mult, ALU.mult).then_inc(S("y_ready"), 1)
            if proj:
                supply_lo(dve, UA + 3, 1 - U % 2)

        def gdn_pool(pool, hp, c):
            if c is not None:
                pool.wait_ge(S("n0_ready"), c + 1)
                pool.tensor_tensor(c4(slot(G_TA)), c4(slot(G_N0)), over_c(ident), ALU.add).then_inc(S("t1_ready"), 1)
                pool.wait_ge(S("nat_ready"), c + 1)
                for b, m in ((G_B1, gm_b1), (G_B2, gm_b2), (G_B3, gm_b3)):
                    pool.tensor_tensor(c4(slot(b)), c4(slot(G_NAT)), over_c(m), ALU.mult).then_inc(S("b_ready"), 1)
            if hp is not None:
                pool.wait_ge(S("decay_ready"), hp + 1)
                pool.tensor_tensor(c4(slot(G_DL)), c4(slot(G_D)), over_c(gm_lower), ALU.mult).then_inc(S("dl_ready"), 1)
                pool.tensor_tensor(c4(slot(G_DU)), c4(slot(G_D)), over_c(upper), ALU.mult).then_inc(S("du_ready"), 1)
                pool.wait_ge(S("expg_ready"), hp + 1)
                pool.wait_ge(S("q_ready"), hp + 1)
                if past(hp):
                    pool.wait_ge(S("o_done"), hp)
                pool.tensor_tensor(slot(G_QD), slot(G_Q), slot(G_EG), ALU.mult).then_inc(S("qd_ready"), 1)

        def gdn(eng, one):
            one(eng, 0, None)
            one(eng, 1, 0)
            with eng.Fori(2, H) as i:
                one(eng, i, i - 1)
            one(eng, None, H - 1)

        X_COS, X_SIN, X_ANG, X_TURNS, X_POS, X_RAW, X_ROT = 0, 1, 2, 3, 4, 5, 2
        X_Q, X_QZ, X_P, X_PT = 8, 16, 18, 22
        TWO_PI = (6.28125, 2029.0 / 2 ** 20, 2 * math.pi - 6.28125 - 2029.0 / 2 ** 20)
        ROUND = 1.5 * 2 ** 23
        TRIG = 15

        def trig_dve(dve, n):
            steps = Steps(dve, "angle_step", TRIG * n)
            dve.wait_ge(S("pos_landed"), 16 * (n + 1))
            if past(2 * n):
                dve.wait_ge(S("trig_ready"), 2 * n)
            steps.link(dve.tensor_copy(slot(X_ANG), slot(X_POS).bitcast(I32)))
            steps.link(dve.tensor_scalar(slot(X_ANG), slot(X_ANG), cst[:, C_FREQ:C_FREQ + 1], None, ALU.mult))
            for dst, turn, shift in ((X_SIN, 0.0, 0.0), (X_COS, 0.25, math.pi / 2)):
                turns = slot(X_TURNS)
                steps.link(dve.tensor_scalar(turns, slot(X_ANG), 1.0 / (2 * math.pi), turn, ALU.mult, ALU.add))
                steps.link(dve.tensor_scalar(turns, turns, ROUND, None, ALU.add))
                steps.link(dve.tensor_scalar(turns, turns, ROUND, None, ALU.subtract))
                src = slot(X_ANG)
                for m in TWO_PI:
                    steps.link(dve.scalar_tensor_tensor(slot(dst), turns, -m, src, ALU.mult, ALU.add))
                    src = slot(dst)
                if shift:
                    steps.link(dve.tensor_scalar(slot(dst), slot(dst), shift, None, ALU.add))
                dve.tensor_scalar(slot(dst), slot(dst), math.pi, -math.pi, ALU.min, ALU.max)\
                   .then_inc(S("trig_arg"), 1)
            assert steps.n == TRIG

        def trig_act(act, n):
            for k, dst in enumerate((X_SIN, X_COS)):
                act.wait_ge(S("trig_arg"), 2 * n + k + 1)
                act.activation(slot(dst), slot(dst), ACT.Sin).then_inc(S("trig_ready"), 1)

        def rope_project_pe(pe, U, i, b, n):
            pe.wait_ge(S("w_lo"), U + i + 1)
            if past(n + i - 1):
                pe.wait_ge(S("rope_raw"), n + i - 1)
            two = 2 * (i % 2)
            project_unit(pe, (U + i) % 2, (two, two + 1), b if i == 0 else None).then_inc(S("unit_used"), 1)

        def rope_rot_pe(pe, i, n):
            two = 4 + 2 * (i % 2)
            pe.wait_ge(S("rope_raw"), n + i + 1)
            if past(n + i - 1):
                pe.wait_ge(S("rope_ready"), n + i - 1)
            pe.matmul(bank[:, two, :], rope_rot, slot(X_RAW), start=True, stop=True)
            pe.matmul(bank[:, two + 1, :], rope_rot, slot(X_RAW + 1), start=True, stop=True).then_inc(S("rot_done"), 1)

        def rope_raw_act(act, U, i, n, scale):
            act.wait_ge(S("unit_used"), U + i + 1)
            if past(n + i):
                act.wait_ge(S("rope_ready"), n + i)
            two = 2 * (i % 2)
            act.activation(slot(X_RAW, 2).rearrange("p (a t) -> p a t", a=2), bank[:, two:two + 2, :], ACT.Copy,
                           scale=scale).then_inc(S("rope_raw"), 1)

        def rope_dve(dve, i, n, dst):
            two = 4 + 2 * (i % 2)

            def pair(ap):
                return ap.rearrange("p (a t) -> p a t", a=2)

            def both(k):
                return slot(k).unsqueeze(1).to_broadcast([P, 2, T])

            dve.wait_ge(S("rot_done"), n + i + 1)
            dve.wait_ge(S("trig_ready"), 2 * (n // 4) + 2)
            steps = Steps(dve, "rope_step", 2 * (n + i))
            if past(n + i):
                dve.wait_ge(S("rope_ready"), n + i)
            steps.link(dve.tensor_tensor(pair(slot(X_ROT, 2)), bank[:, two:two + 2, :], both(X_SIN), ALU.mult))
            steps.link(dve.tensor_tensor(pair(dst), pair(slot(X_RAW, 2)), both(X_COS), ALU.mult))
            dve.tensor_tensor(dst, dst, slot(X_ROT, 2), ALU.add).then_inc(S("rope_ready"), 1)

        def v_unit_pe(pe, U, v):
            pe.wait_ge(S("w_lo"), U + v + 1)
            for kt in range(4):
                for t in range(TT):
                    k = 4 * (v % 2) + kt
                    ins = mm3(pe, bank[:, 4 * (v // 2) + t, :], xh[:, k, t * P:(t + 1) * P], xl[:, k, t * P:(t + 1) * P],
                              *w_block((U + v) % 2, kt * 512, 512), k == 0, k == KD - 1)
            ins.then_inc(S("unit_used"), 1)

        values = arena[:, A_V:A_V + KD * T].rearrange("p (t c) -> p t c", t=TT)

        def v_keep_act(act, U, half):
            act.wait_ge(S("unit_used"), U + 2 * half + 2)
            act.activation(values[:, :, half * 512:(half + 1) * 512], bank[:, 4 * half:4 * half + 4, :], ACT.Copy)\
               .then_inc(S("v_kept"), 1)

        def kv_pe(pe):
            U = BASE["kv"]
            for i in range(4):
                rope_project_pe(pe, U, i, 3, 0)
                if i:
                    rope_rot_pe(pe, i - 1, 0)
            pe.wait_ge(S("rope_raw"), 4)
            v_unit_pe(pe, U + 4, 0)
            rope_rot_pe(pe, 3, 0)
            v_unit_pe(pe, U + 4, 1)
            pe.wait_ge(S("rope_ready"), 4)
            v_unit_pe(pe, U + 4, 2)
            v_unit_pe(pe, U + 4, 3)

        def kv_act(act):
            U = BASE["kv"]
            trig_act(act, 0)
            for i in range(4):
                supply_hi(act, U + i + 2, (U + i) % 2)
                rope_raw_act(act, U, i, 0, 1.0)
            for v in range(4):
                if v < 3:
                    supply_hi(act, U + v + 6, (U + v) % 2)
                if v % 2:
                    v_keep_act(act, U + 4, v // 2)

        def keys(i):
            return arena[:, A_KT + 2 * i * T:A_KT + 2 * (i + 1) * T]

        def kv_dve(dve):
            U = BASE["kv"]
            trig_dve(dve, 0)
            for i in range(4):
                supply_lo(dve, U + i + 2, (U + i) % 2)
                if i:
                    rope_dve(dve, i - 1, 0, keys(i - 1))
            supply_lo(dve, U + 6, U % 2)
            rope_dve(dve, 3, 0, keys(3))
            supply_lo(dve, U + 7, (U + 1) % 2)
            supply_lo(dve, U + 8, U % 2)

        def q_pe(pe):
            U = BASE["q"]
            for i in range(4):
                rope_project_pe(pe, U, i, 5, 4)
                if i:
                    rope_rot_pe(pe, i - 1, 4)
            rope_rot_pe(pe, 3, 4)

        def q_act(act):
            U = BASE["q"]
            trig_act(act, 1)
            for i in range(4):
                if i < 3:
                    supply_hi(act, U + i + 2, (U + i) % 2)
                rope_raw_act(act, U, i, 4, 64 ** -0.5)
            supply_hi(act, U + 5, (U + 3) % 2)

        def q_dve(dve):
            U = BASE["q"]
            trig_dve(dve, 1)
            for i in range(4):
                if i < 3:
                    supply_lo(dve, U + i + 2, (U + i) % 2)
                if i:
                    rope_dve(dve, i - 1, 4, slot(X_Q + 2 * i - 2, 2))
            rope_dve(dve, 3, 4, slot(X_Q + 6, 2))
            supply_lo(dve, U + 5, (U + 3) % 2)

        def attn_pe(pe, hd, g):
            def scores(i):
                n = 4 * hd + i
                if i == 0:
                    pe.wait_ge(S("qz_ready"), 2 * hd + 2)
                if past(n - 1):
                    pe.wait_ge(S("p_ready"), n - 1)
                for m in range(2):
                    ins = pe.matmul(bank[:, 2 * (i % 2) + m, 0:(i + 1) * P], slot(X_QZ + m)[:, i * P:(i + 1) * P],
                                    arena[:, bass.ds(A_KT + hd * T, (i + 1) * P)], start=True, stop=True)
                ins.then_inc(S("sc_done"), 1)

            def turn(e, i):
                n = 4 * e + i
                pe.wait_ge(S("pc_ready"), n + 1)
                if past(n - 1):
                    pe.wait_ge(S("pt_ready"), n - 1)
                for j in range(i + 1):
                    ins = pe.transpose(bank[:, 4 + i % 2, j * P:(j + 1) * P], slot(X_P + 2 * (i % 2))[:, j * P:(j + 1) * P],
                                       ident)
                ins.then_inc(S("ptr_done"), 1)

            def weigh(e, i):
                pe.wait_ge(S("pt_ready"), 4 * e + i + 1)
                if i == 0:
                    if past(e):
                        pe.wait_ge(S("osb_ready"), e)
                for j in range(i + 1):
                    ins = pe.matmul(bank[:, 6, i * P:(i + 1) * P], slot(X_PT + i % 2)[:, j * P:(j + 1) * P],
                                    arena[:, bass.ds(A_V + j * D + e * P, P)], start=j == 0, stop=j == i)
                ins.then_inc(S("pv_done"), 1)

            for i in range(4):
                if hd is not None:
                    scores(i)
                if i < 2:
                    if g is not None:
                        turn(g, i + 2)
                elif hd is not None:
                    turn(hd, i - 2)
                if i < 3:
                    if g is not None:
                        weigh(g, i + 1)
                elif hd is not None:
                    weigh(hd, 0)
            if g is not None:
                pe.wait_ge(S("aon_ready"), g + 1)
                if past(g):
                    pe.wait_ge(S("ay_ready"), g)
                turned(pe, 7, xn[:, 1, :]).then_inc(S("aotr_done"), 1)

        def attn_act(act, hd, g):
            def soft(i):
                n = 4 * hd + i
                act.wait_ge(S("mx_ready"), n + 1)
                if past(n - 1):
                    act.wait_ge(S("ptr_done"), n - 1)
                for m in range(2):
                    ins = act.activation(slot(X_P + 2 * (i % 2) + m)[:, 0:(i + 1) * P],
                                         bank[:, 2 * (i % 2) + m, 0:(i + 1) * P], ACT.Exp,
                                         bias=negmax[:, 2 * (i % 2) + m:2 * (i % 2) + m + 1],
                                         accum_out=rowsum[:, 2 * (i % 2) + m:2 * (i % 2) + m + 1])
                ins.then_inc(S("p_ready"), 1)

            def keep(e, i):
                n = 4 * e + i
                act.wait_ge(S("ptr_done"), n + 1)
                if past(n - 1):
                    act.wait_ge(S("pv_done"), n - 1)
                act.activation(slot(X_PT + i % 2)[:, 0:(i + 1) * P], bank[:, 4 + i % 2, 0:(i + 1) * P], ACT.Copy)\
                   .then_inc(S("pt_ready"), 1)

            for i in range(4):
                if hd is not None:
                    soft(i)
                if i < 2:
                    if g is not None:
                        keep(g, i + 2)
                elif hd is not None:
                    keep(hd, i - 2)
                if i == 2 and g is not None:
                    act.wait_ge(S("pv_done"), 4 * g + 4)
                    if past(g):
                        act.wait_ge(S("aon_ready"), g)
                    act.activation(xn[:, 0, :], bank[:, 6, :], ACT.Copy).then_inc(S("osb_ready"), 1)
            if g is not None:
                rsqrt_act(act, "aovar", g + 1, "ao_est", 2 * g, st[:, 56:60], st[:, 60:64], st[:, 64:68])

        negmax, rowsum = st[:, 0:4], st[:, 4:8]
        rr = st[:, 8:12]

        def attn_dve(dve, hd, g):
            def top(i):
                n = 4 * hd + i
                two = 2 * (i % 2)
                dve.wait_ge(S("sc_done"), n + 1)
                diag = bank[:, two:two + 2, i * P:(i + 1) * P]
                dve.tensor_tensor(diag, diag, causal.unsqueeze(1).to_broadcast([P, 2, P]), ALU.add)\
                   .then_inc(S("masked"), 1)
                dve.wait_ge(S("masked"), n + 1)
                if past(n - 1):
                    dve.wait_ge(S("p_ready"), n - 1)
                dve.tensor_reduce(negmax[:, two:two + 2], bank[:, two:two + 2, 0:(i + 1) * P], AX.X, ALU.max,
                                  negate=True).then_inc(S("mx_ready"), 1)

            def mix(e, i):
                n = 4 * e + i
                two = 2 * (i % 2)
                p0, p1 = (slot(X_P + two + m)[:, 0:(i + 1) * P] for m in range(2))
                dve.wait_ge(S("p_ready"), n + 1)
                steps = Steps(dve, "p_step", 3 * n)
                steps.link(dve.reciprocal(rr[:, two:two + 2], rowsum[:, two:two + 2]))
                steps.link(dve.tensor_scalar(rr[:, two + 1:two + 2], rr[:, two + 1:two + 2], neglam[:, 0:1], None, ALU.mult))
                steps.link(dve.tensor_scalar(p0, p0, rr[:, two:two + 1], None, ALU.mult))
                dve.scalar_tensor_tensor(p0, p1, rr[:, two + 1:two + 2], p0, ALU.mult, ALU.add)\
                   .then_inc(S("pc_ready"), 1)

            for i in range(4):
                if hd is not None:
                    if i == 0:
                        if past(4 * hd):
                            dve.wait_ge(S("sc_done"), 4 * hd)
                        for m in range(2):
                            rows = slice(64 * m, 64 * m + 64)
                            dve.tensor_copy(slot(X_QZ + m)[rows, :], arena[rows, bass.ds((X_Q + hd) * T, T)])\
                               .then_inc(S("qz_ready"), 1)
                    top(i)
                if i == 0:
                    if g is not None:
                        mix(g, 3)
                elif hd is not None:
                    mix(hd, i - 1)
            if g is not None:
                dve.wait_ge(S("osb_ready"), g + 1)
                steps = Steps(dve, "ao_step", 6 * g)
                steps.link(dve.tensor_tensor(sq[:, 0, :], xn[:, 0, :], xn[:, 0, :], ALU.mult))
                steps.link(dve.tensor_reduce(st[:, 52:56], c4(sq[:, 0, :]), AX.X, ALU.add))
                dve.tensor_scalar(st[:, 56:60], st[:, 52:56], 1.0 / P, EPS, ALU.mult, ALU.add)\
                   .then_inc(S("aovar"), 1)
                dve.wait_ge(S("ao_est"), 2 * g + 2)
                steps.link(newton(dve, steps, st[:, 56:60], st[:, 64:68], st[:, 76:80], st[:, 80:84]))
                if past(g):
                    dve.wait_ge(S("aotr_done"), g)
                dve.tensor_tensor(c4(xn[:, 1, :]), c4(xn[:, 0, :]), over_t(st[:, 80:84]), ALU.mult)\
                   .then_inc(S("aon_ready"), 1)
                dve.wait_ge(S("aotr_done"), g + 1)
                dve.tensor_scalar(arena[:, bass.ds(g * T, T)], bank[:, 7, :], neglam[:, 1:2], None, ALU.mult)\
                   .then_inc(S("ay_ready"), 1)

        def lambda_dve(dve):
            dve.wait_ge(S("early_landed"), 16)
            steps = Steps(dve, "lam_step")
            lp = arena[:, A_EARLY:A_EARLY + 256].rearrange("p (a b c) -> p a b c", a=2, b=2)
            pr = arena[:, A_EARLY + 512:A_EARLY + 640].rearrange("p (a c) -> p a c", a=2)
            steps.link(dve.tensor_tensor(pr, lp[:, :, 0, :], lp[:, :, 1, :], ALU.mult))
            dve.tensor_reduce(neglam[:, 2:4], pr, AX.X, ALU.add).then_inc(S("lam_sum"), 1)
            dve.wait_ge(S("lam_exp"), 1)
            dve.scalar_tensor_tensor(neglam[:, 0:1], neglam[:, 3:4], -LAM_INIT, neglam[:, 2:3], ALU.add, ALU.subtract)\
               .then_inc(S("lam_ready"), 1)
            dve.tensor_scalar(neglam[:, 1:2], cst[:, C_SUBLN:C_SUBLN + 1], 1.0 - LAM_INIT, None, ALU.mult)\
               .then_inc(S("lam_ready"), 1)

        AU = {"ffn0": 0, "gdn": FJ, "ffn1": FJ + U_OUT, "ffn2": 2 * FJ + U_OUT, "attn": 3 * FJ + U_OUT,
              "ffn3": 3 * FJ + 2 * U_OUT}

        @block.sync
        def _(sp):
            sp.dma_start(h[:, :, :], xT_in).then_inc(S("x_landed"), 16)
            sp.dma_start(cst[:, :], cst_in).then_inc(S("cst_landed"), 16)
            sp.dma_start(arena[:, A_EARLY:A_EARLY + 384], early_in).then_inc(S("early_landed"), 16)
            for n in range(2):
                sp.dma_start(raw[n][:, :], weights[n, :, :]).then_inc(S(f"raw_landed{n}"), 16)
            sp.dma_start(arena[:, A_GMASK:A_GMASK + 5 * P], masks_in).then_inc(S("masks_landed"), 16)
            with sp.Fori(1, N_UNITS // 2) as i:
                for n in range(2):
                    sp.wait_ge(S("w_lo"), 2 * i + n - 1)
                    sp.dma_start(raw[n][:, :], weights[bass.ds(2 * i + n, 1), :, :].rearrange("a p c -> (a p) c"))\
                      .then_inc(S(f"raw_landed{n}"), 16)
            for k in range(KD):
                sp.wait_ge(S("out_ready"), k + 1)
                sp.dma_start(out[k, :, :], slot(k)).then_inc(S("out_landed"), 16)
            sp.wait_ge(S("out_landed"), 16 * KD)

        def attention(eng, one):
            one(eng, 0, None)
            one(eng, 1, 0)
            with eng.Fori(2, H) as i:
                one(eng, i, i - 1)
            one(eng, None, H - 1)

        @block.tensor
        def _(pe):
            def ffn(f, b, t):
                U = BASE[f"ffn{f}"]
                ffn_pe(pe, f, b, U)
                down_pe(pe, t, FJ, U + 2 * FJ, AU[f"ffn{f}"], ffn_free(f))
                norm_pe(pe, t + 1)

            pe.wait_ge(S("cst_landed"), 16)
            norm_pe(pe, 0)
            ffn(0, 0, 0)
            gdn_pre_pe(pe)
            gdn_cum_pe(pe)
            gdn(pe, gdn_pe)
            down_pe(pe, 1, U_OUT, BASE["gdn_out"], AU["gdn"], {})
            norm_pe(pe, 2)
            ffn(1, 2, 2)
            kv_pe(pe)
            pe.wait_ge(S("v_kept"), 2)
            ffn(2, 4, 3)
            q_pe(pe)
            pe.wait_ge(S("rope_ready"), 8)
            attention(pe, attn_pe)
            down_pe(pe, 4, U_OUT, BASE["attn_out"], AU["attn"], {})
            norm_pe(pe, 5)
            ffn(3, 6, 5)

        @block.scalar
        def _(act):
            def ffn(f, t):
                U = BASE[f"ffn{f}"]
                ffn_act(act, f, U)
                split_a_hi(act, 0, 0, 0)
                split_a_hi(act, 1, 1, 0)
                supply_hi(act, U + 2 * FJ + 1, (U + 1) % 2)
                down_act(act, t, FJ, U + 2 * FJ, AU[f"ffn{f}"])
                norm_act(act, t + 1)

            def enter(b, U):
                build_act(act, b, U)
                supply_hi(act, U + 1, (U + 1) % 2)

            def positions():
                act.dma_start(slot(X_POS).bitcast(I32), pos_in).then_inc(S("pos_landed"), 16)

            act.wait_ge(S("cst_landed"), 16)
            act.wait_ge(S("early_landed"), 16)
            act.activation(bahi[:, :, :].rearrange("p a b -> p (a b)"), arena[:, A_EARLY + 256:A_EARLY + 384], ACT.Copy)\
               .then_inc(S("ba_split"), 1)
            act.wait_ge(S("lam_sum"), 1)
            act.activation(neglam[:, 2:4], neglam[:, 2:4], ACT.Exp).then_inc(S("lam_exp"), 1)
            norm_act(act, 0)
            supply_hi(act, 0, 0)
            enter(0, 0)
            ffn(0, 0)
            enter(1, BASE["gdn_in"])
            gdn_pre_act(act)
            gdn(act, gdn_act)
            act.wait_ge(S("y_ready"), H)
            split_a_hi(act, 0, 0, 0)
            split_a_hi(act, 1, 1, 0)
            down_act(act, 1, U_OUT, BASE["gdn_out"], AU["gdn"])
            norm_act(act, 2)
            enter(2, BASE["ffn1"])
            ffn(1, 2)
            positions()
            enter(3, BASE["kv"])
            kv_act(act)
            enter(4, BASE["ffn2"])
            ffn(2, 3)
            positions()
            enter(5, BASE["q"])
            q_act(act)
            attention(act, attn_act)
            act.wait_ge(S("ay_ready"), H)
            split_a_hi(act, 0, 0, 0)
            split_a_hi(act, 1, 1, 0)
            down_act(act, 4, U_OUT, BASE["attn_out"], AU["attn"])
            norm_act(act, 5)
            enter(6, BASE["ffn3"])
            ffn(3, 5)

        @block.gpsimd
        def _(pool):
            norm_pool(pool, 0)
            norm_pool(pool, 1)
            pool.wait_ge(S("masks_landed"), 16)
            gdn(pool, gdn_pool)
            for r in range(2, 7):
                norm_pool(pool, r)

        @block.vector
        def _(dve):
            def ffn(f, t):
                U = BASE[f"ffn{f}"]
                ffn_dve(dve, f, U, AU[f"ffn{f}"])
                down_dve(dve, t, FJ, U + 2 * FJ, AU[f"ffn{f}"], 0.5)
                norm_dve(dve, t + 1)

            def enter(r, b, U):
                build_dve(dve, r, b, b)
                if b == 3:
                    dve.tensor_copy(acc[:, :], bank[:, 5, :]).then_inc(S("rbc_kept"), 1)
                supply_lo(dve, U + 1, (U + 1) % 2)

            dve.wait_ge(S("cst_landed"), 16)
            dve.wait_ge(S("ba_split"), 1)
            dve.tensor_tensor(balo[:, :, :].rearrange("p a b -> p (a b)"), arena[:, A_EARLY + 256:A_EARLY + 384],
                              bahi[:, :, :].rearrange("p a b -> p (a b)").bitcast(F32), ALU.subtract)\
               .then_inc(S("ba_split"), 1)
            lambda_dve(dve)
            norm_dve(dve, 0)
            supply_lo(dve, 0, 0)
            enter(0, 0, 0)
            ffn(0, 0)
            enter(1, 1, BASE["gdn_in"])
            dve.wait_ge(S("masks_landed"), 16)
            gdn_pre_dve(dve)
            gdn(dve, gdn_dve)
            split_a_lo(dve, 0, 0, AU["gdn"])
            split_a_lo(dve, 1, 1, AU["gdn"])
            down_dve(dve, 1, U_OUT, BASE["gdn_out"], AU["gdn"], 1.0)
            norm_dve(dve, 2)
            enter(2, 2, BASE["ffn1"])
            ffn(1, 2)
            enter(3, 3, BASE["kv"])
            kv_dve(dve)
            enter(3, 4, BASE["ffn2"])
            ffn(2, 3)
            enter(4, 5, BASE["q"])
            q_dve(dve)
            dve.wait_ge(S("lam_ready"), 2)
            dve.memset(slot(X_QZ, 2), 0.0).then_inc(S("qz_zero"), 1)
            dve.wait_ge(S("qz_zero"), 1)
            attention(dve, attn_dve)
            split_a_lo(dve, 0, 0, AU["attn"])
            split_a_lo(dve, 1, 1, AU["attn"])
            down_dve(dve, 4, U_OUT, BASE["attn_out"], AU["attn"], 1.0)
            norm_dve(dve, 5)
            enter(5, 6, BASE["ffn3"])
            ffn(3, 5)
            dve.wait_ge(S("rbc_done"), 7)
            for k in range(KD):
                dve.scalar_tensor_tensor(slot(k), h[:, k, :], cst[:, C_GAIN + 7 * KD + k:C_GAIN + 7 * KD + k + 1],
                                         bank[:, 5, :], ALU.mult, ALU.mult).then_inc(S("out_ready"), 1)




def _constants():
    import numpy as np
    p = np.arange(P)
    ident = np.eye(P)
    upper = p[:, None] <= p[None, :]
    lower = p[:, None] > p[None, :]
    diag = p[:, None] // 16 == p[None, :] // 16
    levels = []
    for w in (16, 32, 64):
        levels.append((p[:, None] // (2 * w) == p[None, :] // (2 * w)) & (p[:, None] % (2 * w) < w)
                      & (p[None, :] % (2 * w) >= w))
    half = ROPE_DIM // 2
    rot = np.zeros((P, P))
    freq = np.zeros(P, np.float32)
    inv = (np.float32(1.0) / (np.float32(ROPE_THETA) ** (np.arange(half, dtype=np.float32) / np.float32(half))))
    for m in range(P):
        f = m % 64
        if f < half:
            rot[m + half, m] = -1.0
        elif f < ROPE_DIM:
            rot[m - half, m] = 1.0
        if f < ROPE_DIM:
            freq[m] = inv[f % half]
    causal = np.where(p[None, :] <= p[:, None], 0.0, -3.0e38)
    cst = np.concatenate([ident, np.ones((P, P)), upper, rot, causal], 1).astype(np.float32)
    masks = np.concatenate([lower, diag, *levels], 1).astype(np.float32)
    return cst, masks, freq


def kernel(**inputs):
    import numpy as np
    import concourse.bacc as bacc
    from concourse.bass_utils import run_bass_kernel_spmd

    a = {k: np.asarray(v) for k, v in inputs.items()}

    def cols(w):
        return w.reshape(KD, P, -1, 256).transpose(2, 1, 0, 3).reshape(-1, P, UNIT)

    def rows(w):
        return w.reshape(-1, 2, P, D).transpose(0, 2, 1, 3).reshape(-1, P, UNIT)

    def ffn(gu, dn):
        both = np.stack([cols(gu[:, :FF]), cols(gu[:, FF:])], 1).reshape(-1, P, UNIT)
        return [both, rows(dn)]

    w_in = a["gdn_w_in"][0]
    q, k, v, z = (w_in[:, n * D:(n + 1) * D].reshape(D, H, P) for n in range(4))
    per_head = np.stack([q, k, v, z], 2).reshape(D, H * 4 * P)
    kv = a["kv_w"]
    v_units = kv[:, D:].reshape(2, 4, P, 2, 512).transpose(3, 0, 2, 1, 4).reshape(4, P, UNIT)
    f1u, f1d, f2u, f2d = (a[n] for n in ("ffn1_w_gate_up", "ffn1_w_down", "ffn2_w_gate_up", "ffn2_w_down"))
    units = [*ffn(f1u[0], f1d[0]), cols(per_head), rows(a["gdn_w_out"][0]), *ffn(f2u[0], f2d[0]),
             cols(kv[:, :D]), v_units, *ffn(f1u[1], f1d[1]), cols(a["diff_w_q"][0]), rows(a["diff_w_out"][0]),
             *ffn(f2u[1], f2d[1])]
    weights = np.concatenate(units, 0)
    assert weights.shape[0] == N_UNITS

    cst, masks, freq = _constants()
    gains = np.stack([a["ffn1_norm"][0], a["mix_norm"][0], a["ffn2_norm"][0], a["kv_norm"], a["ffn1_norm"][1],
                      a["mix_norm"][1], a["ffn2_norm"][1], a["final_norm"]])
    gains = gains.reshape(8, KD, P).transpose(2, 0, 1).reshape(P, 8 * KD)
    conv = a["gdn_conv"][0].reshape(4, 3, H, P).transpose(3, 2, 1, 0).reshape(P, H * 12)

    def on_all(v):
        return np.broadcast_to(v.reshape(1, -1), (P, v.size))

    cst = np.concatenate([cst, gains, conv, on_all(a["gdn_a_log"]), on_all(a["gdn_dt_bias"]),
                          a["gdn_out_norm"].reshape(P, 1), a["diff_subln"].reshape(P, 1), freq.reshape(P, 1)], 1)
    w_ba = w_in[:, 4 * D:].reshape(KD, P, 16).transpose(1, 0, 2).reshape(P, KD * 16)
    early = np.concatenate([on_all(a["diff_lambda"]), w_ba], 1)
    xT = a["x"][0].T.reshape(KD, P, T).transpose(1, 0, 2)
    pos = on_all(a["positions"])

    nc = bacc.Bacc("TRN2", target_bir_lowering=False, num_devices=1)
    arrays, aps = {}, []
    for name, arr in (("weights", weights), ("cst_in", cst), ("masks_in", masks), ("early_in", early),
                      ("xT_in", xT), ("pos_in", pos)):
        arr = np.ascontiguousarray(arr)
        arrays[name] = arr
        aps.append(nc.dram_tensor(name, arr.shape, mybir.dt.from_np(arr.dtype), kind="ExternalInput").ap())
    out = nc.dram_tensor("outT", (KD, P, T), F32, kind="ExternalOutput").ap()
    trunk_kernel(nc, *aps, out)
    r = run_bass_kernel_spmd(nc, [arrays], core_ids=[0])
    return np.ascontiguousarray(r.results[0]["outT"].reshape(D, T).T).reshape(1, T, D)
```

```python
import math
from contextlib import ExitStack

import concourse.bass as bass
from concourse import mybir

ALU = mybir.AluOpType
ACT = mybir.ActivationFunctionType
AX = mybir.AxisListType
F32 = mybir.dt.float32
F32R = mybir.dt.float32r
I32 = mybir.dt.int32

P = 128
D = 1024
T = 512
KD = D // P
TT = T // P
FF = 2816
FT = FF // P
FJ = FT // 2
H = 8
EPS = 1e-6
UNIT = 2048
LAM_INIT = 0.8 - 0.6 * math.exp(-0.3 * 1)
ROPE_THETA = 500000.0
ROPE_DIM = 16

U_FFN = 2 * FJ + FJ
U_IN, U_OUT, U_KV, U_Q = 2 * H, D * D // (P * UNIT), 8, 4
BASE = {}
_at = 0
for _name, _n in (("ffn0", U_FFN), ("gdn_in", U_IN), ("gdn_out", U_OUT), ("ffn1", U_FFN), ("kv", U_KV),
                  ("ffn2", U_FFN), ("q", U_Q), ("attn_out", U_OUT), ("ffn3", U_FFN)):
    BASE[_name] = _at
    _at += _n
N_UNITS = _at

C_IDENT, C_ONES, C_UPPER, C_ROPE, C_CAUSAL = (P * n for n in range(5))
C_GAIN = 5 * P
C_CONV = C_GAIN + 8 * KD
C_ALOG = C_CONV + H * 12
C_DTB = C_ALOG + H
C_ONORM = C_DTB + H
C_SUBLN = C_ONORM + 1
C_FREQ = C_SUBLN + 1
N_CST = C_FREQ + 1

A_ACT, A_SILU, A_KT, A_V = 0, FT * T, FT * T + 2 * T, FT * T + 2 * T + KD * T
N_ARENA = A_V + KD * T
A_EARLY = A_KT
A_GMASK = N_ARENA - 5 * P

HEAD_COLS = 7
K_G, K_CUM, K_BETA, K_NBETA, K_BEXPG, K_KDEC, K_LAST = range(HEAD_COLS)


def trunk_kernel(nc, weights, cst_in, masks_in, early_in, xT_in, pos_in, out):
    ctx = ExitStack()
    with ctx:
        def sb(name, shape, dt=F32):
            return ctx.enter_context(nc.sbuf_tensor(name, shape, dt))

        h = sb("h", [P, KD, T])
        xh = sb("xh", [P, KD, T], F32R)
        xl = sb("xl", [P, KD, T], F32R)
        raw = [sb(f"raw{n}", [P, UNIT]) for n in range(2)]
        whi = [sb(f"whi{n}", [P, UNIT], F32R) for n in range(2)]
        wlo = [sb(f"wlo{n}", [P, UNIT], F32R) for n in range(2)]
        ahi = [sb(f"ahi{n}", [P, 2, T], F32R) for n in range(2)]
        alo = [sb(f"alo{n}", [P, 2, T], F32R) for n in range(2)]
        arena = sb("arena", [P, N_ARENA])
        sq = sb("sq", [P, 2, T])
        acc = sb("acc", [P, T])
        xn = sb("xn", [P, 2, T])
        cst = sb("cst", [P, N_CST])
        bahi = sb("bahi", [P, KD, 16], F32R)
        balo = sb("balo", [P, KD, 16], F32R)
        hc = sb("hc", [P, HEAD_COLS, TT, H])
        hcur = sb("hcur", [P, HEAD_COLS, TT])
        cwh = sb("cwh", [P, 3, 4])
        gcur = sb("gcur", [P, 2, TT])
        st = sb("st", [P, 96])
        neglam = sb("neglam", [P, 4])
        bank = ctx.enter_context(nc.psum_tensor("bank", [P, 8, T], F32))

        ident = cst[:, C_IDENT:C_IDENT + P]
        ones = cst[:, C_ONES:C_ONES + P]
        upper = cst[:, C_UPPER:C_UPPER + P]
        rope_rot = cst[:, C_ROPE:C_ROPE + P]
        causal = cst[:, C_CAUSAL:C_CAUSAL + P]

        def slot(n, w=1):
            return arena[:, n * T:(n + w) * T]

        def c4(ap):
            return ap.rearrange("p (c t) -> p c t", c=TT)

        def over_t(cols):
            return cols.unsqueeze(2).to_broadcast([P, TT, P])

        def over_c(mask):
            return mask.unsqueeze(1).to_broadcast([P, TT, P])

        (G_QS, G_KS, G_Q, G_K, G_V, G_Z, G_DL, G_DU, G_D, G_EG, G_QD, G_QK, G_NA, G_N0, G_N0T, G_NAT,
         G_B1, G_B2, G_B3, G_N2, G_N2T, G_N4, G_TA, G_TB, G_KBG, G_KD, G_VB) = range(8, 35)
        PRE0 = 35 * T
        S0 = PRE0 + 3 * (T + 4)
        assert S0 + P <= A_GMASK
        pre3 = arena[:, PRE0:S0].rearrange("p (q t) -> p q t", q=3)
        pre_pad = pre3[:, :, 0:3]
        state = arena[:, S0:S0 + P]
        gm_lower, gm_diag, gm_b1, gm_b2, gm_b3 = (arena[:, A_GMASK + n * P:A_GMASK + (n + 1) * P] for n in range(5))

        sems = {}

        def S(name):
            if name not in sems:
                sems[name] = ctx.enter_context(nc.semaphore(name))
            return sems[name]

        block = ctx.enter_context(nc.Block())

        def past(count):
            return not isinstance(count, int) or count > 0

        def supply_hi(act, n, s):
            act.wait_ge(S(f"raw_landed{s}"), (n - s) * 8 + 16)
            if past(n - 1):
                act.wait_ge(S("unit_used"), n - 1)
            act.activation(whi[s][:, :], raw[s][:, :], ACT.Copy).then_inc(S("w_hi"), 1)

        def supply_lo(dve, n, s):
            dve.wait_ge(S("w_hi"), n + 1)
            dve.tensor_tensor(wlo[s][:, :], raw[s][:, :], whi[s][:, :].bitcast(F32), ALU.subtract)\
               .then_inc(S("w_lo"), 1)

        def mm3(pe, o, ah, al, bh, bl, start, stop):
            pe.matmul(o, ah, bh, start=start, stop=False)
            pe.matmul(o, ah, bl, start=False, stop=False)
            return pe.matmul(o, al, bh, start=False, stop=stop)

        def w_block(s, lo, width=P):
            return whi[s][:, lo:lo + width], wlo[s][:, lo:lo + width]

        def project_unit(pe, s, banks, x_build=None, part=None):
            a, b = part or (0, 2 * KD)
            for n in range(a, b):
                k, f = n // 2, n % 2
                if x_build is not None and f == 0:
                    pe.wait_ge(S("x_lo"), 8 * x_build + k + 1)
                last = mm3(pe, bank[:, banks[f], :], *w_block(s, k * 256 + f * P), xh[:, k, :], xl[:, k, :],
                           k == 0, k == KD - 1)
            return last

        def norm_act(act, r):
            for d in range(KD):
                if r == 0:
                    if d == 0:
                        act.wait_ge(S("x_landed"), 16)
                else:
                    act.wait_ge(S("h_ready"), 8 * (r - 1) + d + 1)
                if d == 0:
                    if past(6 * r):
                        act.wait_ge(S("sq_summed"), 6 * r)
                elif d == 1:
                    if past(r):
                        act.wait_ge(S("ss_done"), r)
                else:
                    act.wait_ge(S("sq_summed"), 6 * r + max(d - 2, 1))
                act.activation(sq[:, d % 2, :], h[:, d, :], ACT.Square).then_inc(S("sq_ready"), 1)

        def norm_pool(pool, r):
            if past(r):
                pool.wait_ge(S("ss_done"), r)
            if r == 4:
                pool.wait_ge(S("xn_ready"), 40)
            for d in range(1, KD - 1):
                pool.wait_ge(S("sq_ready"), 8 * r + d + 1)
                if d == 1:
                    ins = pool.tensor_tensor(acc[:, :], sq[:, 0, :], sq[:, 1, :], ALU.add)
                else:
                    pool.wait_ge(S("sq_summed"), 6 * r + d - 1)
                    ins = pool.tensor_tensor(acc[:, :], acc[:, :], sq[:, d % 2, :], ALU.add)
                ins.then_inc(S("sq_summed"), 1)

        def norm_pe(pe, r):
            pe.wait_ge(S("sq_summed"), 6 * (r + 1))
            pe.wait_ge(S("sq_ready"), 8 * (r + 1))
            if r:
                pe.wait_ge(S("h_ready"), 8 * (r - 1) + 2)
            for t in range(TT):
                pe.matmul(bank[:, 4, t:t + 1], acc[:, t * P:(t + 1) * P], ones[:, 0:1], start=True, stop=False)
                last = pe.matmul(bank[:, 4, t:t + 1], sq[:, 1, t * P:(t + 1) * P], ones[:, 0:1],
                                 start=False, stop=True)
            last.then_inc(S("ss_done"), 1)
            pe.wait_ge(S("rstd_ready"), r + 1)
            spread(pe, bank[:, 5, :], st[:, 16:20]).then_inc(S("rbc_done"), 1)

        def spread(pe, o, cols):
            for t in range(TT):
                last = pe.matmul(o[:, t * P:(t + 1) * P], cols[:, t:t + 1].to_broadcast([P, P]), ident,
                                 start=True, stop=True)
            return last

        class Steps:

            def __init__(self, eng, name, base=0):
                self.eng, self.name, self.base, self.n = eng, name, base, 0

            def link(self, ins):
                self.n += 1
                ins.then_inc(S(self.name), 1)
                self.eng.wait_ge(S(self.name), self.base + self.n)

        RSQRT = 10

        def rsqrt(eng, steps, v, tmp, o, done):
            steps.link(eng.tensor_scalar(o.bitcast(I32), v.bitcast(I32), -0.5, float(0x5F3759DF), ALU.mult, ALU.add))
            yield
            for n in range(3):
                steps.link(eng.tensor_tensor(tmp, o, v, ALU.mult))
                yield
                steps.link(eng.scalar_tensor_tensor(tmp, tmp, -0.5, o, ALU.mult, ALU.mult))
                yield
                ins = eng.scalar_tensor_tensor(o, tmp, 1.5, o, ALU.add, ALU.mult)
                if n < 2:
                    steps.link(ins)
                else:
                    ins.then_inc(S(done), 1)
                yield

        def norm_dve(dve, r):
            dve.wait_ge(S("ss_done"), r + 1)
            steps = Steps(dve, "small_step", RSQRT * r)
            steps.link(dve.tensor_scalar(st[:, 4:8], bank[:, 4, 0:4], 1.0 / D, EPS, ALU.mult, ALU.add))
            if past(r):
                dve.wait_ge(S("rbc_done"), r)
            for last in rsqrt(dve, steps, st[:, 4:8], st[:, 12:16], st[:, 16:20], "rstd_ready"):
                pass

        def build_dve(dve, r, b, g):
            kept = b == 4
            rbc = acc[:, :] if kept else bank[:, 5, :]
            dve.wait_ge(S("rbc_done"), r + 1)
            if kept:
                dve.wait_ge(S("rbc_kept"), 1)
            for k in range(KD + 1):
                if k < KD:
                    if k >= 2:
                        dve.wait_ge(S("x_lo"), 8 * b + k - 1)
                    elif b:
                        dve.wait_ge(S("x_lo"), 8 * b)
                    dve.scalar_tensor_tensor(xn[:, k % 2, :], h[:, k, :], cst[:, C_GAIN + g * KD + k:C_GAIN + g * KD + k + 1],
                                             rbc, ALU.mult, ALU.mult).then_inc(S("xn_ready"), 1)
                if k:
                    dve.wait_ge(S("x_hi"), 8 * b + k)
                    dve.tensor_tensor(xl[:, k - 1, :], xn[:, (k - 1) % 2, :], xh[:, k - 1, :].bitcast(F32),
                                      ALU.subtract).then_inc(S("x_lo"), 1)

        def build_act(act, b, n_used):
            if past(n_used):
                act.wait_ge(S("unit_used"), n_used)
            for k in range(KD):
                act.wait_ge(S("xn_ready"), 8 * b + k + 1)
                act.activation(xh[:, k, :], xn[:, k % 2, :], ACT.Copy).then_inc(S("x_hi"), 1)

        def ffn_pe(pe, f, b, U):
            s = U % 2

            def gate(j, first=False):
                pe.wait_ge(S("w_lo"), U + 2 * j + 1)
                if past(FJ * f + j):
                    pe.wait_ge(S("silu_ready"), FJ * f + j)
                project_unit(pe, s, (0, 1), b if first else None).then_inc(S("unit_used"), 1)

            def up(j):
                pe.wait_ge(S("w_lo"), U + 2 * j + 2)
                if past(FJ * f + j):
                    pe.wait_ge(S("act_ready"), FJ * f + j)
                project_unit(pe, 1 - s, (2, 3)).then_inc(S("unit_used"), 1)

            gate(0, True)
            up(0)
            with pe.Fori(1, FJ) as j:
                gate(j)
                up(j)

        def ffn_free(f):
            return {4: ("silu_ready", FJ * (f + 1)), 6: ("act_ready", FJ * (f + 1))}

        def ffn_act(act, f, U):
            s = U % 2

            def silu(j):
                act.wait_ge(S("unit_used"), U + 2 * j + 1)
                if past(FJ * f + j):
                    act.wait_ge(S("act_ready"), FJ * f + j)
                act.activation(arena[:, A_SILU:A_SILU + 2 * T].rearrange("p (a t) -> p a t", a=2), bank[:, 0:2, :],
                               ACT.Silu).then_inc(S("silu_ready"), 1)

            supply_hi(act, U + 2, s)
            silu(0)
            with act.Fori(1, FJ) as j:
                supply_hi(act, U + 2 * j + 1, 1 - s)
                supply_hi(act, U + 2 * j + 2, s)
                silu(j)

        def ffn_dve(dve, f, U, AU):
            s = U % 2

            def product(j):
                dve.wait_ge(S("unit_used"), U + 2 * j + 2)
                dve.wait_ge(S("silu_ready"), FJ * f + j + 1)
                dve.tensor_tensor(arena[:, bass.ds(A_ACT + j * (2 * T), 2 * T)].rearrange("p (a t) -> p a t", a=2),
                                  arena[:, A_SILU:A_SILU + 2 * T].rearrange("p (a t) -> p a t", a=2),
                                  bank[:, 2:4, :], ALU.mult).then_inc(S("act_ready"), 1)

            with dve.Fori(0, FJ - 1) as j:
                supply_lo(dve, U + 2 * j + 2, s)
                product(j)
                supply_lo(dve, U + 2 * j + 3, 1 - s)
            supply_lo(dve, U + 2 * FJ, s)
            split_a_lo(dve, 0, 0, AU)
            split_a_lo(dve, 1, 1, AU)
            product(FJ - 1)
            supply_lo(dve, U + 2 * FJ + 1, 1 - s)

        def a_pair(u):
            return arena[:, bass.ds(A_ACT + u * (2 * T), 2 * T)].rearrange("p (a t) -> p a t", a=2)

        def split_a_hi(act, u, s, AU):
            act.activation(ahi[s][:, :, :], a_pair(u), ACT.Copy).then_inc(S("a_hi"), 1)

        def split_a_lo(dve, u, s, AU):
            dve.wait_ge(S("a_hi"), AU + u + 1)
            dve.tensor_tensor(alo[s][:, :, :], a_pair(u), ahi[s][:, :, :].bitcast(F32), ALU.subtract)\
               .then_inc(S("a_lo"), 1)

        def down_pe(pe, t, n, U, AU, free):
            def unit(u, first=False, last=False):
                ws, xs = (U + u) % 2, u % 2
                if first:
                    pe.wait_ge(S("a_lo"), AU + 1)
                pe.wait_ge(S("w_lo"), U + u + 1)
                pe.wait_ge(S("a_lo"), AU + u + 1)
                order = [(d, kt) for d in range(KD) for kt in range(2)] if last else \
                    [(d, kt) for kt in range(2) for d in range(KD)]
                for d, kt in order:
                    if first and kt == 0 and d in free:
                        pe.wait_ge(S(free[d][0]), free[d][1])
                    ins = mm3(pe, bank[:, (d + 4) % 8, :], *w_block(ws, kt * D + d * P), ahi[xs][:, kt, :],
                              alo[xs][:, kt, :], first and kt == 0, last and kt == 1)
                    if last and kt == 1 and d < KD - 1:
                        ins.then_inc(S("down_done"), 1)
                ins.then_inc(S("unit_used"), 1)

            unit(0, first=True)
            pairs = max(0, (n - 2) // 2 - (n < 6))
            if pairs:
                with pe.Fori(0, pairs) as i:
                    for q in range(2):
                        loop_unit(pe, i, q, U, AU)
            for u in range(1 + 2 * pairs, n - 1):
                unit(u)
            unit(n - 1, last=True)

        def loop_unit(pe, i, q, U, AU):
            ws, xs = (U + 1 + q) % 2, (1 + q) % 2
            pe.wait_ge(S("w_lo"), U + 2 * i + q + 2)
            pe.wait_ge(S("a_lo"), AU + 2 * i + q + 2)
            for kt in range(2):
                for d in range(KD):
                    ins = mm3(pe, bank[:, (d + 4) % 8, :], *w_block(ws, kt * D + d * P), ahi[xs][:, kt, :],
                              alo[xs][:, kt, :], False, False)
            ins.then_inc(S("unit_used"), 1)

        def down_act(act, t, n, U, AU):
            def after(u, sw, sa, a):
                supply_hi(act, U + u + 2, sw)
                if a:
                    act.wait_ge(S("unit_used"), U + u + 1)
                    split_a_hi(act, u + 2, sa, AU)

            loops = (n - 3) // 2 if n > 4 else 0
            if loops:
                with act.Fori(0, loops) as i:
                    after(2 * i, U % 2, 0, True)
                    after(2 * i + 1, (U + 1) % 2, 1, True)
            for u in range(2 * loops, n - 1):
                if U + u + 2 < N_UNITS:
                    supply_hi(act, U + u + 2, (U + u) % 2)
                if u + 2 < n:
                    act.wait_ge(S("unit_used"), U + u + 1)
                    split_a_hi(act, u + 2, u % 2, AU)

        def down_dve(dve, t, n, U, AU, scale):
            loops = (n - 3) // 2 if n > 4 else 0
            if loops:
                with dve.Fori(0, loops) as i:
                    for q in range(2):
                        supply_lo(dve, U + 2 * i + q + 2, (U + q) % 2)
                        dve.wait_ge(S("a_hi"), AU + 2 * i + q + 3)
                        dve.tensor_tensor(alo[q][:, :, :], a_pair(2 * i + q + 2), ahi[q][:, :, :].bitcast(F32),
                                          ALU.subtract).then_inc(S("a_lo"), 1)
            for u in range(2 * loops, n - 1):
                if U + u + 2 < N_UNITS:
                    supply_lo(dve, U + u + 2, (U + u) % 2)
                if u + 2 < n:
                    split_a_lo(dve, u + 2, u % 2, AU)
            for d in range(KD):
                if d < KD - 1:
                    dve.wait_ge(S("down_done"), 7 * t + d + 1)
                else:
                    dve.wait_ge(S("unit_used"), U + n)
                dve.scalar_tensor_tensor(h[:, d, :], bank[:, (d + 4) % 8, :], scale, h[:, d, :], ALU.mult, ALU.add)\
                   .then_inc(S("h_ready"), 1)

        def gdn_pre_pe(pe):
            pe.wait_ge(S("x_lo"), 16)
            pe.wait_ge(S("ba_split"), 2)
            for t in range(TT):
                for k in range(KD):
                    last = mm3(pe, bank[:, 6, t * 16:(t + 1) * 16], xh[:, k, t * P:(t + 1) * P],
                               xl[:, k, t * P:(t + 1) * P], bahi[:, k, :], balo[:, k, :], k == 0, k == KD - 1)
            last.then_inc(S("ba_done"), 1)

        def gdn_cum_pe(pe):
            pe.wait_ge(S("pre_dve"), PRE_G)
            g = hc[:, K_G, :, :].rearrange("p a b -> p (a b)")
            pe.matmul(bank[:, 7, 0:32], upper, g, start=True, stop=True)
            pe.matmul(bank[:, 7, 32:64], ones, g, start=True, stop=True).then_inc(S("cum_done"), 1)

        PRE_G = 12
        small = [slot(0)[:, n * 32:(n + 1) * 32].rearrange("p (a b) -> p a b", a=TT) for n in range(16)]
        sm_x, sm_e1, sm_ax, sm_e2, sm_u, sm_ln, sm_t, sm_ru, sm_gl, sm_d, sm_eg = small[2:13]
        ba = slot(0)[:, 0:64].rearrange("p (a b) -> p a b", a=TT)
        alog_e = slot(0)[:, 480:488]

        def gdn_pre_act(act):
            act.wait_ge(S("pre_dve"), 2)
            act.activation(sm_e1, ba[:, :, 0:H], ACT.Exp, scale=-1.0).then_inc(S("pre_act"), 1)
            act.activation(sm_ax, sm_x, ACT.Abs).then_inc(S("pre_act"), 1)
            act.activation(alog_e, cst[:, C_ALOG:C_ALOG + H], ACT.Exp).then_inc(S("pre_act"), 1)
            act.wait_ge(S("pre_act"), 3)
            act.activation(sm_e2, sm_ax, ACT.Exp, scale=-1.0).then_inc(S("pre_act"), 1)
            act.wait_ge(S("pre_dve"), 3)
            act.activation(sm_ln, sm_u, ACT.Ln).then_inc(S("pre_act"), 1)
            act.wait_ge(S("pre_dve"), PRE_G + 3)
            act.activation(sm_eg, hc[:, K_CUM, :, :], ACT.Exp).then_inc(S("pre_act"), 1)
            act.activation(hc[:, K_KDEC, :, :], sm_d, ACT.Exp).then_inc(S("pre_act"), 1)
            act.activation(hc[:, K_LAST, :, :], sm_gl, ACT.Exp).then_inc(S("pre_act"), 1)

        def gdn_pre_dve(dve):
            dve.memset(pre_pad, 0.0).then_inc(S("pad_ready"), 1)
            st_ = Steps(dve, "pre_dve")
            dve.wait_ge(S("ba_done"), 1)
            st_.link(dve.tensor_copy(slot(0)[:, 0:64], bank[:, 6, 0:64]))
            dtb = cst[:, C_DTB:C_DTB + H].unsqueeze(1).to_broadcast([P, TT, H])
            st_.link(dve.tensor_tensor(sm_x, ba[:, :, H:2 * H], dtb, ALU.add))
            dve.wait_ge(S("pre_act"), 4)
            st_.link(dve.tensor_scalar(sm_u, sm_e2, 1.0, None, ALU.add))
            st_.link(dve.scalar_tensor_tensor(sm_t, sm_u, -1.0, sm_e2, ALU.add, ALU.subtract))
            st_.link(dve.reciprocal(sm_ru, sm_u))
            st_.link(dve.tensor_tensor(sm_t, sm_t, sm_ru, ALU.mult))
            dve.wait_ge(S("pre_act"), 5)
            st_.link(dve.tensor_tensor(sm_ln, sm_ln, sm_t, ALU.subtract))
            st_.link(dve.scalar_tensor_tensor(sm_x, sm_x, 0.0, sm_ln, ALU.max, ALU.add))
            st_.link(dve.scalar_tensor_tensor(hc[:, K_G, :, :], sm_x, -1.0,
                                              alog_e.unsqueeze(1).to_broadcast([P, TT, H]), ALU.mult, ALU.mult))
            st_.link(dve.tensor_scalar(sm_e1, sm_e1, 1.0, None, ALU.add))
            st_.link(dve.reciprocal(hc[:, K_BETA, :, :], sm_e1))
            st_.link(dve.tensor_scalar(hc[:, K_NBETA, :, :], hc[:, K_BETA, :, :], -1.0, None, ALU.mult))
            assert st_.n == PRE_G
            dve.wait_ge(S("cum_done"), 1)
            flat = "p a b -> p (a b)"
            st_.link(dve.tensor_copy(hc[:, K_CUM, :, :].rearrange(flat), bank[:, 7, 0:32]))
            st_.link(dve.tensor_copy(sm_gl.rearrange(flat), bank[:, 7, 32:64]))
            st_.link(dve.tensor_tensor(sm_d, sm_gl, hc[:, K_CUM, :, :], ALU.subtract))
            dve.wait_ge(S("pre_act"), 8)
            st_.link(dve.tensor_tensor(hc[:, K_BEXPG, :, :], hc[:, K_BETA, :, :], sm_eg, ALU.mult))

        def chunks(pe, b, lhs, rhs, start=True, stop=True):
            for n in range(TT):
                cs = slice(n * P, (n + 1) * P)
                last = pe.matmul(bank[:, b, cs], lhs[:, cs], rhs[:, cs], start=start, stop=stop)
            return last

        def turned(pe, b, src):
            for n in range(TT):
                cs = slice(n * P, (n + 1) * P)
                last = pe.transpose(bank[:, b, cs], src[:, cs], ident)
            return last

        def gdn_pe(pe, hp, c, o):
            U = BASE["gdn_in"]
            core, proj, fin = c is not None, hp is not None, o is not None
            UA = U + 2 * hp if proj else None
            at = 0

            def more(count):
                nonlocal at
                if not proj:
                    return
                for n in range(at, at + count):
                    f, k = n // KD, n % KD
                    if n == 0:
                        pe.wait_ge(S("w_lo"), UA + 1)
                        if core:
                            pe.wait_ge(S("k_ready"), hp)
                    if n == 2 * KD:
                        pe.wait_ge(S("w_lo"), UA + 2)
                        if core:
                            pe.wait_ge(S("expg_ready"), hp)
                    if n == 3 * KD and core:
                        pe.wait_ge(S("z_silu"), hp)
                    ins = mm3(pe, bank[:, f, :], *w_block((U + f // 2) % 2, k * 256 + (f % 2) * P), xh[:, k, :],
                              xl[:, k, :], k == 0, k == KD - 1)
                    if k == KD - 1:
                        ins.then_inc(S(("q_projected", "unit_used", "v_projected", "unit_used")[f]), 1)
                at += count

            if core:
                pe.wait_ge(S("k_ready"), c + 1)
                chunks(pe, 4, slot(G_K), slot(G_K)).then_inc(S("kk_done"), 1)
                chunks(pe, 7, slot(G_K), slot(G_Q)).then_inc(S("qk_done"), 1)
            more(3)
            if core:
                pe.wait_ge(S("na_ready"), c + 1)
                turned(pe, 4, slot(G_NA)).then_inc(S("nat_done"), 1)
            more(2)
            if core:
                pe.wait_ge(S("n0t_ready"), c + 1)
                if fin:
                    pe.wait_ge(S("oc_ready"), c)
                chunks(pe, 5, slot(G_N0T), slot(G_N0)).then_inc(S("n2_done"), 1)
                if fin:
                    pe.wait_ge(S("wt_ready"), c)
                chunks(pe, 6, slot(G_N0), slot(G_N0T)).then_inc(S("n2t_done"), 1)
            more(1)
            if core:
                pe.wait_ge(S("n2_ready"), c + 1)
                pe.wait_ge(S("n2t_ready"), c + 1)
                pe.wait_ge(S("nat_ready"), c + 1)
                chunks(pe, 4, slot(G_N2), slot(G_N2T)).then_inc(S("n4t_done"), 1)
                pe.wait_ge(S("qkm_ready"), c + 1)
                chunks(pe, 7, slot(G_N2T), slot(G_N2)).then_inc(S("n4_done"), 1)
                pe.wait_ge(S("t1_ready"), c + 1)
                chunks(pe, 5, slot(G_N2T), slot(G_TA)).then_inc(S("p2_done"), 1)
            more(1)
            if core:
                pe.wait_ge(S("n4t_ready"), c + 1)
                pe.wait_ge(S("n4_ready"), c + 1)
                chunks(pe, 6, slot(G_N4), slot(G_N0T)).then_inc(S("n8t_done"), 1)
                pe.wait_ge(S("t2_ready"), c + 1)
                chunks(pe, 7, slot(G_N0T), slot(G_TB)).then_inc(S("p4_done"), 1)
                pe.wait_ge(S("v_silu"), c + 1)
                turned(pe, 5, slot(G_V)).then_inc(S("vtr_done"), 1)
            more(2)
            if core:
                pe.wait_ge(S("n8t_ready"), c + 1)
                pe.wait_ge(S("t4_ready"), c + 1)
                chunks(pe, 4, slot(G_NA), slot(G_TA)).then_inc(S("p8_done"), 1)
                turned(pe, 6, slot(G_K)).then_inc(S("ktr_done"), 1)
            more(2)
            if core:
                pe.wait_ge(S("t8_ready"), c + 1)
                pe.wait_ge(S("vb_ready"), c + 1)
                turned(pe, 5, slot(G_TB)).then_inc(S("tt_done"), 1)
                pe.wait_ge(S("b_ready"), 3 * c + 1)
                pe.wait_ge(S("kd_ready"), c + 1)
                chunks(pe, 6, slot(G_B1), slot(G_TB)).then_inc(S("w1_done"), 1)
            more(2)
            if core:
                pe.wait_ge(S("tt_ready"), c + 1)
                pe.wait_ge(S("w1_ready"), c + 1)
                chunks(pe, 7, slot(G_N2), slot(G_N2T)).then_inc(S("ta_done"), 1)
                chunks(pe, 4, slot(G_N2T), slot(G_N2)).then_inc(S("tta_done"), 1)
            if fin:
                if not core:
                    pe.wait_ge(S("wt_ready"), H)
                pe.wait_ge(S("on_ready"), o + 1)
                turned(pe, 6, xn[:, 1, :]).then_inc(S("otr_done"), 1)
            more(2)
            if core:
                pe.wait_ge(S("ta_ready"), c + 1)
                pe.wait_ge(S("b_ready"), 3 * c + 2)
                chunks(pe, 5, slot(G_B2), slot(G_TA)).then_inc(S("w2_done"), 1)
            more(2)
            if core:
                pe.wait_ge(S("tta_ready"), c + 1)
                pe.wait_ge(S("w2_ready"), c + 1)
                if fin:
                    pe.wait_ge(S("y_ready"), o + 1)
                chunks(pe, 6, slot(G_N4), slot(G_N2T)).then_inc(S("tb_done"), 1)
                chunks(pe, 7, slot(G_N2T), slot(G_N4)).then_inc(S("ttb_done"), 1)
            more(2)
            if core:
                pe.wait_ge(S("tb_ready"), c + 1)
                pe.wait_ge(S("b_ready"), 3 * c + 3)
                chunks(pe, 4, slot(G_B3), slot(G_TB)).then_inc(S("w3_done"), 1)
            more(2)
            if core:
                pe.wait_ge(S("ttb_ready"), c + 1)
                pe.wait_ge(S("w3_ready"), c + 1)
                chunks(pe, 5, slot(G_N2T), slot(G_N2)).then_inc(S("ttc_done"), 1)
            more(2)
            if core:
                pe.wait_ge(S("ttc_ready"), c + 1)
                chunks(pe, 6, slot(G_KBG), slot(G_N4)).then_inc(S("wt_done"), 1)
            more(1)
            if proj:
                pe.wait_ge(S("qk_sq"), 2 * hp + 2)
                for q in range(2):
                    for t in range(TT):
                        ins = pe.matmul(bank[:, 0, q * TT + t:q * TT + t + 1], sq[:, q, t * P:(t + 1) * P],
                                        ones[:, 0:1], start=True, stop=True)
                ins.then_inc(S("qk_ss"), 1)
            for n in range(TT):
                cs = slice(n * P, (n + 1) * P)
                if core:
                    ins = pe.matmul(bank[:, 7, cs], slot(G_N4)[:, cs], slot(G_VB)[:, cs], start=True, stop=n == 0)
                    if n == 0:
                        pe.wait_ge(S("wt_ready"), c + 1)
                    else:
                        pe.wait_ge(S("s_ready"), 3 * c + n)
                        ins = pe.matmul(bank[:, 7, cs], slot(G_N0)[:, cs], state, start=False, stop=True)
                    ins.then_inc(S("u_done"), 1)
                    if n == 0:
                        pe.wait_ge(S("qd_ready"), c + 1)
                    else:
                        pe.matmul(bank[:, 5, cs], slot(G_QD)[:, cs], state, start=True, stop=False)
                if n < 2:
                    more(1)
                elif proj and n == 2:
                    pe.wait_ge(S("gcur_ready"), 2 * hp + 2)
                    pe.wait_ge(S("v_pre"), hp + 1)
                    for t in range(TT):
                        ins = pe.matmul(bank[:, 2, t * P:(t + 1) * P], gcur[:, 0, t:t + 1].to_broadcast([P, P]),
                                        upper, start=True, stop=True)
                    ins.then_inc(S("gbc_done"), 1)
                elif proj:
                    spread(pe, bank[:, 0, :], st[:, 48:52]).then_inc(S("k_bc"), 1)
                if core:
                    pe.wait_ge(S("u_ready"), 4 * c + n + 1)
                    if n < TT - 1:
                        pe.matmul(bank[:, 4, 0:P], slot(G_KD)[:, cs], slot(G_N0T)[:, cs], start=True, stop=True)\
                          .then_inc(S("s_done"), 1)
                    ins = pe.matmul(bank[:, 5, cs], slot(G_QK)[:, cs], slot(G_N0T)[:, cs], start=n == 0, stop=True)
                    if n == TT - 1:
                        ins.then_inc(S("o_done"), 1)
                if n < 2:
                    more(1)
                elif proj and n == 2:
                    pe.wait_ge(S("qk_rn"), hp + 1)
                    spread(pe, bank[:, 1, :], st[:, 44:48]).then_inc(S("q_bc"), 1)
            more(4)
            assert at in (0, 4 * KD)

        def gdn_act(act, hp, c, o):
            U = BASE["gdn_in"]
            core, proj, fin = c is not None, hp is not None, o is not None
            UA = U + 2 * hp if proj else None

            def keep(b, dst, need, name, scale=1.0):
                if core:
                    act.wait_ge(S(need), c + 1)
                    act.activation(slot(dst), bank[:, b, :], ACT.Copy, scale=scale).then_inc(S(name), 1)

            def silu_square(q):
                if proj:
                    x = slot(G_QS + q)
                    act.wait_ge(S("qk_conv"), 8 * hp + 4 * q + 4)
                    act.activation(x, x, ACT.Silu).then_inc(S("qk_silu"), 1)
                    act.wait_ge(S("qk_silu"), 2 * hp + q + 1)
                    if core:
                        act.wait_ge(S("qk_ss"), hp)
                    act.activation(sq[:, q, :], x, ACT.Square).then_inc(S("qk_sq"), 1)

            if core:
                act.wait_ge(S("v_conv"), 4 * c + 4)
                act.activation(slot(G_V), slot(G_V), ACT.Silu).then_inc(S("v_silu"), 1)
                supply_hi(act, U + 2 * c + 3, (U + 1) % 2)
                act.wait_ge(S("n0t_ready"), c + 1)
            keep(4, G_NAT, "nat_done", "nat_ready")
            keep(5, G_N2, "n2_done", "n2_ready")
            keep(7, G_N4, "n4_done", "n4_ready")
            keep(6, G_NA, "n8t_done", "n8t_ready")
            if proj:
                act.wait_ge(S("q_projected"), hp + 1)
                act.wait_ge(S("pad_ready"), 1)
                if core:
                    act.wait_ge(S("qk_conv"), 8 * hp)
                act.activation(pre3[:, 0, 3:3 + T], bank[:, 0, :], ACT.Copy).then_inc(S("qk_pre"), 1)
            keep(5, G_N2, "tt_done", "tt_ready")
            keep(5, G_N2T, "w2_done", "w2_ready")
            if proj:
                act.wait_ge(S("unit_used"), UA + 1)
                act.activation(pre3[:, 1, 3:3 + T], bank[:, 1, :], ACT.Copy).then_inc(S("qk_pre"), 1)
            if core:
                if fin:
                    act.wait_ge(S("y_ready"), c)
                act.wait_ge(S("unit_used"), U + 2 * c + 2)
                act.activation(slot(G_Z), bank[:, 3, :], ACT.Silu).then_inc(S("z_silu"), 1)
            silu_square(0)
            keep(4, G_N2T, "w3_done", "w3_ready")
            if proj:
                supply_hi(act, UA + 2, U % 2)
            silu_square(1)
            keep(6, G_N0, "wt_done", "wt_ready", -1.0)
            if proj:
                act.wait_ge(S("v_projected"), hp + 1)
                if core:
                    act.wait_ge(S("v_conv"), 4 * hp)
                act.activation(pre3[:, 2, 3:3 + T], bank[:, 2, :], ACT.Copy).then_inc(S("v_pre"), 1)
                act.wait_ge(S("gbc_done"), hp + 1)
                if core:
                    act.wait_ge(S("du_ready"), hp)
                for t in range(TT):
                    cs = slice(t * P, (t + 1) * P)
                    ins = act.activation(slot(G_D)[:, cs], bank[:, 2, cs], ACT.Abs, scale=-1.0, bias=gcur[:, 1, t:t + 1])
                ins.then_inc(S("dabs_ready"), 1)
                act.wait_ge(S("dabs_ready"), hp + 1)
                act.activation(slot(G_D), slot(G_D), ACT.Exp, scale=-1.0).then_inc(S("decay_ready"), 1)
                if core:
                    act.wait_ge(S("qd_ready"), hp)
                act.activation(slot(G_EG), bank[:, 2, :], ACT.Exp).then_inc(S("expg_ready"), 1)
            if core:
                act.wait_ge(S("o_done"), c + 1)
                if fin:
                    act.wait_ge(S("otr_done"), c)
                for t in range(TT):
                    cs = slice(t * P, (t + 1) * P)
                    act.activation(xn[:, 1, cs], bank[:, 5, cs], ACT.Square, accum_out=st[:, 52 + t:53 + t])
                act.activation(xn[:, 0, :], bank[:, 5, :], ACT.Copy).then_inc(S("oc_ready"), 1)

        def gdn_dve(dve, hp, c, o):
            core, proj, fin = c is not None, hp is not None, o is not None

            def add(b, a, o, need, name):
                if core:
                    dve.wait_ge(S(need), c + 1)
                    dve.tensor_tensor(slot(o), bank[:, b, :], slot(a), ALU.add).then_inc(S(name), 1)

            def keep(b, dst, need, name):
                if core:
                    dve.wait_ge(S(need), c + 1)
                    dve.tensor_copy(slot(dst), bank[:, b, :]).then_inc(S(name), 1)

            def conv(q, dst, name, base):
                if not proj:
                    return
                for j in range(4):
                    x, w = pre3[:, q, j:j + T], cwh[:, q, j:j + 1]
                    if j == 0:
                        ins = dve.tensor_scalar(slot(dst), x, w, None, ALU.mult)
                    else:
                        dve.wait_ge(S(name), base + j)
                        ins = dve.scalar_tensor_tensor(slot(dst), x, w, slot(dst), ALU.mult, ALU.add)
                    ins.then_inc(S(name), 1)

            o_steps = Steps(dve, "o_step", RSQRT * o if fin else 0)
            o_norm = rsqrt(dve, o_steps, st[:, 56:60], st[:, 76:80], st[:, 80:84], "o_rn")

            def out_steps(count):
                if fin:
                    for _ in range(count):
                        next(o_norm)

            if fin:
                dve.wait_ge(S("oc_ready"), o + 1)
                o_steps.link(dve.tensor_scalar(st[:, 56:60], st[:, 52:56], 1.0 / P, EPS, ALU.mult, ALU.add))
            if core:
                if fin:
                    dve.wait_ge(S("s_ready"), 3 * c)
                dve.tensor_copy(hcur[:, :, :], hc[:, :, :, bass.ds(c, 1)].rearrange("p a b c -> p a (b c)"))\
                   .then_inc(S("hcur_ready"), 1)
                dve.wait_ge(S("kk_done"), c + 1)
                dve.wait_ge(S("dl_ready"), c + 1)
                dve.tensor_tensor(slot(G_NA), bank[:, 4, :], slot(G_DL), ALU.mult).then_inc(S("na_ready"), 1)
                dve.wait_ge(S("na_ready"), c + 1)
                dve.tensor_tensor(c4(slot(G_N0)), c4(slot(G_NA)), over_c(gm_diag), ALU.mult)\
                   .then_inc(S("n0_ready"), 1)
            out_steps(1)
            if core:
                dve.wait_ge(S("nat_done"), c + 1)
                dve.tensor_tensor(c4(slot(G_N0T)), c4(bank[:, 4, :]), over_c(gm_diag), ALU.mult)\
                   .then_inc(S("n0t_ready"), 1)
            out_steps(3)
            keep(6, G_N2T, "n2t_done", "n2t_ready")
            if core:
                dve.wait_ge(S("qk_done"), c + 1)
                dve.wait_ge(S("du_ready"), c + 1)
                dve.tensor_tensor(slot(G_QK), bank[:, 7, :], slot(G_DU), ALU.mult).then_inc(S("qkm_ready"), 1)
            out_steps(2)
            keep(4, G_N0T, "n4t_done", "n4t_ready")
            add(5, G_TA, G_TB, "p2_done", "t2_ready")
            out_steps(4)
            add(7, G_TB, G_TA, "p4_done", "t4_ready")
            if core:
                dve.wait_ge(S("hcur_ready"), c + 1)
                dve.wait_ge(S("vtr_done"), c + 1)
                dve.tensor_tensor(c4(slot(G_VB)), c4(bank[:, 5, :]), over_t(hcur[:, K_BETA, :]), ALU.mult)\
                   .then_inc(S("vb_ready"), 1)
            add(4, G_TA, G_TB, "p8_done", "t8_ready")
            if core:
                dve.wait_ge(S("ktr_done"), c + 1)
                dve.tensor_tensor(c4(slot(G_KBG)), c4(bank[:, 6, :]), over_t(hcur[:, K_BEXPG, :]), ALU.mult)
                dve.tensor_tensor(c4(slot(G_KD)), c4(bank[:, 6, :]), over_t(hcur[:, K_KDEC, :]), ALU.mult)\
                   .then_inc(S("kd_ready"), 1)
            keep(6, G_N2T, "w1_done", "w1_ready")
            if fin:
                dve.wait_ge(S("o_rn"), o + 1)
                dve.tensor_tensor(c4(xn[:, 1, :]), c4(xn[:, 0, :]), over_t(st[:, 80:84]), ALU.mult)\
                   .then_inc(S("on_ready"), 1)
            add(7, G_TB, G_TA, "ta_done", "ta_ready")
            if core:
                dve.wait_ge(S("tt_ready"), c + 1)
            add(4, G_N2, G_N4, "tta_done", "tta_ready")
            if fin:
                dve.wait_ge(S("otr_done"), o + 1)
                dve.wait_ge(S("z_silu"), o + 1)
                dve.scalar_tensor_tensor(arena[:, bass.ds(o * T, T)], bank[:, 6, :], cst[:, C_ONORM:C_ONORM + 1],
                                         slot(G_Z), ALU.mult, ALU.mult).then_inc(S("y_ready"), 1)
            if proj:
                if core:
                    dve.wait_ge(S("v_conv"), 4 * hp)
                    dve.wait_ge(S("expg_ready"), hp)
                dve.tensor_copy(cwh[:, :, :].rearrange("p a b -> p (a b)"), cst[:, bass.ds(C_CONV + 12 * hp, 12)])\
                   .then_inc(S("gcur_ready"), 1)
                dve.tensor_copy(gcur[:, :, :], hc[:, 0:2, :, bass.ds(hp, 1)].rearrange("p a b c -> p a (b c)"))\
                   .then_inc(S("gcur_ready"), 1)
                dve.wait_ge(S("gcur_ready"), 2 * hp + 2)
                dve.wait_ge(S("qk_pre"), 2 * hp + 1)
                if core:
                    dve.wait_ge(S("k_ready"), hp)
            conv(0, G_QS, "qk_conv", 8 * hp if proj else 0)
            add(6, G_TA, G_TB, "tb_done", "tb_ready")
            add(7, G_N4, G_N2, "ttb_done", "ttb_ready")
            if proj:
                dve.wait_ge(S("qk_pre"), 2 * hp + 2)
            conv(1, G_KS, "qk_conv", 8 * hp + 4 if proj else 0)
            add(5, G_N2, G_N4, "ttc_done", "ttc_ready")
            steps = Steps(dve, "qk_step", RSQRT * hp if proj else 0)
            norms = rsqrt(dve, steps, st[:, 20:28], st[:, 68:76], st[:, 44:52], "qk_rn")

            def norm_steps(count):
                if proj:
                    for _ in range(count):
                        next(norms)

            for n in range(TT):
                cs = slice(n * P, (n + 1) * P)
                if core:
                    dve.wait_ge(S("u_done"), 4 * c + n + 1)
                    dve.tensor_copy(slot(G_N0T)[:, cs], bank[:, 7, cs]).then_inc(S("u_ready"), 1)
                if proj and n == 0:
                    dve.wait_ge(S("qk_ss"), hp + 1)
                    if core:
                        dve.wait_ge(S("k_bc"), hp)
                    steps.link(dve.tensor_scalar(st[:, 20:28], bank[:, 0, 0:8], EPS, None, ALU.add))
                    norm_steps(3)
                elif n == 1:
                    norm_steps(4)
                if core and n < TT - 1:
                    dve.wait_ge(S("s_done"), 3 * c + n + 1)
                    if n == 0:
                        ins = dve.tensor_copy(state, bank[:, 4, 0:P])
                    else:
                        dve.wait_ge(S("s_ready"), 3 * c + n)
                        ins = dve.scalar_tensor_tensor(state, state, hcur[:, K_LAST, n:n + 1], bank[:, 4, 0:P],
                                                       ALU.mult, ALU.add)
                    ins.then_inc(S("s_ready"), 1)
                if n == 0:
                    norm_steps(3)
            if proj:
                dve.wait_ge(S("q_bc"), hp + 1)
                if core:
                    dve.wait_ge(S("qd_ready"), hp)
                dve.scalar_tensor_tensor(slot(G_Q), slot(G_QS), float(P) ** -0.5, bank[:, 1, :], ALU.mult, ALU.mult)
                dve.wait_ge(S("k_bc"), hp + 1)
                dve.tensor_tensor(slot(G_K), slot(G_KS), bank[:, 0, :], ALU.mult).then_inc(S("k_ready"), 1)
                dve.wait_ge(S("v_pre"), hp + 1)
            conv(2, G_V, "v_conv", 4 * hp if proj else 0)

        def gdn_pool(pool, hp, c, o):
            U = BASE["gdn_in"]
            if c is not None:
                pool.wait_ge(S("decay_ready"), c + 1)
                pool.wait_ge(S("mb_ready"), c + 1)
                pool.tensor_tensor(slot(G_DL), slot(G_DL), slot(G_D), ALU.mult).then_inc(S("dl_ready"), 1)
                pool.tensor_tensor(c4(slot(G_DU)), c4(slot(G_D)), over_c(upper), ALU.mult).then_inc(S("du_ready"), 1)
                pool.wait_ge(S("n0_ready"), c + 1)
                pool.tensor_tensor(c4(slot(G_TA)), c4(slot(G_N0)), over_c(ident), ALU.add).then_inc(S("t1_ready"), 1)
                pool.wait_ge(S("nat_ready"), c + 1)
                pool.tensor_tensor(c4(slot(G_B1)), c4(slot(G_NAT)), over_c(gm_b1), ALU.mult).then_inc(S("b_ready"), 1)
                supply_lo(pool, U + 2 * c + 3, (U + 1) % 2)
                pool.tensor_tensor(c4(slot(G_B2)), c4(slot(G_NAT)), over_c(gm_b2), ALU.mult).then_inc(S("b_ready"), 1)
                pool.tensor_tensor(c4(slot(G_B3)), c4(slot(G_NAT)), over_c(gm_b3), ALU.mult).then_inc(S("b_ready"), 1)
                if o is not None:
                    pool.wait_ge(S("o_done"), c)
                pool.tensor_tensor(slot(G_QD), slot(G_Q), slot(G_EG), ALU.mult).then_inc(S("qd_ready"), 1)
            if hp is not None:
                if c is not None:
                    pool.wait_ge(S("na_ready"), hp)
                else:
                    pool.wait_ge(S("pre_dve"), PRE_G)
                    pool.wait_ge(S("w_lo"), U + 2)
                pool.tensor_tensor(c4(slot(G_DL)), over_c(gm_lower), hc[:, K_NBETA, :, bass.ds(hp, 1)].to_broadcast([P, TT, P]),
                                   ALU.mult).then_inc(S("mb_ready"), 1)
                supply_lo(pool, U + 2 * hp + 2, U % 2)

        def gdn(eng, one):
            one(eng, 0, None, None)
            one(eng, 1, 0, None)
            one(eng, 2, 1, 0)
            with eng.Fori(3, H) as i:
                one(eng, i, i - 1, i - 2)
            one(eng, None, H - 1, H - 2)

        def gdn_end(eng, one):
            one(eng, None, None, H - 1)

        X_COS, X_SIN, X_ANG, X_TURNS, X_POS, X_RAW, X_ROT = 0, 1, 2, 3, 4, 5, 2
        X_Q, X_QZ, X_P, X_PT = 8, 16, 18, 22
        TWO_PI = (6.28125, 2029.0 / 2 ** 20, 2 * math.pi - 6.28125 - 2029.0 / 2 ** 20)
        ROUND = 1.5 * 2 ** 23
        TRIG = 15

        def trig_dve(dve, n):
            steps = Steps(dve, "angle_step", TRIG * n)
            dve.wait_ge(S("pos_landed"), 16 * (n + 1))
            if past(2 * n):
                dve.wait_ge(S("trig_ready"), 2 * n)
            steps.link(dve.tensor_copy(slot(X_ANG), slot(X_POS).bitcast(I32)))
            steps.link(dve.tensor_scalar(slot(X_ANG), slot(X_ANG), cst[:, C_FREQ:C_FREQ + 1], None, ALU.mult))
            for dst, turn, shift in ((X_SIN, 0.0, 0.0), (X_COS, 0.25, math.pi / 2)):
                turns = slot(X_TURNS)
                steps.link(dve.tensor_scalar(turns, slot(X_ANG), 1.0 / (2 * math.pi), turn, ALU.mult, ALU.add))
                steps.link(dve.tensor_scalar(turns, turns, ROUND, None, ALU.add))
                steps.link(dve.tensor_scalar(turns, turns, ROUND, None, ALU.subtract))
                src = slot(X_ANG)
                for m in TWO_PI:
                    steps.link(dve.scalar_tensor_tensor(slot(dst), turns, -m, src, ALU.mult, ALU.add))
                    src = slot(dst)
                if shift:
                    steps.link(dve.tensor_scalar(slot(dst), slot(dst), shift, None, ALU.add))
                dve.tensor_scalar(slot(dst), slot(dst), math.pi, -math.pi, ALU.min, ALU.max)\
                   .then_inc(S("trig_arg"), 1)
            assert steps.n == TRIG

        def trig_act(act, n):
            for k, dst in enumerate((X_SIN, X_COS)):
                act.wait_ge(S("trig_arg"), 2 * n + k + 1)
                act.activation(slot(dst), slot(dst), ACT.Sin).then_inc(S("trig_ready"), 1)

        def rope_project_pe(pe, U, i, b, n):
            pe.wait_ge(S("w_lo"), U + i + 1)
            if past(n + i - 1):
                pe.wait_ge(S("rope_raw"), n + i - 1)
            two = 2 * (i % 2)
            project_unit(pe, (U + i) % 2, (two, two + 1), b if i == 0 else None).then_inc(S("unit_used"), 1)

        def rope_rot_pe(pe, i, n):
            two = 4 + 2 * (i % 2)
            pe.wait_ge(S("rope_raw"), n + i + 1)
            if past(n + i - 1):
                pe.wait_ge(S("rope_ready"), n + i - 1)
            pe.matmul(bank[:, two, :], rope_rot, slot(X_RAW), start=True, stop=True)
            pe.matmul(bank[:, two + 1, :], rope_rot, slot(X_RAW + 1), start=True, stop=True).then_inc(S("rot_done"), 1)

        def rope_raw_act(act, U, i, n, scale):
            act.wait_ge(S("unit_used"), U + i + 1)
            if past(n + i):
                act.wait_ge(S("rope_ready"), n + i)
            two = 2 * (i % 2)
            act.activation(slot(X_RAW, 2).rearrange("p (a t) -> p a t", a=2), bank[:, two:two + 2, :], ACT.Copy,
                           scale=scale).then_inc(S("rope_raw"), 1)

        def rope_dve(dve, i, n, dst):
            two = 4 + 2 * (i % 2)

            def pair(ap):
                return ap.rearrange("p (a t) -> p a t", a=2)

            def both(k):
                return slot(k).unsqueeze(1).to_broadcast([P, 2, T])

            dve.wait_ge(S("rot_done"), n + i + 1)
            dve.wait_ge(S("trig_ready"), 2 * (n // 4) + 2)
            steps = Steps(dve, "rope_step", 2 * (n + i))
            if past(n + i):
                dve.wait_ge(S("rope_ready"), n + i)
            steps.link(dve.tensor_tensor(pair(slot(X_ROT, 2)), bank[:, two:two + 2, :], both(X_SIN), ALU.mult))
            steps.link(dve.tensor_tensor(pair(dst), pair(slot(X_RAW, 2)), both(X_COS), ALU.mult))
            dve.tensor_tensor(dst, dst, slot(X_ROT, 2), ALU.add).then_inc(S("rope_ready"), 1)

        def v_unit_pe(pe, U, v):
            pe.wait_ge(S("w_lo"), U + v + 1)
            for kt in range(4):
                for t in range(TT):
                    k = 4 * (v % 2) + kt
                    ins = mm3(pe, bank[:, 4 * (v // 2) + t, :], xh[:, k, t * P:(t + 1) * P], xl[:, k, t * P:(t + 1) * P],
                              *w_block((U + v) % 2, kt * 512, 512), k == 0, k == KD - 1)
            ins.then_inc(S("unit_used"), 1)

        values = arena[:, A_V:A_V + KD * T].rearrange("p (t c) -> p t c", t=TT)

        def v_keep_act(act, U, half):
            act.wait_ge(S("unit_used"), U + 2 * half + 2)
            act.activation(values[:, :, half * 512:(half + 1) * 512], bank[:, 4 * half:4 * half + 4, :], ACT.Copy)\
               .then_inc(S("v_kept"), 1)

        def kv_pe(pe):
            U = BASE["kv"]
            for i in range(4):
                rope_project_pe(pe, U, i, 3, 0)
                if i:
                    rope_rot_pe(pe, i - 1, 0)
            pe.wait_ge(S("rope_raw"), 4)
            v_unit_pe(pe, U + 4, 0)
            rope_rot_pe(pe, 3, 0)
            v_unit_pe(pe, U + 4, 1)
            pe.wait_ge(S("rope_ready"), 4)
            v_unit_pe(pe, U + 4, 2)
            v_unit_pe(pe, U + 4, 3)

        def kv_act(act):
            U = BASE["kv"]
            trig_act(act, 0)
            for i in range(4):
                supply_hi(act, U + i + 2, (U + i) % 2)
                rope_raw_act(act, U, i, 0, 1.0)
            for v in range(4):
                if v < 3:
                    supply_hi(act, U + v + 6, (U + v) % 2)
                if v % 2:
                    v_keep_act(act, U + 4, v // 2)

        def keys(i):
            return arena[:, A_KT + 2 * i * T:A_KT + 2 * (i + 1) * T]

        def kv_dve(dve):
            U = BASE["kv"]
            trig_dve(dve, 0)
            for i in range(4):
                supply_lo(dve, U + i + 2, (U + i) % 2)
                if i:
                    rope_dve(dve, i - 1, 0, keys(i - 1))
            supply_lo(dve, U + 6, U % 2)
            rope_dve(dve, 3, 0, keys(3))
            supply_lo(dve, U + 7, (U + 1) % 2)
            supply_lo(dve, U + 8, U % 2)

        def q_pe(pe):
            U = BASE["q"]
            for i in range(4):
                rope_project_pe(pe, U, i, 5, 4)
                if i:
                    rope_rot_pe(pe, i - 1, 4)
            rope_rot_pe(pe, 3, 4)

        def q_act(act):
            U = BASE["q"]
            trig_act(act, 1)
            for i in range(4):
                if i < 3:
                    supply_hi(act, U + i + 2, (U + i) % 2)
                rope_raw_act(act, U, i, 4, 64 ** -0.5)
            supply_hi(act, U + 5, (U + 3) % 2)

        def q_dve(dve):
            U = BASE["q"]
            trig_dve(dve, 1)
            for i in range(4):
                if i < 3:
                    supply_lo(dve, U + i + 2, (U + i) % 2)
                if i:
                    rope_dve(dve, i - 1, 4, slot(X_Q + 2 * i - 2, 2))
            rope_dve(dve, 3, 4, slot(X_Q + 6, 2))
            supply_lo(dve, U + 5, (U + 3) % 2)

        def attn_pe(pe, hd, g, o, nxt):
            def scores(i):
                n = 4 * hd + i
                if i == 0:
                    pe.wait_ge(S("qz_ready"), 2 * hd + 2)
                if past(n - 1):
                    pe.wait_ge(S("p_ready"), n - 1)
                for m in range(2):
                    ins = pe.matmul(bank[:, 2 * (i % 2) + m, 0:(i + 1) * P], slot(X_QZ + m)[:, i * P:(i + 1) * P],
                                    arena[:, bass.ds(A_KT + hd * T, (i + 1) * P)], start=True, stop=True)
                ins.then_inc(S("sc_done"), 1)

            def turn(e, i):
                n = 4 * e + i
                pe.wait_ge(S("pc_ready"), n + 1)
                if past(n - 1):
                    pe.wait_ge(S("pt_ready"), n - 1)
                for j in range(i + 1):
                    ins = pe.transpose(bank[:, 4 + i % 2, j * P:(j + 1) * P], slot(X_P + 2 * (i % 2))[:, j * P:(j + 1) * P],
                                       ident)
                ins.then_inc(S("ptr_done"), 1)

            def weigh(e, i):
                n = 4 * e + i
                pe.wait_ge(S("pt_ready"), n + 1)
                if past(n):
                    pe.wait_ge(S("ob_ready"), n)
                for j in range(i + 1):
                    ins = pe.matmul(bank[:, 6, i * P:(i + 1) * P], slot(X_PT + i % 2)[:, j * P:(j + 1) * P],
                                    arena[:, bass.ds(A_V + j * D + e * P, P)], start=j == 0, stop=j == i)
                ins.then_inc(S("pv_done"), 1)

            for i in range(4):
                if hd is not None:
                    scores(i)
                if i < 2:
                    if g is not None:
                        turn(g, i + 2)
                elif hd is not None:
                    turn(hd, i - 2)
                if i == 3 and o is not None:
                    pe.wait_ge(S("aon_ready"), o + 1)
                    if past(o):
                        pe.wait_ge(S("ay_ready"), o)
                    turned(pe, 7, xn[:, 1, :]).then_inc(S("aotr_done"), 1)
                if i < 3:
                    if g is not None:
                        weigh(g, i + 1)
                elif hd is not None:
                    weigh(hd, 0)

        def attn_act(act, hd, g, o, nxt):
            def soft(i):
                n = 4 * hd + i
                act.wait_ge(S("mx_ready"), n + 1)
                if past(n - 1):
                    act.wait_ge(S("ptr_done"), n - 1)
                for m in range(2):
                    ins = act.activation(slot(X_P + 2 * (i % 2) + m)[:, 0:(i + 1) * P],
                                         bank[:, 2 * (i % 2) + m, 0:(i + 1) * P], ACT.Exp,
                                         bias=negmax[:, 2 * (i % 2) + m:2 * (i % 2) + m + 1],
                                         accum_out=rowsum[:, 2 * (i % 2) + m:2 * (i % 2) + m + 1])
                ins.then_inc(S("p_ready"), 1)

            def keep(e, i):
                n = 4 * e + i
                act.wait_ge(S("ptr_done"), n + 1)
                if past(n - 1):
                    act.wait_ge(S("pv_done"), n - 1)
                act.activation(slot(X_PT + i % 2)[:, 0:(i + 1) * P], bank[:, 4 + i % 2, 0:(i + 1) * P], ACT.Copy)\
                   .then_inc(S("pt_ready"), 1)

            def out_block(e, i):
                act.wait_ge(S("pv_done"), 4 * e + i + 1)
                act.activation(arena[:, bass.ds(e * T + i * P, P)], bank[:, 6, i * P:(i + 1) * P], ACT.Copy,
                               scale=rr[:, 2 * i:2 * i + 1]).then_inc(S("ob_ready"), 1)

            for i in range(4):
                if hd is not None:
                    soft(i)
                if i < 2:
                    if g is not None:
                        keep(g, i + 2)
                elif hd is not None:
                    keep(hd, i - 2)
                if i < 3:
                    if g is not None:
                        out_block(g, i + 1)
                elif hd is not None:
                    out_block(hd, 0)

        negmax, rowsum = st[:, 0:4], st[:, 4:8]
        rr = st[:, 84:92]
        mixer = st[:, 92:96]

        def queries(dve, hd):
            for m in range(2):
                rows = slice(64 * m, 64 * m + 64)
                dve.tensor_copy(slot(X_QZ + m)[rows, :], arena[rows, bass.ds((X_Q + hd) * T, T)])\
                   .then_inc(S("qz_ready"), 1)

        def attn_dve(dve, hd, g, o, nxt):
            def top(i):
                n = 4 * hd + i
                two = 2 * (i % 2)
                dve.wait_ge(S("sc_done"), n + 1)
                diag = bank[:, two:two + 2, i * P:(i + 1) * P]
                dve.tensor_tensor(diag, diag, causal.unsqueeze(1).to_broadcast([P, 2, P]), ALU.add)\
                   .then_inc(S("masked"), 1)
                dve.wait_ge(S("masked"), n + 1)
                if past(n - 1):
                    dve.wait_ge(S("p_ready"), n - 1)
                dve.tensor_reduce(negmax[:, two:two + 2], bank[:, two:two + 2, 0:(i + 1) * P], AX.X, ALU.max,
                                  negate=True).then_inc(S("mx_ready"), 1)

            def mix(e, i):
                n = 4 * e + i
                two = 2 * (i % 2)
                p0, p1 = (slot(X_P + two + m)[:, 0:(i + 1) * P] for m in range(2))
                dve.wait_ge(S("p_ready"), n + 1)
                if past(n - 3):
                    dve.wait_ge(S("ob_ready"), n - 3)
                steps = Steps(dve, "p_step", 2 * n)
                steps.link(dve.reciprocal(rr[:, 2 * i:2 * i + 2], rowsum[:, two:two + 2]))
                steps.link(dve.scalar_tensor_tensor(mixer[:, i:i + 1], rr[:, 2 * i + 1:2 * i + 2], neglam[:, 0:1],
                                                    rowsum[:, two:two + 1], ALU.mult, ALU.mult))
                dve.scalar_tensor_tensor(p0, p1, mixer[:, i:i + 1], p0, ALU.mult, ALU.add)\
                   .then_inc(S("pc_ready"), 1)

            steps = Steps(dve, "ao_step", (RSQRT + 2) * o if o is not None else 0)
            norm = rsqrt(dve, steps, st[:, 56:60], st[:, 76:80], st[:, 80:84], "ao_rn")

            def norm_steps(count):
                if o is not None:
                    for _ in range(count):
                        next(norm)

            for i in range(4):
                if hd is not None:
                    top(i)
                if i == 0 and o is not None:
                    raw_out = arena[:, bass.ds(o * T, T)]
                    dve.wait_ge(S("ob_ready"), 4 * o + 4)
                    steps.link(dve.tensor_tensor(sq[:, 0, :], raw_out, raw_out, ALU.mult))
                if i == 3 and nxt is not None:
                    dve.wait_ge(S("sc_done"), 4 * nxt)
                    queries(dve, nxt)
                if i == 0:
                    if g is not None:
                        mix(g, 3)
                elif hd is not None:
                    mix(hd, i - 1)
                if i == 0 and o is not None:
                    steps.link(dve.tensor_reduce(st[:, 52:56], c4(sq[:, 0, :]), AX.X, ALU.add))
                    steps.link(dve.tensor_scalar(st[:, 56:60], st[:, 52:56], 1.0 / P, EPS, ALU.mult, ALU.add))
                if i == 1:
                    norm_steps(5)
                if i == 2 and o is not None:
                    norm_steps(5)
                    dve.wait_ge(S("ao_rn"), o + 1)
                    if past(o):
                        dve.wait_ge(S("aotr_done"), o)
                    dve.tensor_tensor(c4(xn[:, 1, :]), c4(raw_out), over_t(st[:, 80:84]), ALU.mult)\
                       .then_inc(S("aon_ready"), 1)
            if o is not None:
                dve.wait_ge(S("aotr_done"), o + 1)
                dve.tensor_scalar(arena[:, bass.ds(o * T, T)], bank[:, 7, :], neglam[:, 1:2], None, ALU.mult)\
                   .then_inc(S("ay_ready"), 1)

        def lambda_dve(dve):
            dve.wait_ge(S("early_landed"), 16)
            steps = Steps(dve, "lam_step")
            lp = arena[:, A_EARLY:A_EARLY + 256].rearrange("p (a b c) -> p a b c", a=2, b=2)
            pr = arena[:, A_EARLY + 512:A_EARLY + 640].rearrange("p (a c) -> p a c", a=2)
            steps.link(dve.tensor_tensor(pr, lp[:, :, 0, :], lp[:, :, 1, :], ALU.mult))
            dve.tensor_reduce(neglam[:, 2:4], pr, AX.X, ALU.add).then_inc(S("lam_sum"), 1)
            dve.wait_ge(S("lam_exp"), 1)
            dve.scalar_tensor_tensor(neglam[:, 0:1], neglam[:, 3:4], -LAM_INIT, neglam[:, 2:3], ALU.add, ALU.subtract)\
               .then_inc(S("lam_ready"), 1)
            dve.tensor_scalar(neglam[:, 1:2], cst[:, C_SUBLN:C_SUBLN + 1], 1.0 - LAM_INIT, None, ALU.mult)\
               .then_inc(S("lam_ready"), 1)

        AU = {"ffn0": 0, "gdn": FJ, "ffn1": FJ + U_OUT, "ffn2": 2 * FJ + U_OUT, "attn": 3 * FJ + U_OUT,
              "ffn3": 3 * FJ + 2 * U_OUT}

        @block.sync
        def _(sp):
            sp.dma_start(h[:, :, :], xT_in).then_inc(S("x_landed"), 16)
            sp.dma_start(cst[:, :], cst_in).then_inc(S("cst_landed"), 16)
            sp.dma_start(arena[:, A_EARLY:A_EARLY + 384], early_in).then_inc(S("early_landed"), 16)
            for n in range(2):
                sp.dma_start(raw[n][:, :], weights[n, :, :]).then_inc(S(f"raw_landed{n}"), 16)
            sp.dma_start(arena[:, A_GMASK:A_GMASK + 5 * P], masks_in).then_inc(S("masks_landed"), 16)
            with sp.Fori(1, N_UNITS // 2) as i:
                for n in range(2):
                    sp.wait_ge(S("w_lo"), 2 * i + n - 1)
                    sp.dma_start(raw[n][:, :], weights[bass.ds(2 * i + n, 1), :, :].rearrange("a p c -> (a p) c"))\
                      .then_inc(S(f"raw_landed{n}"), 16)
            for k in range(KD):
                sp.wait_ge(S("out_ready"), k + 1)
                sp.dma_start(out[k, :, :], slot(k)).then_inc(S("out_landed"), 16)
            sp.wait_ge(S("out_landed"), 16 * KD)

        def attention(eng, one):
            one(eng, 0, None, None, 1)
            one(eng, 1, 0, None, 2)
            one(eng, 2, 1, 0, 3)
            with eng.Fori(3, H - 1) as i:
                one(eng, i, i - 1, i - 2, i + 1)
            one(eng, H - 1, H - 2, H - 3, None)
            one(eng, None, H - 1, H - 2, None)

        def attention_end(eng, one):
            one(eng, None, None, H - 1, None)

        @block.tensor
        def _(pe):
            def ffn(f, b, t):
                U = BASE[f"ffn{f}"]
                ffn_pe(pe, f, b, U)
                down_pe(pe, t, FJ, U + 2 * FJ, AU[f"ffn{f}"], ffn_free(f))
                norm_pe(pe, t + 1)

            pe.wait_ge(S("cst_landed"), 16)
            norm_pe(pe, 0)
            ffn(0, 0, 0)
            gdn_pre_pe(pe)
            gdn_cum_pe(pe)
            gdn(pe, gdn_pe)
            gdn_end(pe, gdn_pe)
            down_pe(pe, 1, U_OUT, BASE["gdn_out"], AU["gdn"], {1: ("oc_ready", H), 2: ("y_ready", H)})
            norm_pe(pe, 2)
            ffn(1, 2, 2)
            kv_pe(pe)
            pe.wait_ge(S("v_kept"), 2)
            ffn(2, 4, 3)
            q_pe(pe)
            pe.wait_ge(S("rope_ready"), 8)
            attention(pe, attn_pe)
            attention_end(pe, attn_pe)
            down_pe(pe, 4, U_OUT, BASE["attn_out"], AU["attn"], {2: ("ob_ready", 4 * H), 3: ("ay_ready", H)})
            norm_pe(pe, 5)
            ffn(3, 6, 5)

        @block.scalar
        def _(act):
            def ffn(f, t):
                U = BASE[f"ffn{f}"]
                ffn_act(act, f, U)
                split_a_hi(act, 0, 0, 0)
                split_a_hi(act, 1, 1, 0)
                supply_hi(act, U + 2 * FJ + 1, (U + 1) % 2)
                down_act(act, t, FJ, U + 2 * FJ, AU[f"ffn{f}"])
                norm_act(act, t + 1)

            def enter(b, U):
                build_act(act, b, U)
                supply_hi(act, U + 1, (U + 1) % 2)

            def positions():
                act.dma_start(slot(X_POS).bitcast(I32), pos_in).then_inc(S("pos_landed"), 16)

            act.wait_ge(S("cst_landed"), 16)
            act.wait_ge(S("early_landed"), 16)
            act.activation(bahi[:, :, :].rearrange("p a b -> p (a b)"), arena[:, A_EARLY + 256:A_EARLY + 384], ACT.Copy)\
               .then_inc(S("ba_split"), 1)
            act.wait_ge(S("lam_sum"), 1)
            act.activation(neglam[:, 2:4], neglam[:, 2:4], ACT.Exp).then_inc(S("lam_exp"), 1)
            norm_act(act, 0)
            supply_hi(act, 0, 0)
            enter(0, 0)
            ffn(0, 0)
            enter(1, BASE["gdn_in"])
            gdn_pre_act(act)
            gdn(act, gdn_act)
            act.wait_ge(S("y_ready"), 4)
            split_a_hi(act, 0, 0, 0)
            split_a_hi(act, 1, 1, 0)
            act.wait_ge(S("y_ready"), H)
            down_act(act, 1, U_OUT, BASE["gdn_out"], AU["gdn"])
            norm_act(act, 2)
            enter(2, BASE["ffn1"])
            ffn(1, 2)
            positions()
            enter(3, BASE["kv"])
            kv_act(act)
            enter(4, BASE["ffn2"])
            ffn(2, 3)
            positions()
            enter(5, BASE["q"])
            q_act(act)
            attention(act, attn_act)
            act.wait_ge(S("ay_ready"), 4)
            split_a_hi(act, 0, 0, 0)
            split_a_hi(act, 1, 1, 0)
            act.wait_ge(S("ay_ready"), H)
            down_act(act, 4, U_OUT, BASE["attn_out"], AU["attn"])
            norm_act(act, 5)
            enter(6, BASE["ffn3"])
            ffn(3, 5)

        @block.gpsimd
        def _(pool):
            norm_pool(pool, 0)
            norm_pool(pool, 1)
            pool.wait_ge(S("masks_landed"), 16)
            gdn(pool, gdn_pool)
            gdn_end(pool, gdn_pool)
            for r in range(2, 7):
                norm_pool(pool, r)

        @block.vector
        def _(dve):
            def ffn(f, t):
                U = BASE[f"ffn{f}"]
                ffn_dve(dve, f, U, AU[f"ffn{f}"])
                down_dve(dve, t, FJ, U + 2 * FJ, AU[f"ffn{f}"], 0.5)
                norm_dve(dve, t + 1)

            def enter(r, b, U):
                build_dve(dve, r, b, b)
                if b == 3:
                    dve.tensor_copy(acc[:, :], bank[:, 5, :]).then_inc(S("rbc_kept"), 1)
                supply_lo(dve, U + 1, (U + 1) % 2)

            dve.wait_ge(S("cst_landed"), 16)
            dve.wait_ge(S("ba_split"), 1)
            dve.tensor_tensor(balo[:, :, :].rearrange("p a b -> p (a b)"), arena[:, A_EARLY + 256:A_EARLY + 384],
                              bahi[:, :, :].rearrange("p a b -> p (a b)").bitcast(F32), ALU.subtract)\
               .then_inc(S("ba_split"), 1)
            lambda_dve(dve)
            norm_dve(dve, 0)
            supply_lo(dve, 0, 0)
            enter(0, 0, 0)
            ffn(0, 0)
            enter(1, 1, BASE["gdn_in"])
            dve.wait_ge(S("masks_landed"), 16)
            gdn_pre_dve(dve)
            gdn(dve, gdn_dve)
            split_a_lo(dve, 0, 0, AU["gdn"])
            split_a_lo(dve, 1, 1, AU["gdn"])
            gdn_end(dve, gdn_dve)
            dve.wait_ge(S("w_lo"), BASE["gdn_out"] + 2)
            down_dve(dve, 1, U_OUT, BASE["gdn_out"], AU["gdn"], 1.0)
            norm_dve(dve, 2)
            enter(2, 2, BASE["ffn1"])
            ffn(1, 2)
            enter(3, 3, BASE["kv"])
            kv_dve(dve)
            enter(3, 4, BASE["ffn2"])
            ffn(2, 3)
            enter(4, 5, BASE["q"])
            q_dve(dve)
            dve.wait_ge(S("lam_ready"), 2)
            dve.memset(slot(X_QZ, 2), 0.0).then_inc(S("qz_zero"), 1)
            dve.wait_ge(S("qz_zero"), 1)
            queries(dve, 0)
            attention(dve, attn_dve)
            split_a_lo(dve, 0, 0, AU["attn"])
            split_a_lo(dve, 1, 1, AU["attn"])
            attention_end(dve, attn_dve)
            down_dve(dve, 4, U_OUT, BASE["attn_out"], AU["attn"], 1.0)
            norm_dve(dve, 5)
            enter(5, 6, BASE["ffn3"])
            ffn(3, 5)
            dve.wait_ge(S("rbc_done"), 7)
            for k in range(KD):
                dve.scalar_tensor_tensor(slot(k), h[:, k, :], cst[:, C_GAIN + 7 * KD + k:C_GAIN + 7 * KD + k + 1],
                                         bank[:, 5, :], ALU.mult, ALU.mult).then_inc(S("out_ready"), 1)




def _constants():
    import numpy as np
    p = np.arange(P)
    ident = np.eye(P)
    upper = p[:, None] <= p[None, :]
    lower = p[:, None] > p[None, :]
    diag = p[:, None] // 16 == p[None, :] // 16
    levels = []
    for w in (16, 32, 64):
        levels.append((p[:, None] // (2 * w) == p[None, :] // (2 * w)) & (p[:, None] % (2 * w) < w)
                      & (p[None, :] % (2 * w) >= w))
    half = ROPE_DIM // 2
    rot = np.zeros((P, P))
    freq = np.zeros(P, np.float32)
    inv = (np.float32(1.0) / (np.float32(ROPE_THETA) ** (np.arange(half, dtype=np.float32) / np.float32(half))))
    for m in range(P):
        f = m % 64
        if f < half:
            rot[m + half, m] = -1.0
        elif f < ROPE_DIM:
            rot[m - half, m] = 1.0
        if f < ROPE_DIM:
            freq[m] = inv[f % half]
    causal = np.where(p[None, :] <= p[:, None], 0.0, -3.0e38)
    cst = np.concatenate([ident, np.ones((P, P)), upper, rot, causal], 1).astype(np.float32)
    masks = np.concatenate([lower, diag, *levels], 1).astype(np.float32)
    return cst, masks, freq


def kernel(**inputs):
    import numpy as np
    import concourse.bacc as bacc
    from concourse.bass_utils import run_bass_kernel_spmd

    a = {k: np.asarray(v) for k, v in inputs.items()}

    def cols(w):
        return w.reshape(KD, P, -1, 256).transpose(2, 1, 0, 3).reshape(-1, P, UNIT)

    def rows(w):
        return w.reshape(-1, 2, P, D).transpose(0, 2, 1, 3).reshape(-1, P, UNIT)

    def ffn(gu, dn):
        both = np.stack([cols(gu[:, :FF]), cols(gu[:, FF:])], 1).reshape(-1, P, UNIT)
        return [both, rows(dn)]

    w_in = a["gdn_w_in"][0]
    q, k, v, z = (w_in[:, n * D:(n + 1) * D].reshape(D, H, P) for n in range(4))
    per_head = np.stack([q, k, v, z], 2).reshape(D, H * 4 * P)
    kv = a["kv_w"]
    v_units = kv[:, D:].reshape(2, 4, P, 2, 512).transpose(3, 0, 2, 1, 4).reshape(4, P, UNIT)
    f1u, f1d, f2u, f2d = (a[n] for n in ("ffn1_w_gate_up", "ffn1_w_down", "ffn2_w_gate_up", "ffn2_w_down"))
    units = [*ffn(f1u[0], f1d[0]), cols(per_head), rows(a["gdn_w_out"][0]), *ffn(f2u[0], f2d[0]),
             cols(kv[:, :D]), v_units, *ffn(f1u[1], f1d[1]), cols(a["diff_w_q"][0]), rows(a["diff_w_out"][0]),
             *ffn(f2u[1], f2d[1])]
    weights = np.concatenate(units, 0)
    assert weights.shape[0] == N_UNITS

    cst, masks, freq = _constants()
    gains = np.stack([a["ffn1_norm"][0], a["mix_norm"][0], a["ffn2_norm"][0], a["kv_norm"], a["ffn1_norm"][1],
                      a["mix_norm"][1], a["ffn2_norm"][1], a["final_norm"]])
    gains = gains.reshape(8, KD, P).transpose(2, 0, 1).reshape(P, 8 * KD)
    conv = a["gdn_conv"][0].reshape(4, 3, H, P).transpose(3, 2, 1, 0).reshape(P, H * 12)

    def on_all(v):
        return np.broadcast_to(v.reshape(1, -1), (P, v.size))

    cst = np.concatenate([cst, gains, conv, on_all(a["gdn_a_log"]), on_all(a["gdn_dt_bias"]),
                          a["gdn_out_norm"].reshape(P, 1), a["diff_subln"].reshape(P, 1), freq.reshape(P, 1)], 1)
    w_ba = w_in[:, 4 * D:].reshape(KD, P, 16).transpose(1, 0, 2).reshape(P, KD * 16)
    early = np.concatenate([on_all(a["diff_lambda"]), w_ba], 1)
    xT = a["x"][0].T.reshape(KD, P, T).transpose(1, 0, 2)
    pos = on_all(a["positions"])

    nc = bacc.Bacc("TRN2", target_bir_lowering=False, num_devices=1)
    arrays, aps = {}, []
    for name, arr in (("weights", weights), ("cst_in", cst), ("masks_in", masks), ("early_in", early),
                      ("xT_in", xT), ("pos_in", pos)):
        arr = np.ascontiguousarray(arr)
        arrays[name] = arr
        aps.append(nc.dram_tensor(name, arr.shape, mybir.dt.from_np(arr.dtype), kind="ExternalInput").ap())
    out = nc.dram_tensor("outT", (KD, P, T), F32, kind="ExternalOutput").ap()
    trunk_kernel(nc, *aps, out)
    r = run_bass_kernel_spmd(nc, [arrays], core_ids=[0])
    return np.ascontiguousarray(r.results[0]["outT"].reshape(D, T).T).reshape(1, T, D)
```

```python
import math
from contextlib import ExitStack

import concourse.bass as bass
from concourse import mybir

ALU = mybir.AluOpType
ACT = mybir.ActivationFunctionType
AX = mybir.AxisListType
F32 = mybir.dt.float32
F32R = mybir.dt.float32r
I32 = mybir.dt.int32

P = 128
D = 1024
T = 512
KD = D // P
TT = T // P
FF = 2816
FT = FF // P
FJ = FT // 2
H = 8
EPS = 1e-6
UNIT = 2048
LAM_INIT = 0.8 - 0.6 * math.exp(-0.3 * 1)
ROPE_THETA = 500000.0
ROPE_DIM = 16

U_FFN = 2 * FJ + FJ
U_IN, U_OUT, U_KV, U_Q = 2 * H, D * D // (P * UNIT), 8, 4
BASE = {}
_at = 0
for _name, _n in (("ffn0", U_FFN), ("gdn_in", U_IN), ("gdn_out", U_OUT), ("ffn1", U_FFN), ("kv", U_KV),
                  ("ffn2", U_FFN), ("q", U_Q), ("attn_out", U_OUT), ("ffn3", U_FFN)):
    BASE[_name] = _at
    _at += _n
N_UNITS = _at

C_IDENT, C_ONES, C_UPPER, C_ROPE, C_CAUSAL = (P * n for n in range(5))
C_GAIN = 5 * P
C_CONV = C_GAIN + 8 * KD
C_ALOG = C_CONV + H * 12
C_DTB = C_ALOG + H
C_ONORM = C_DTB + H
C_SUBLN = C_ONORM + 1
C_FREQ = C_SUBLN + 1
N_CST = C_FREQ + 1

A_ACT, A_SILU, A_KT, A_V = 0, FT * T, FT * T + 2 * T, FT * T + 2 * T + KD * T
N_ARENA = A_V + KD * T
A_EARLY = A_KT
A_GMASK = N_ARENA - 5 * P

HEAD_COLS = 7
K_G, K_CUM, K_BETA, K_NBETA, K_BEXPG, K_KDEC, K_LAST = range(HEAD_COLS)


def trunk_kernel(nc, weights, cst_in, masks_in, early_in, xT_in, pos_in, out):
    ctx = ExitStack()
    with ctx:
        def sb(name, shape, dt=F32):
            return ctx.enter_context(nc.sbuf_tensor(name, shape, dt))

        h = sb("h", [P, KD, T])
        xh = sb("xh", [P, KD, T], F32R)
        xl = sb("xl", [P, KD, T], F32R)
        raw = [sb(f"raw{n}", [P, UNIT]) for n in range(2)]
        whi = [sb(f"whi{n}", [P, UNIT], F32R) for n in range(2)]
        wlo = [sb(f"wlo{n}", [P, UNIT], F32R) for n in range(2)]
        ahi = [sb(f"ahi{n}", [P, 2, T], F32R) for n in range(2)]
        alo = [sb(f"alo{n}", [P, 2, T], F32R) for n in range(2)]
        arena = sb("arena", [P, N_ARENA])
        sq = sb("sq", [P, 2, T])
        acc = sb("acc", [P, T])
        xn = sb("xn", [P, 2, T])
        cst = sb("cst", [P, N_CST])
        bahi = sb("bahi", [P, KD, 16], F32R)
        balo = sb("balo", [P, KD, 16], F32R)
        hc = sb("hc", [P, HEAD_COLS, TT, H])
        hcur = sb("hcur", [P, HEAD_COLS, TT])
        cwh = sb("cwh", [P, 3, 4])
        gcur = sb("gcur", [P, 2, TT])
        st = sb("st", [P, 96])
        neglam = sb("neglam", [P, 4])
        bank = ctx.enter_context(nc.psum_tensor("bank", [P, 8, T], F32))

        ident = cst[:, C_IDENT:C_IDENT + P]
        ones = cst[:, C_ONES:C_ONES + P]
        upper = cst[:, C_UPPER:C_UPPER + P]
        rope_rot = cst[:, C_ROPE:C_ROPE + P]
        causal = cst[:, C_CAUSAL:C_CAUSAL + P]

        def slot(n, w=1):
            return arena[:, n * T:(n + w) * T]

        def c4(ap):
            return ap.rearrange("p (c t) -> p c t", c=TT)

        def over_t(cols):
            return cols.unsqueeze(2).to_broadcast([P, TT, P])

        def over_c(mask):
            return mask.unsqueeze(1).to_broadcast([P, TT, P])

        (G_QS, G_KS, G_Q, G_K, G_V, G_Z, G_DL, G_DU, G_D, G_EG, G_QD, G_QK, G_NA, G_N0, G_N0T, G_NAT,
         G_B1, G_B2, G_B3, G_N2, G_N2T, G_N4, G_TA, G_TB, G_KBG, G_KD, G_VB) = range(8, 35)
        PRE0 = 35 * T
        S0 = PRE0 + 3 * (T + 4)
        assert S0 + P <= A_GMASK
        pre3 = arena[:, PRE0:S0].rearrange("p (q t) -> p q t", q=3)
        pre_pad = pre3[:, :, 0:3]
        state = arena[:, S0:S0 + P]
        gm_lower, gm_diag, gm_b1, gm_b2, gm_b3 = (arena[:, A_GMASK + n * P:A_GMASK + (n + 1) * P] for n in range(5))

        sems = {}

        def S(name):
            if name not in sems:
                sems[name] = ctx.enter_context(nc.semaphore(name))
            return sems[name]

        block = ctx.enter_context(nc.Block())

        def past(count):
            return not isinstance(count, int) or count > 0

        def supply_hi(act, n, s):
            act.wait_ge(S(f"raw_landed{s}"), (n - s) * 8 + 16)
            if past(n - 1):
                act.wait_ge(S("unit_used"), n - 1)
            act.activation(whi[s][:, :], raw[s][:, :], ACT.Copy).then_inc(S("w_hi"), 1)

        def supply_lo(dve, n, s):
            dve.wait_ge(S("w_hi"), n + 1)
            dve.tensor_tensor(wlo[s][:, :], raw[s][:, :], whi[s][:, :].bitcast(F32), ALU.subtract)\
               .then_inc(S("w_lo"), 1)

        def mm3(pe, o, ah, al, bh, bl, start, stop):
            pe.matmul(o, ah, bh, start=start, stop=False)
            pe.matmul(o, ah, bl, start=False, stop=False)
            return pe.matmul(o, al, bh, start=False, stop=stop)

        def w_block(s, lo, width=P):
            return whi[s][:, lo:lo + width], wlo[s][:, lo:lo + width]

        def project_unit(pe, s, banks, x_build=None, part=None):
            a, b = part or (0, 2 * KD)
            for n in range(a, b):
                k, f = n // 2, n % 2
                if x_build is not None and f == 0:
                    pe.wait_ge(S("x_lo"), 8 * x_build + k + 1)
                last = mm3(pe, bank[:, banks[f], :], *w_block(s, k * 256 + f * P), xh[:, k, :], xl[:, k, :],
                           k == 0, k == KD - 1)
            return last

        def square(act, r, d):
            if r == 0:
                if d in (0, 2):
                    act.wait_ge(S(f"x_landed{d // 2}"), 16)
            else:
                act.wait_ge(S("h_ready"), 8 * (r - 1) + d + 1)
            if d == 0:
                if past(6 * r):
                    act.wait_ge(S("sq_summed"), 6 * r)
            elif d == 1:
                if past(r):
                    act.wait_ge(S("ss_done"), r)
            else:
                act.wait_ge(S("sq_summed"), 6 * r + max(d - 2, 1))
            act.activation(sq[:, d % 2, :], h[:, d, :], ACT.Square).then_inc(S("sq_ready"), 1)

        def enter_act(act, r, b, U):
            for d in range(KD + 2):
                if d >= 2:
                    k = d - 2
                    if b == 4 and k in (0, 4):
                        act.wait_ge(S("unit_used"), U - 1 + k // 4)
                    act.wait_ge(S("xn_ready"), 8 * b + k + 1)
                    act.activation(xh[:, k, :], xn[:, k % 2, :], ACT.Copy).then_inc(S("x_hi"), 1)
                if d < KD and b != 4:
                    square(act, r, d)
            supply_hi(act, U + 1, (U + 1) % 2)

        def norm_pool(pool, r):
            if past(r):
                pool.wait_ge(S("ss_done"), r)
            for d in range(1, KD - 1):
                pool.wait_ge(S("sq_ready"), 8 * r + d + 1)
                if d == 1:
                    ins = pool.tensor_tensor(acc[:, :], sq[:, 0, :], sq[:, 1, :], ALU.add)
                else:
                    pool.wait_ge(S("sq_summed"), 6 * r + d - 1)
                    ins = pool.tensor_tensor(acc[:, :], acc[:, :], sq[:, d % 2, :], ALU.add)
                ins.then_inc(S("sq_summed"), 1)

        def norm_sums(pe, r):
            pe.wait_ge(S("sq_summed"), 6 * (r + 1))
            pe.wait_ge(S("sq_ready"), 8 * (r + 1))
            if r:
                pe.wait_ge(S("h_ready"), 8 * (r - 1) + 2)
            for t in range(TT):
                pe.matmul(bank[:, 4, t:t + 1], acc[:, t * P:(t + 1) * P], ones[:, 0:1], start=True, stop=False)
                last = pe.matmul(bank[:, 4, t:t + 1], sq[:, 1, t * P:(t + 1) * P], ones[:, 0:1],
                                 start=False, stop=True)
            last.then_inc(S("ss_done"), 1)

        def norm_spread(pe, r):
            pe.wait_ge(S("rstd_ready"), r + 1)
            spread(pe, bank[:, 5, :], st[:, 16:20]).then_inc(S("rbc_done"), 1)

        def spread(pe, o, cols):
            for t in range(TT):
                last = pe.matmul(o[:, t * P:(t + 1) * P], cols[:, t:t + 1].to_broadcast([P, P]), ident,
                                 start=True, stop=True)
            return last

        class Steps:

            def __init__(self, eng, name, base=0):
                self.eng, self.name, self.base, self.n = eng, name, base, 0

            def link(self, ins):
                self.n += 1
                ins.then_inc(S(self.name), 1)
                self.eng.wait_ge(S(self.name), self.base + self.n)

        RSQRT = 10

        def rsqrt(eng, steps, v, tmp, o, done):
            steps.link(eng.tensor_scalar(o.bitcast(I32), v.bitcast(I32), -0.5, float(0x5F3759DF), ALU.mult, ALU.add))
            yield
            for n in range(3):
                steps.link(eng.tensor_tensor(tmp, o, v, ALU.mult))
                yield
                steps.link(eng.scalar_tensor_tensor(tmp, tmp, -0.5, o, ALU.mult, ALU.mult))
                yield
                ins = eng.scalar_tensor_tensor(o, tmp, 1.5, o, ALU.add, ALU.mult)
                if n < 2:
                    steps.link(ins)
                else:
                    ins.then_inc(S(done), 1)
                yield

        def norm_dve(dve, r):
            dve.wait_ge(S("ss_done"), r + 1)
            steps = Steps(dve, "small_step", RSQRT * r)
            steps.link(dve.tensor_scalar(st[:, 4:8], bank[:, 4, 0:4], 1.0 / D, EPS, ALU.mult, ALU.add))
            if past(r):
                dve.wait_ge(S("rbc_done"), r)
            for last in rsqrt(dve, steps, st[:, 4:8], st[:, 12:16], st[:, 16:20], "rstd_ready"):
                pass

        def residual(dve, t, d, scale):
            if d < KD - 1:
                dve.wait_ge(S("down_done"), 7 * t + d + 1)
            else:
                dve.wait_ge(S("unit_used"), DOWN_END[t])
            dve.scalar_tensor_tensor(h[:, d, :], bank[:, (d + 4) % 8, :], scale, h[:, d, :], ALU.mult, ALU.add)\
               .then_inc(S("h_ready"), 1)

        def enter_dve(dve, t, scale, r, b, U):
            for d in range(KD + 3):
                if b == 0 and d == 3:
                    supply_lo(dve, 0, 0)
                if d < KD and t is not None:
                    residual(dve, t, d, scale)
                if 2 <= d < KD + 2:
                    k = d - 2
                    if k >= 2:
                        dve.wait_ge(S("x_lo"), 8 * b + k - 1)
                    elif b:
                        dve.wait_ge(S("x_lo"), 8 * b)
                    if t is not None:
                        dve.wait_ge(S("h_ready"), 8 * t + k + 1)
                    elif b == 0 and k in (0, 2):
                        dve.wait_ge(S(f"x_landed{k // 2}"), 16)
                    dve.tensor_scalar(xn[:, k % 2, :], h[:, k, :], cst[:, C_GAIN + b * KD + k:C_GAIN + b * KD + k + 1],
                                      None, ALU.mult).then_inc(S("xn_ready"), 1)
                if d >= 3:
                    k = d - 3
                    dve.wait_ge(S("x_hi"), 8 * b + k + 1)
                    dve.tensor_tensor(xl[:, k, :], xn[:, k % 2, :], xh[:, k, :].bitcast(F32), ALU.subtract)\
                       .then_inc(S("x_lo"), 1)
            supply_lo(dve, U + 1, (U + 1) % 2)
            if b != 4:
                norm_dve(dve, r)
                dve.wait_ge(S("rbc_done"), r + 1)
                dve.tensor_copy(acc[:, :], bank[:, 5, :]).then_inc(S("rbc_kept"), 1)
                dve.wait_ge(S("rbc_kept"), r + 1)

        def two(ap):
            return ap.rearrange("p (a t) -> p a t", a=2)

        rbc2 = acc[:, :].unsqueeze(1).to_broadcast([P, 2, T])

        def ffn_pe(pe, f, t, r, b, U):
            s = U % 2

            def gate(j, part=None):
                return project_unit(pe, s, (0, 1), b if part else None, part)

            def up(j, part=None):
                return project_unit(pe, 1 - s, (2, 3), None, part)

            pe.wait_ge(S("w_lo"), U + 1)
            if r:
                pe.wait_ge(S("h_ready"), 8 * (r - 1) + 6)
            gate(0, (0, 8))
            if b != 4:
                norm_sums(pe, r)
            gate(0, (8, 16)).then_inc(S("unit_used"), 1)
            pe.wait_ge(S("w_lo"), U + 2)
            if r:
                pe.wait_ge(S("h_ready"), 8 * (r - 1) + 8)
            up(0, (0, 4))
            if b != 4:
                norm_spread(pe, r)
            up(0, (4, 16)).then_inc(S("unit_used"), 1)
            with pe.Fori(1, FJ) as j:
                pe.wait_ge(S("w_lo"), U + 2 * j + 1)
                pe.wait_ge(S("gate_scaled"), FJ * f + j)
                gate(j).then_inc(S("unit_used"), 1)
                pe.wait_ge(S("w_lo"), U + 2 * j + 2)
                pe.wait_ge(S("up_scaled"), FJ * f + j)
                up(j).then_inc(S("unit_used"), 1)

        def ffn_free(f):
            return {4: ("gate_scaled", FJ * (f + 1)), 6: ("up_scaled", FJ * (f + 1))}

        silu_pair = arena[:, A_SILU:A_SILU + 2 * T]

        def ffn_act(act, f, U):
            s = U % 2

            def silu(j):
                act.wait_ge(S("gate_scaled"), FJ * f + j + 1)
                act.activation(silu_pair, silu_pair, ACT.Silu).then_inc(S("silu_ready"), 1)

            supply_hi(act, U + 2, s)
            silu(0)
            with act.Fori(1, FJ) as j:
                supply_hi(act, U + 2 * j + 1, 1 - s)
                supply_hi(act, U + 2 * j + 2, s)
                silu(j)

        def ffn_dve(dve, f, U, AU):
            s = U % 2

            def gate_scale(j):
                if past(FJ * f + j):
                    dve.wait_ge(S("act_ready"), FJ * f + j)
                dve.wait_ge(S("unit_used"), U + 2 * j + 1)
                dve.tensor_tensor(two(silu_pair), bank[:, 0:2, :], rbc2, ALU.mult).then_inc(S("gate_scaled"), 1)

            def up_scale(j):
                dve.wait_ge(S("unit_used"), U + 2 * j + 2)
                dve.tensor_tensor(a_pair(j), bank[:, 2:4, :], rbc2, ALU.mult).then_inc(S("up_scaled"), 1)

            def product(j):
                dve.wait_ge(S("silu_ready"), FJ * f + j + 1)
                dve.wait_ge(S("up_scaled"), FJ * f + j + 1)
                dve.tensor_tensor(a_pair(j), a_pair(j), two(silu_pair), ALU.mult).then_inc(S("act_ready"), 1)

            def step(j):
                gate_scale(j)
                supply_lo(dve, U + 2 * j + 2, s)
                up_scale(j)
                supply_lo(dve, U + 2 * j + 3, 1 - s)
                product(j)

            step(0)
            with dve.Fori(1, FJ - 1) as j:
                step(j)
            gate_scale(FJ - 1)
            supply_lo(dve, U + 2 * FJ, s)
            split_a_lo(dve, 0, 0, AU)
            split_a_lo(dve, 1, 1, AU)
            up_scale(FJ - 1)
            product(FJ - 1)
            supply_lo(dve, U + 2 * FJ + 1, 1 - s)

        def a_pair(u):
            return arena[:, bass.ds(A_ACT + u * (2 * T), 2 * T)].rearrange("p (a t) -> p a t", a=2)

        def split_a_hi(act, u, s, AU):
            act.activation(ahi[s][:, :, :], a_pair(u), ACT.Copy).then_inc(S("a_hi"), 1)

        def split_a_lo(dve, u, s, AU):
            dve.wait_ge(S("a_hi"), AU + u + 1)
            dve.tensor_tensor(alo[s][:, :, :], a_pair(u), ahi[s][:, :, :].bitcast(F32), ALU.subtract)\
               .then_inc(S("a_lo"), 1)

        def down_pe(pe, t, n, U, AU, free, turn=None, late=None):
            def unit(u, first=False, last=False):
                ws, xs = (U + u) % 2, u % 2
                if first:
                    pe.wait_ge(S("a_lo"), AU + 1)
                pe.wait_ge(S("w_lo"), U + u + 1)
                pe.wait_ge(S("a_lo"), AU + u + 1)
                order = [(d, kt) for d in range(KD) for kt in range(2)] if last else \
                    [(d, kt) for kt in range(2) for d in range(KD)]
                if turn is not None and u < 2:
                    order = [(d, kt) for d in (0, 5 - late, 1, late) for kt in range(2)]
                for d, kt in order:
                    if first and turn is not None and (d, kt) == (late, 0):
                        turn()
                    if first and kt == 0 and d in free:
                        pe.wait_ge(S(free[d][0]), free[d][1])
                    ins = mm3(pe, bank[:, (d + 4) % 8, :], *w_block(ws, kt * D + d * P), ahi[xs][:, kt, :],
                              alo[xs][:, kt, :], first and kt == 0, last and kt == 1)
                    if last and kt == 1 and d < KD - 1:
                        ins.then_inc(S("down_done"), 1)
                ins.then_inc(S("unit_used"), 1)

            unit(0, first=True)
            pairs = max(0, (n - 2) // 2 - (n < 6))
            if pairs:
                with pe.Fori(0, pairs) as i:
                    for q in range(2):
                        loop_unit(pe, i, q, U, AU)
            for u in range(1 + 2 * pairs, n - 1):
                unit(u)
            unit(n - 1, last=True)

        def early_product(pe, order, n, U, AU):
            u, d = order[n // 2]
            kt = n % 2
            if n % 2 == 0:
                pe.wait_ge(S("w_lo"), U + u + 1)
                pe.wait_ge(S("a_lo"), AU + u + 1)
            mm3(pe, bank[:, d - 4, :], *w_block((U + u) % 2, kt * D + d * P), ahi[u][:, kt, :], alo[u][:, kt, :],
                u == 0 and kt == 0, False)

        def loop_unit(pe, i, q, U, AU):
            ws, xs = (U + 1 + q) % 2, (1 + q) % 2
            pe.wait_ge(S("w_lo"), U + 2 * i + q + 2)
            pe.wait_ge(S("a_lo"), AU + 2 * i + q + 2)
            for kt in range(2):
                for d in range(KD):
                    ins = mm3(pe, bank[:, (d + 4) % 8, :], *w_block(ws, kt * D + d * P), ahi[xs][:, kt, :],
                              alo[xs][:, kt, :], False, False)
            ins.then_inc(S("unit_used"), 1)

        def down_act(act, t, n, U, AU):
            def after(u, sw, sa, a):
                supply_hi(act, U + u + 2, sw)
                if a:
                    act.wait_ge(S("unit_used"), U + u + 1)
                    split_a_hi(act, u + 2, sa, AU)

            loops = (n - 3) // 2 if n > 4 else 0
            if loops:
                with act.Fori(0, loops) as i:
                    after(2 * i, U % 2, 0, True)
                    after(2 * i + 1, (U + 1) % 2, 1, True)
            for u in range(2 * loops, n - 1):
                if U + u + 2 < N_UNITS:
                    supply_hi(act, U + u + 2, (U + u) % 2)
                if u + 2 < n:
                    act.wait_ge(S("unit_used"), U + u + 1)
                    split_a_hi(act, u + 2, u % 2, AU)

        def down_dve(dve, n, U, AU):
            loops = (n - 3) // 2 if n > 4 else 0
            if loops:
                with dve.Fori(0, loops) as i:
                    for q in range(2):
                        supply_lo(dve, U + 2 * i + q + 2, (U + q) % 2)
                        dve.wait_ge(S("a_hi"), AU + 2 * i + q + 3)
                        dve.tensor_tensor(alo[q][:, :, :], a_pair(2 * i + q + 2), ahi[q][:, :, :].bitcast(F32),
                                          ALU.subtract).then_inc(S("a_lo"), 1)
            for u in range(2 * loops, n - 1):
                if U + u + 2 < N_UNITS:
                    supply_lo(dve, U + u + 2, (U + u) % 2)
                if u + 2 < n:
                    split_a_lo(dve, u + 2, u % 2, AU)

        def gdn_pre_pe(pe):
            pe.wait_ge(S("x_lo"), 16)
            pe.wait_ge(S("ba_split"), 2)
            pe.wait_ge(S("h_ready"), 8)
            for k in range(KD):
                last = mm3(pe, bank[0:16, 6, :], bahi[:, k, :], balo[:, k, :], xh[:, k, :], xl[:, k, :],
                           k == 0, k == KD - 1)
            last.then_inc(S("ba_done"), 1)

        def gdn_turn_pe(pe):
            pe.wait_ge(S("ba_scaled"), 1)
            for t in range(TT):
                last = pe.transpose(bank[:, 7, t * 16:(t + 1) * 16], ba_rows[0:16, t * P:(t + 1) * P], ident[0:16, 0:16])
            last.then_inc(S("ba_turned"), 1)

        def gdn_cum_pe(pe):
            pe.wait_ge(S("pre_dve"), PRE_G)
            g = hc[:, K_G, :, :].rearrange("p a b -> p (a b)")
            pe.matmul(bank[:, 7, 0:32], upper, g, start=True, stop=True)
            pe.matmul(bank[:, 7, 32:64], ones, g, start=True, stop=True).then_inc(S("cum_done"), 1)

        PRE_G = 12
        small = [slot(0)[:, n * 32:(n + 1) * 32].rearrange("p (a b) -> p a b", a=TT) for n in range(16)]
        sm_x, sm_e1, sm_ax, sm_e2, sm_u, sm_ln, sm_t, sm_ru, sm_gl, sm_d, sm_eg = small[2:13]
        ba = slot(0)[:, 0:64].rearrange("p (a b) -> p a b", a=TT)
        alog_e = slot(0)[:, 480:488]
        ba_rows = slot(1)

        def gdn_pre_act(act):
            act.wait_ge(S("pre_dve"), 2)
            act.activation(sm_e1, ba[:, :, 0:H], ACT.Exp, scale=-1.0).then_inc(S("pre_act"), 1)
            act.activation(sm_ax, sm_x, ACT.Abs).then_inc(S("pre_act"), 1)
            act.activation(alog_e, cst[:, C_ALOG:C_ALOG + H], ACT.Exp).then_inc(S("pre_act"), 1)
            act.wait_ge(S("pre_act"), 3)
            act.activation(sm_e2, sm_ax, ACT.Exp, scale=-1.0).then_inc(S("pre_act"), 1)
            act.wait_ge(S("pre_dve"), 3)
            act.activation(sm_ln, sm_u, ACT.Ln).then_inc(S("pre_act"), 1)
            act.wait_ge(S("pre_dve"), PRE_G + 3)
            act.activation(sm_eg, hc[:, K_CUM, :, :], ACT.Exp).then_inc(S("pre_act"), 1)
            act.activation(hc[:, K_KDEC, :, :], sm_d, ACT.Exp).then_inc(S("pre_act"), 1)
            act.activation(hc[:, K_LAST, :, :], sm_gl, ACT.Exp).then_inc(S("pre_act"), 1)

        def gdn_pre_dve(dve):
            st_ = Steps(dve, "pre_dve")
            dve.wait_ge(S("ba_turned"), 1)
            st_.link(dve.tensor_copy(slot(0)[:, 0:64], bank[:, 7, 0:64]))
            dtb = cst[:, C_DTB:C_DTB + H].unsqueeze(1).to_broadcast([P, TT, H])
            st_.link(dve.tensor_tensor(sm_x, ba[:, :, H:2 * H], dtb, ALU.add))
            dve.wait_ge(S("pre_act"), 4)
            st_.link(dve.tensor_scalar(sm_u, sm_e2, 1.0, None, ALU.add))
            st_.link(dve.scalar_tensor_tensor(sm_t, sm_u, -1.0, sm_e2, ALU.add, ALU.subtract))
            st_.link(dve.reciprocal(sm_ru, sm_u))
            st_.link(dve.tensor_tensor(sm_t, sm_t, sm_ru, ALU.mult))
            dve.wait_ge(S("pre_act"), 5)
            st_.link(dve.tensor_tensor(sm_ln, sm_ln, sm_t, ALU.subtract))
            st_.link(dve.scalar_tensor_tensor(sm_x, sm_x, 0.0, sm_ln, ALU.max, ALU.add))
            st_.link(dve.scalar_tensor_tensor(hc[:, K_G, :, :], sm_x, -1.0,
                                              alog_e.unsqueeze(1).to_broadcast([P, TT, H]), ALU.mult, ALU.mult))
            st_.link(dve.tensor_scalar(sm_e1, sm_e1, 1.0, None, ALU.add))
            st_.link(dve.reciprocal(hc[:, K_BETA, :, :], sm_e1))
            st_.link(dve.tensor_scalar(hc[:, K_NBETA, :, :], hc[:, K_BETA, :, :], -1.0, None, ALU.mult))
            assert st_.n == PRE_G

        def gdn_cum_dve(dve):
            st_ = Steps(dve, "pre_dve", PRE_G)
            dve.wait_ge(S("cum_done"), 1)
            flat = "p a b -> p (a b)"
            st_.link(dve.tensor_copy(hc[:, K_CUM, :, :].rearrange(flat), bank[:, 7, 0:32]))
            st_.link(dve.tensor_copy(sm_gl.rearrange(flat), bank[:, 7, 32:64]))
            st_.link(dve.tensor_tensor(sm_d, sm_gl, hc[:, K_CUM, :, :], ALU.subtract))
            dve.wait_ge(S("pre_act"), 8)
            st_.link(dve.tensor_tensor(hc[:, K_BEXPG, :, :], hc[:, K_BETA, :, :], sm_eg, ALU.mult))

        def chunks(pe, b, lhs, rhs, start=True, stop=True):
            for n in range(TT):
                cs = slice(n * P, (n + 1) * P)
                last = pe.matmul(bank[:, b, cs], lhs[:, cs], rhs[:, cs], start=start, stop=stop)
            return last

        def half(ap, w, which):
            return ap.rearrange("p (n h w) -> p n h w", h=2, w=w)[:, :, which, :]

        def half_chunks(pe, b, lhs, rhs, w, which):
            for n in range(TT):
                cs = slice(n * P, (n + 1) * P)
                last = pe.matmul(half(bank[:, b, cs], w, which), lhs[:, cs], half(rhs[:, cs], w, which),
                                 start=True, stop=True)
            return last

        def turned(pe, b, src):
            for n in range(TT):
                cs = slice(n * P, (n + 1) * P)
                last = pe.transpose(bank[:, b, cs], src[:, cs], ident)
            return last

        GDN_EARLY = [(u, d) for u in range(2) for d in (4, 5, 6)] + [(0, 7), (1, 7)]

        def gdn_pe(pe, hp, c, o):
            U = BASE["gdn_in"]
            core, proj, fin = c is not None, hp is not None, o is not None
            UA = U + 2 * hp if proj else None
            first = proj and not core
            at = 0

            def more(count):
                nonlocal at
                if not proj:
                    if core and at < 16:
                        if at == 4:
                            pe.wait_ge(S("expg_ready"), H)
                        if at == 12:
                            pe.wait_ge(S("z_pre"), H)
                        early_product(pe, GDN_EARLY, at, BASE["gdn_out"], AU["gdn"])
                        at += 1
                    return
                for n in range(at, at + count):
                    f, k = n // KD, n % KD
                    if first and n < KD:
                        pe.wait_ge(S("x_lo"), 8 + n + 1)
                    if n == 0:
                        pe.wait_ge(S("w_lo"), UA + 1)
                        if first:
                            pe.wait_ge(S("h_ready"), 6)
                        if core:
                            pe.wait_ge(S("k_ready"), hp)
                    if n == 2 * KD:
                        pe.wait_ge(S("w_lo"), UA + 2)
                        if core:
                            pe.wait_ge(S("expg_ready"), hp)
                    if n == 3 * KD and core:
                        pe.wait_ge(S("z_pre"), hp)
                    ins = mm3(pe, bank[:, f, :], *w_block((U + f // 2) % 2, k * 256 + (f % 2) * P), xh[:, k, :],
                              xl[:, k, :], k == 0, k == KD - 1)
                    if k == KD - 1:
                        ins.then_inc(S(("q_projected", "unit_used", "v_projected", "unit_used")[f]), 1)
                at += count

            if core:
                pe.wait_ge(S("k_ready"), c + 1)
                chunks(pe, 4, slot(G_K), slot(G_K)).then_inc(S("kk_done"), 1)
                chunks(pe, 7, slot(G_K), slot(G_Q)).then_inc(S("qk_done"), 1)
            more(3)
            if core:
                pe.wait_ge(S("na_ready"), c + 1)
                turned(pe, 4, slot(G_NA)).then_inc(S("nat_done"), 1)
            more(2)
            if core:
                pe.wait_ge(S("n0t_ready"), c + 1)
                if fin:
                    pe.wait_ge(S("oc_ready"), c)
                chunks(pe, 5, slot(G_N0T), slot(G_N0)).then_inc(S("n2_done"), 1)
                if fin:
                    pe.wait_ge(S("wt_ready"), c)
                chunks(pe, 6, slot(G_N0), slot(G_N0T)).then_inc(S("n2t_done"), 1)
            more(1)
            if core:
                pe.wait_ge(S("n2_ready"), c + 1)
                pe.wait_ge(S("n2t_ready"), c + 1)
                pe.wait_ge(S("nat_ready"), c + 1)
                chunks(pe, 4, slot(G_N2), slot(G_N2T)).then_inc(S("n4t_done"), 1)
                pe.wait_ge(S("qkm_ready"), c + 1)
                chunks(pe, 7, slot(G_N2T), slot(G_N2)).then_inc(S("n4_done"), 1)
                pe.wait_ge(S("t1_ready"), c + 1)
                chunks(pe, 5, slot(G_N2T), slot(G_TA)).then_inc(S("p2_done"), 1)
            more(1)
            if core:
                pe.wait_ge(S("n4t_ready"), c + 1)
                pe.wait_ge(S("n4_ready"), c + 1)
                chunks(pe, 6, slot(G_N4), slot(G_N0T)).then_inc(S("n8t_done"), 1)
                pe.wait_ge(S("t2_ready"), c + 1)
                chunks(pe, 7, slot(G_N0T), slot(G_TB)).then_inc(S("p4_done"), 1)
                pe.wait_ge(S("v_silu"), c + 1)
                turned(pe, 5, slot(G_V)).then_inc(S("vtr_done"), 1)
            more(2)
            if first:
                norm_sums(pe, 1)
            if core:
                pe.wait_ge(S("n8t_ready"), c + 1)
                pe.wait_ge(S("t4_ready"), c + 1)
                chunks(pe, 4, slot(G_NA), slot(G_TA)).then_inc(S("p8_done"), 1)
                turned(pe, 6, slot(G_K)).then_inc(S("ktr_done"), 1)
            more(2)
            if core:
                pe.wait_ge(S("t8_ready"), c + 1)
                pe.wait_ge(S("vb_ready"), c + 1)
                turned(pe, 5, slot(G_TB)).then_inc(S("tt_done"), 1)
                pe.wait_ge(S("b_ready"), 3 * c + 1)
                pe.wait_ge(S("kd_ready"), c + 1)
                chunks(pe, 6, slot(G_B1), slot(G_TB)).then_inc(S("w1_done"), 1)
            more(2)
            if first:
                norm_spread(pe, 1)
                gdn_pre_pe(pe)
            if core:
                pe.wait_ge(S("tt_ready"), c + 1)
                pe.wait_ge(S("w1_ready"), c + 1)
                half_chunks(pe, 7, slot(G_N2), slot(G_N2T), 16, 0).then_inc(S("ta_done"), 1)
                half_chunks(pe, 4, slot(G_N2T), slot(G_N2), 16, 1).then_inc(S("tta_done"), 1)
            if fin:
                if not core:
                    pe.wait_ge(S("wt_ready"), H)
                pe.wait_ge(S("on_ready"), o + 1)
                turned(pe, 6, xn[:, 1, :]).then_inc(S("otr_done"), 1)
            more(2)
            if first:
                gdn_turn_pe(pe)
            if core:
                pe.wait_ge(S("ta_ready"), c + 1)
                pe.wait_ge(S("b_ready"), 3 * c + 2)
                chunks(pe, 5, slot(G_B2), slot(G_TB)).then_inc(S("w2_done"), 1)
            more(2)
            if core:
                pe.wait_ge(S("tta_ready"), c + 1)
                pe.wait_ge(S("w2_ready"), c + 1)
                if fin:
                    pe.wait_ge(S("y_ready"), o + 1)
                half_chunks(pe, 6, slot(G_N2), slot(G_N2T), 32, 0).then_inc(S("tb_done"), 1)
                half_chunks(pe, 7, slot(G_N2T), slot(G_N2), 32, 1).then_inc(S("ttb_done"), 1)
            more(2)
            if core:
                pe.wait_ge(S("tb_ready"), c + 1)
                pe.wait_ge(S("b_ready"), 3 * c + 3)
                chunks(pe, 4, slot(G_B3), slot(G_TB)).then_inc(S("w3_done"), 1)
            more(2)
            if core:
                pe.wait_ge(S("ttb_ready"), c + 1)
                pe.wait_ge(S("w3_ready"), c + 1)
                half_chunks(pe, 5, slot(G_N2T), slot(G_N2), 64, 1).then_inc(S("ttc_done"), 1)
            more(2)
            if core:
                pe.wait_ge(S("ttc_ready"), c + 1)
                chunks(pe, 6, slot(G_KBG), slot(G_N2)).then_inc(S("wt_done"), 1)
            more(1)
            if proj:
                pe.wait_ge(S("qk_sq"), 2 * hp + 2)
                for q in range(2):
                    for t in range(TT):
                        ins = pe.matmul(bank[:, 0, q * TT + t:q * TT + t + 1], sq[:, q, t * P:(t + 1) * P],
                                        ones[:, 0:1], start=True, stop=True)
                ins.then_inc(S("qk_ss"), 1)
            for n in range(TT):
                cs = slice(n * P, (n + 1) * P)
                if core:
                    ins = pe.matmul(bank[:, 7, cs], slot(G_N2)[:, cs], slot(G_VB)[:, cs], start=True, stop=n == 0)
                    if n == 0:
                        pe.wait_ge(S("wt_ready"), c + 1)
                    else:
                        pe.wait_ge(S("s_ready"), 3 * c + n)
                        ins = pe.matmul(bank[:, 7, cs], slot(G_N0)[:, cs], state, start=False, stop=True)
                    ins.then_inc(S("u_done"), 1)
                    if n == 0:
                        pe.wait_ge(S("qd_ready"), c + 1)
                    else:
                        pe.matmul(bank[:, 5, cs], slot(G_QD)[:, cs], state, start=True, stop=False)
                if n < 2:
                    more(1)
                elif proj and n == 2:
                    if first:
                        gdn_cum_pe(pe)
                    pe.wait_ge(S("gcur_ready"), 2 * hp + 2)
                    pe.wait_ge(S("v_pre"), hp + 1)
                    for t in range(TT):
                        ins = pe.matmul(bank[:, 2, t * P:(t + 1) * P], gcur[:, 0, t:t + 1].to_broadcast([P, P]),
                                        upper, start=True, stop=True)
                    ins.then_inc(S("gbc_done"), 1)
                elif proj:
                    spread(pe, bank[:, 0, :], st[:, 48:52]).then_inc(S("k_bc"), 1)
                if core:
                    pe.wait_ge(S("u_ready"), 4 * c + n + 1)
                    if n < TT - 1:
                        pe.matmul(bank[:, 4, 0:P], slot(G_KD)[:, cs], slot(G_N0T)[:, cs], start=True, stop=True)\
                          .then_inc(S("s_done"), 1)
                    ins = pe.matmul(bank[:, 5, cs], slot(G_QK)[:, cs], slot(G_N0T)[:, cs], start=n == 0, stop=True)
                    if n == TT - 1:
                        ins.then_inc(S("o_done"), 1)
                if n < 2:
                    more(1)
                elif proj and n == 2:
                    pe.wait_ge(S("qk_rn"), hp + 1)
                    spread(pe, bank[:, 1, :], st[:, 44:48]).then_inc(S("q_bc"), 1)
            more(4)
            assert at == (4 * KD if proj else 16 if core else 0)

        def gdn_act(act, hp, c, o):
            U = BASE["gdn_in"]
            core, proj, fin = c is not None, hp is not None, o is not None
            UA = U + 2 * hp if proj else None

            def keep(b, dst, need, name, scale=1.0):
                if core:
                    act.wait_ge(S(need), c + 1)
                    act.activation(slot(dst), bank[:, b, :], ACT.Copy, scale=scale).then_inc(S(name), 1)

            def silu_square(q):
                if proj:
                    x = slot(G_QS + q)
                    act.wait_ge(S("qk_conv"), 8 * hp + 4 * q + 4)
                    act.activation(x, x, ACT.Silu).then_inc(S("qk_silu"), 1)
                    act.wait_ge(S("qk_silu"), 2 * hp + q + 1)
                    if core:
                        act.wait_ge(S("qk_ss"), hp)
                    act.activation(sq[:, q, :], x, ACT.Square).then_inc(S("qk_sq"), 1)

            if core:
                act.wait_ge(S("v_conv"), 4 * c + 4)
                act.activation(slot(G_V), slot(G_V), ACT.Silu).then_inc(S("v_silu"), 1)
                supply_hi(act, U + 2 * c + 3, (U + 1) % 2)
                act.wait_ge(S("n0t_ready"), c + 1)
            keep(4, G_NAT, "nat_done", "nat_ready")
            keep(5, G_N2, "n2_done", "n2_ready")
            keep(7, G_N4, "n4_done", "n4_ready")
            keep(6, G_NA, "n8t_done", "n8t_ready")
            keep(5, G_N2, "tt_done", "tt_ready")
            keep(5, G_N2T, "w2_done", "w2_ready")
            if core:
                act.wait_ge(S("z_pre"), c + 1)
                act.activation(slot(G_Z), slot(G_Z), ACT.Silu).then_inc(S("z_silu"), 1)
            silu_square(0)
            keep(4, G_N2T, "w3_done", "w3_ready")
            if proj:
                supply_hi(act, UA + 2, U % 2)
            silu_square(1)
            keep(6, G_N0, "wt_done", "wt_ready", -1.0)
            if not core:
                gdn_pre_act(act)
            if proj:
                act.wait_ge(S("gbc_done"), hp + 1)
                if core:
                    act.wait_ge(S("du_ready"), hp)
                for t in range(TT):
                    cs = slice(t * P, (t + 1) * P)
                    ins = act.activation(slot(G_D)[:, cs], bank[:, 2, cs], ACT.Abs, scale=-1.0, bias=gcur[:, 1, t:t + 1])
                ins.then_inc(S("dabs_ready"), 1)
                act.wait_ge(S("dabs_ready"), hp + 1)
                act.activation(slot(G_D), slot(G_D), ACT.Exp, scale=-1.0).then_inc(S("decay_ready"), 1)
                if core:
                    act.wait_ge(S("qd_ready"), hp)
                act.activation(slot(G_EG), bank[:, 2, :], ACT.Exp).then_inc(S("expg_ready"), 1)
            if core:
                act.wait_ge(S("o_done"), c + 1)
                if fin:
                    act.wait_ge(S("otr_done"), c)
                for t in range(TT):
                    cs = slice(t * P, (t + 1) * P)
                    act.activation(xn[:, 1, cs], bank[:, 5, cs], ACT.Square, accum_out=st[:, 52 + t:53 + t])
                act.activation(xn[:, 0, :], bank[:, 5, :], ACT.Copy).then_inc(S("oc_ready"), 1)

        def gdn_dve(dve, hp, c, o):
            core, proj, fin = c is not None, hp is not None, o is not None

            U = BASE["gdn_in"]

            def conv_in(q, need, count, name, used):
                if proj:
                    dve.wait_ge(S(need), count)
                    if core:
                        dve.wait_ge(S("v_conv" if q == 2 else "qk_conv"), used)
                    else:
                        dve.wait_ge(S("pad_ready"), 1)
                    dve.tensor_tensor(pre3[:, q, 3:3 + T], bank[:, q, :], acc[:, :], ALU.mult).then_inc(S(name), 1)

            def add(b, a, o, need, name):
                if core:
                    dve.wait_ge(S(need), c + 1)
                    dve.tensor_tensor(slot(o), bank[:, b, :], slot(a), ALU.add).then_inc(S(name), 1)

            def grow(b, o, w, which, need, name):
                if core:
                    dve.wait_ge(S(need), c + 1)
                    dve.tensor_tensor(half(slot(o), w, which), half(bank[:, b, :], w, which), half(slot(o), w, which),
                                      ALU.add).then_inc(S(name), 1)

            def keep(b, dst, need, name):
                if core:
                    dve.wait_ge(S(need), c + 1)
                    dve.tensor_copy(slot(dst), bank[:, b, :]).then_inc(S(name), 1)

            def conv(q, dst, name, base):
                if not proj:
                    return
                for j in range(4):
                    x, w = pre3[:, q, j:j + T], cwh[:, q, j:j + 1]
                    if j == 0:
                        ins = dve.tensor_scalar(slot(dst), x, w, None, ALU.mult)
                    else:
                        dve.wait_ge(S(name), base + j)
                        ins = dve.scalar_tensor_tensor(slot(dst), x, w, slot(dst), ALU.mult, ALU.add)
                    ins.then_inc(S(name), 1)

            o_steps = Steps(dve, "o_step", RSQRT * o if fin else 0)
            o_norm = rsqrt(dve, o_steps, st[:, 56:60], st[:, 76:80], st[:, 80:84], "o_rn")

            def out_steps(count):
                if fin:
                    for _ in range(count):
                        next(o_norm)

            if fin:
                dve.wait_ge(S("oc_ready"), o + 1)
                o_steps.link(dve.tensor_scalar(st[:, 56:60], st[:, 52:56], 1.0 / P, EPS, ALU.mult, ALU.add))
            if core:
                if fin:
                    dve.wait_ge(S("s_ready"), 3 * c)
                dve.tensor_copy(hcur[:, :, :], hc[:, :, :, bass.ds(c, 1)].rearrange("p a b c -> p a (b c)"))\
                   .then_inc(S("hcur_ready"), 1)
                dve.wait_ge(S("kk_done"), c + 1)
                dve.wait_ge(S("dl_ready"), c + 1)
                dve.tensor_tensor(slot(G_NA), bank[:, 4, :], slot(G_DL), ALU.mult).then_inc(S("na_ready"), 1)
                dve.wait_ge(S("na_ready"), c + 1)
                dve.tensor_tensor(c4(slot(G_N0)), c4(slot(G_NA)), over_c(gm_diag), ALU.mult)\
                   .then_inc(S("n0_ready"), 1)
            out_steps(1)
            if core:
                dve.wait_ge(S("nat_done"), c + 1)
                dve.tensor_tensor(c4(slot(G_N0T)), c4(bank[:, 4, :]), over_c(gm_diag), ALU.mult)\
                   .then_inc(S("n0t_ready"), 1)
            out_steps(3)
            keep(6, G_N2T, "n2t_done", "n2t_ready")
            if core:
                dve.wait_ge(S("qk_done"), c + 1)
                dve.wait_ge(S("du_ready"), c + 1)
                dve.tensor_tensor(slot(G_QK), bank[:, 7, :], slot(G_DU), ALU.mult).then_inc(S("qkm_ready"), 1)
            out_steps(2)
            keep(4, G_N0T, "n4t_done", "n4t_ready")
            add(5, G_TA, G_TB, "p2_done", "t2_ready")
            out_steps(4)
            add(7, G_TB, G_TA, "p4_done", "t4_ready")
            if core:
                dve.wait_ge(S("hcur_ready"), c + 1)
                dve.wait_ge(S("vtr_done"), c + 1)
                dve.tensor_tensor(c4(slot(G_VB)), c4(bank[:, 5, :]), over_t(hcur[:, K_BETA, :]), ALU.mult)\
                   .then_inc(S("vb_ready"), 1)
            conv_in(0, "q_projected", hp + 1 if proj else 0, "qk_pre", 8 * hp if proj else 0)
            add(4, G_TA, G_TB, "p8_done", "t8_ready")
            if core:
                dve.wait_ge(S("ktr_done"), c + 1)
                dve.tensor_tensor(c4(slot(G_KBG)), c4(bank[:, 6, :]), over_t(hcur[:, K_BEXPG, :]), ALU.mult)
                dve.tensor_tensor(c4(slot(G_KD)), c4(bank[:, 6, :]), over_t(hcur[:, K_KDEC, :]), ALU.mult)\
                   .then_inc(S("kd_ready"), 1)
            keep(6, G_N2T, "w1_done", "w1_ready")
            if fin:
                dve.wait_ge(S("o_rn"), o + 1)
                dve.tensor_tensor(c4(xn[:, 1, :]), c4(xn[:, 0, :]), over_t(st[:, 80:84]), ALU.mult)\
                   .then_inc(S("on_ready"), 1)
            grow(7, G_TB, 16, 0, "ta_done", "ta_ready")
            if core:
                dve.wait_ge(S("tt_ready"), c + 1)
            grow(4, G_N2, 16, 1, "tta_done", "tta_ready")
            if fin:
                dve.wait_ge(S("otr_done"), o + 1)
                dve.wait_ge(S("z_silu"), o + 1)
                dve.scalar_tensor_tensor(arena[:, bass.ds(o * T, T)], bank[:, 6, :], cst[:, C_ONORM:C_ONORM + 1],
                                         slot(G_Z), ALU.mult, ALU.mult).then_inc(S("y_ready"), 1)
            if core:
                if fin:
                    dve.wait_ge(S("y_ready"), c)
                dve.wait_ge(S("unit_used"), U + 2 * c + 2)
                dve.tensor_tensor(slot(G_Z), bank[:, 3, :], acc[:, :], ALU.mult).then_inc(S("z_pre"), 1)
            if proj:
                if core:
                    dve.wait_ge(S("v_conv"), 4 * hp)
                dve.tensor_copy(cwh[:, :, :].rearrange("p a b -> p (a b)"), cst[:, bass.ds(C_CONV + 12 * hp, 12)])\
                   .then_inc(S("gcur_ready"), 1)
                dve.wait_ge(S("gcur_ready"), 2 * hp + 1)
                dve.wait_ge(S("qk_pre"), 2 * hp + 1)
                if core:
                    dve.wait_ge(S("k_ready"), hp)
            conv(0, G_QS, "qk_conv", 8 * hp if proj else 0)
            grow(6, G_TB, 32, 0, "tb_done", "tb_ready")
            grow(7, G_N2, 32, 1, "ttb_done", "ttb_ready")
            conv_in(1, "unit_used", U + 2 * hp + 1 if proj else 0, "qk_pre", 8 * hp if proj else 0)
            if proj:
                dve.wait_ge(S("qk_pre"), 2 * hp + 2)
            conv(1, G_KS, "qk_conv", 8 * hp + 4 if proj else 0)
            grow(5, G_N2, 64, 1, "ttc_done", "ttc_ready")
            def decay_columns():
                if proj:
                    if core:
                        dve.wait_ge(S("expg_ready"), hp)
                    dve.tensor_copy(gcur[:, :, :], hc[:, 0:2, :, bass.ds(hp, 1)].rearrange("p a b c -> p a (b c)"))\
                       .then_inc(S("gcur_ready"), 1)

            conv_in(2, "v_projected", hp + 1 if proj else 0, "v_pre", 4 * hp if proj else 0)
            steps = Steps(dve, "qk_step", RSQRT * hp if proj else 0)
            norms = rsqrt(dve, steps, st[:, 20:28], st[:, 68:76], st[:, 44:52], "qk_rn")

            def norm_steps(count):
                if proj:
                    for _ in range(count):
                        next(norms)

            if core:
                decay_columns()
            elif proj:
                gdn_pre_dve(dve)
            for n in range(TT):
                cs = slice(n * P, (n + 1) * P)
                if core:
                    dve.wait_ge(S("u_done"), 4 * c + n + 1)
                    dve.tensor_copy(slot(G_N0T)[:, cs], bank[:, 7, cs]).then_inc(S("u_ready"), 1)
                if proj and n == 0:
                    dve.wait_ge(S("qk_ss"), hp + 1)
                    if core:
                        dve.wait_ge(S("k_bc"), hp)
                    steps.link(dve.tensor_scalar(st[:, 20:28], bank[:, 0, 0:8], EPS, None, ALU.add))
                    norm_steps(3)
                elif n == 1:
                    norm_steps(4)
                    if proj and not core:
                        gdn_cum_dve(dve)
                        decay_columns()
                if core and n < TT - 1:
                    dve.wait_ge(S("s_done"), 3 * c + n + 1)
                    if n == 0:
                        ins = dve.tensor_copy(state, bank[:, 4, 0:P])
                    else:
                        dve.wait_ge(S("s_ready"), 3 * c + n)
                        ins = dve.scalar_tensor_tensor(state, state, hcur[:, K_LAST, n:n + 1], bank[:, 4, 0:P],
                                                       ALU.mult, ALU.add)
                    ins.then_inc(S("s_ready"), 1)
                if n == 0:
                    norm_steps(3)
            if proj:
                dve.wait_ge(S("q_bc"), hp + 1)
                if core:
                    dve.wait_ge(S("qd_ready"), hp)
                dve.scalar_tensor_tensor(slot(G_Q), slot(G_QS), float(P) ** -0.5, bank[:, 1, :], ALU.mult, ALU.mult)
                dve.wait_ge(S("k_bc"), hp + 1)
                dve.tensor_tensor(slot(G_K), slot(G_KS), bank[:, 0, :], ALU.mult).then_inc(S("k_ready"), 1)
                dve.wait_ge(S("v_pre"), hp + 1)
            conv(2, G_V, "v_conv", 4 * hp if proj else 0)

        def gdn_pool(pool, hp, c, o):
            U = BASE["gdn_in"]
            if c is not None:
                pool.wait_ge(S("decay_ready"), c + 1)
                pool.wait_ge(S("mb_ready"), c + 1)
                pool.tensor_tensor(slot(G_DL), slot(G_DL), slot(G_D), ALU.mult).then_inc(S("dl_ready"), 1)
                pool.tensor_tensor(c4(slot(G_DU)), c4(slot(G_D)), over_c(upper), ALU.mult).then_inc(S("du_ready"), 1)
                pool.wait_ge(S("n0_ready"), c + 1)
                pool.tensor_tensor(c4(slot(G_TA)), c4(slot(G_N0)), over_c(ident), ALU.add).then_inc(S("t1_ready"), 1)
                pool.wait_ge(S("nat_ready"), c + 1)
                pool.tensor_tensor(c4(slot(G_B1)), c4(slot(G_NAT)), over_c(gm_b1), ALU.mult).then_inc(S("b_ready"), 1)
                supply_lo(pool, U + 2 * c + 3, (U + 1) % 2)
                pool.tensor_tensor(c4(slot(G_B2)), c4(slot(G_NAT)), over_c(gm_b2), ALU.mult).then_inc(S("b_ready"), 1)
                pool.tensor_tensor(c4(slot(G_B3)), c4(slot(G_NAT)), over_c(gm_b3), ALU.mult).then_inc(S("b_ready"), 1)
                if o is not None:
                    pool.wait_ge(S("o_done"), c)
                pool.tensor_tensor(slot(G_QD), slot(G_Q), slot(G_EG), ALU.mult).then_inc(S("qd_ready"), 1)
            if hp is not None:
                if c is not None:
                    pool.wait_ge(S("na_ready"), hp)
                else:
                    pool.wait_ge(S("pre_dve"), PRE_G)
                    pool.wait_ge(S("w_lo"), U + 2)
                pool.tensor_tensor(c4(slot(G_DL)), over_c(gm_lower), hc[:, K_NBETA, :, bass.ds(hp, 1)].to_broadcast([P, TT, P]),
                                   ALU.mult).then_inc(S("mb_ready"), 1)
                supply_lo(pool, U + 2 * hp + 2, U % 2)

        def gdn(eng, one):
            one(eng, 0, None, None)
            one(eng, 1, 0, None)
            one(eng, 2, 1, 0)
            with eng.Fori(3, H) as i:
                one(eng, i, i - 1, i - 2)

        def gdn_last(eng, one):
            one(eng, None, H - 1, H - 2)

        def gdn_end(eng, one):
            one(eng, None, None, H - 1)

        X_COS, X_SIN, X_ANG, X_TURNS, X_POS, X_RAW, X_ROT, X_PART = 0, 1, 2, 3, 4, 5, 2, 5
        X_Q, X_QZ, X_P, X_PT = 8, 16, 18, 22
        TWO_PI = (6.28125, 2029.0 / 2 ** 20, 2 * math.pi - 6.28125 - 2029.0 / 2 ** 20)
        ROUND = 1.5 * 2 ** 23
        TRIG = 21

        def trig_pool(pool, n, AU):
            pool.wait_ge(S("a_lo"), AU + 3)
            pool.dma_start(slot(X_POS).bitcast(I32), pos_in).then_inc(S("pos_landed"), 16)
            steps = Steps(pool, "angle_step", TRIG * n)
            pool.wait_ge(S("pos_landed"), 16 * (n + 1))
            steps.link(pool.tensor_copy(slot(X_ANG), slot(X_POS).bitcast(I32)))
            steps.link(pool.tensor_scalar(slot(X_ANG), slot(X_ANG), cst[:, C_FREQ:C_FREQ + 1], None, ALU.mult))
            for dst, turn, shift in ((X_SIN, 0.0, 0.0), (X_COS, 0.25, math.pi / 2)):
                turns = slot(X_TURNS)
                steps.link(pool.tensor_scalar(turns, slot(X_ANG), 1.0 / (2 * math.pi), turn, ALU.mult, ALU.add))
                steps.link(pool.tensor_scalar(turns, turns, ROUND, None, ALU.add))
                steps.link(pool.tensor_scalar(turns, turns, ROUND, None, ALU.subtract))
                src = slot(X_ANG)
                for m in TWO_PI:
                    steps.link(pool.tensor_scalar(slot(X_PART), turns, -m, None, ALU.mult))
                    steps.link(pool.tensor_tensor(slot(dst), slot(X_PART), src, ALU.add))
                    src = slot(dst)
                if shift:
                    steps.link(pool.tensor_scalar(slot(dst), slot(dst), shift, None, ALU.add))
                pool.tensor_scalar(slot(dst), slot(dst), math.pi, -math.pi, ALU.min, ALU.max)\
                   .then_inc(S("trig_arg"), 1)
            assert steps.n == TRIG

        def trig_act(act, n):
            for k, dst in enumerate((X_SIN, X_COS)):
                act.wait_ge(S("trig_arg"), 2 * n + k + 1)
                act.activation(slot(dst), slot(dst), ACT.Sin).then_inc(S("trig_ready"), 1)

        def rope_project_pe(pe, U, i, r, b, n):
            def part(a, e):
                return project_unit(pe, (U + i) % 2, (pair, pair + 1), b if i == 0 else None, (a, e))

            pair = 2 * (i % 2)
            pe.wait_ge(S("w_lo"), U + i + 1)
            if i == 0:
                pe.wait_ge(S("h_ready"), 8 * (r - 1) + 6)
                part(0, 8)
                norm_sums(pe, r)
                part(8, 16).then_inc(S("unit_used"), 1)
                return
            if i == 1:
                pe.wait_ge(S("h_ready"), 8 * (r - 1) + 8)
            else:
                pe.wait_ge(S("rope_raw"), n + i - 1)
            part(0, 4)
            if i == 1:
                norm_spread(pe, r)
                part(4, 12)
            rope_rot_pe(pe, i - 1, n)
            part(12 if i == 1 else 4, 16).then_inc(S("unit_used"), 1)

        def rope_rot_pe(pe, i, n):
            pair = 4 + 2 * (i % 2)
            pe.wait_ge(S("rope_raw"), n + i + 1)
            if past(n + i - 1):
                pe.wait_ge(S("rope_ready"), n + i - 1)
            if i == 0:
                pe.wait_ge(S("rbc_kept"), 4 + n // 4)
            pe.matmul(bank[:, pair, :], rope_rot, slot(X_RAW), start=True, stop=True)
            pe.matmul(bank[:, pair + 1, :], rope_rot, slot(X_RAW + 1), start=True, stop=True).then_inc(S("rot_done"), 1)

        def rope_raw_dve(dve, U, i, n, scale):
            pair = 2 * (i % 2)
            dve.wait_ge(S("unit_used"), U + i + 1)
            if past(n + i):
                dve.wait_ge(S("rope_ready"), n + i)
            dve.scalar_tensor_tensor(two(slot(X_RAW, 2)), bank[:, pair:pair + 2, :], scale, rbc2, ALU.mult, ALU.mult)\
               .then_inc(S("rope_raw"), 1)

        def rope_dve(dve, i, n, dst):
            pair = 4 + 2 * (i % 2)

            def both(k):
                return slot(k).unsqueeze(1).to_broadcast([P, 2, T])

            dve.wait_ge(S("rot_done"), n + i + 1)
            dve.wait_ge(S("trig_ready"), 2 * (n // 4) + 2)
            steps = Steps(dve, "rope_step", 2 * (n + i))
            if past(n + i):
                dve.wait_ge(S("rope_ready"), n + i)
            steps.link(dve.tensor_tensor(two(slot(X_ROT, 2)), bank[:, pair:pair + 2, :], both(X_SIN), ALU.mult))
            steps.link(dve.tensor_tensor(two(dst), two(slot(X_RAW, 2)), both(X_COS), ALU.mult))
            dve.tensor_tensor(dst, dst, slot(X_ROT, 2), ALU.add).then_inc(S("rope_ready"), 1)

        def v_unit_pe(pe, U, v):
            pe.wait_ge(S("w_lo"), U + v + 1)
            for kt in range(4):
                for t in range(TT):
                    k = 4 * (v % 2) + kt
                    ins = mm3(pe, bank[:, 4 * (v // 2) + t, :], xh[:, k, t * P:(t + 1) * P], xl[:, k, t * P:(t + 1) * P],
                              *w_block((U + v) % 2, kt * 512, 512), k == 0, k == KD - 1)
            ins.then_inc(S("unit_used"), 1)

        values = arena[:, A_V:A_V + KD * T].rearrange("p (t c) -> p t c", t=TT)

        def v_keep_act(act, U, half):
            act.wait_ge(S("unit_used"), U + 2 * half + 2)
            act.wait_ge(S("rstd_ready"), 4)
            for t in range(TT):
                ins = act.activation(values[:, t, half * 512:(half + 1) * 512], bank[:, 4 * half + t, :], ACT.Copy,
                                     scale=st[:, 16 + t:17 + t])
            ins.then_inc(S("v_kept"), 1)

        def kv_pe(pe):
            U = BASE["kv"]
            for i in range(4):
                rope_project_pe(pe, U, i, 3, 3, 0)
            pe.wait_ge(S("rope_raw"), 4)
            v_unit_pe(pe, U + 4, 0)
            rope_rot_pe(pe, 3, 0)
            v_unit_pe(pe, U + 4, 1)
            pe.wait_ge(S("rope_ready"), 4)
            v_unit_pe(pe, U + 4, 2)
            v_unit_pe(pe, U + 4, 3)

        def kv_act(act):
            U = BASE["kv"]
            trig_act(act, 0)
            for i in range(4):
                supply_hi(act, U + i + 2, (U + i) % 2)
            for v in range(4):
                if v < 3:
                    supply_hi(act, U + v + 6, (U + v) % 2)
                if v == 1:
                    v_keep_act(act, U + 4, 0)

        def keys(i):
            return arena[:, A_KT + 2 * i * T:A_KT + 2 * (i + 1) * T]

        def kv_dve(dve):
            U = BASE["kv"]
            for i in range(4):
                if i:
                    rope_dve(dve, i - 1, 0, keys(i - 1))
                rope_raw_dve(dve, U, i, 0, 1.0)
                supply_lo(dve, U + i + 2, (U + i) % 2)
            supply_lo(dve, U + 6, U % 2)
            rope_dve(dve, 3, 0, keys(3))
            supply_lo(dve, U + 7, (U + 1) % 2)
            supply_lo(dve, U + 8, U % 2)

        def q_pe(pe):
            U = BASE["q"]
            for i in range(4):
                rope_project_pe(pe, U, i, 4, 5, 4)
            rope_rot_pe(pe, 3, 4)

        def q_act(act):
            U = BASE["q"]
            trig_act(act, 1)
            for i in range(4):
                if i < 3:
                    supply_hi(act, U + i + 2, (U + i) % 2)

        def q_dve(dve):
            U = BASE["q"]
            dve.memset(slot(X_QZ, 2), 0.0).then_inc(S("qz_zero"), 1)
            for i in range(4):
                if i:
                    rope_dve(dve, i - 1, 4, slot(X_Q + 2 * i - 2, 2))
                rope_raw_dve(dve, U, i, 4, 64 ** -0.5)
                if i < 3:
                    supply_lo(dve, U + i + 2, (U + i) % 2)
            rope_dve(dve, 3, 4, slot(X_Q + 6, 2))

        ATTN_EARLY = [(u, d) for first in (4, 6) for u in range(2) for d in (first, first + 1)]

        def attn_pe(pe, hd, g, o, nxt):
            def scores(i):
                n = 4 * hd + i
                if i == 0:
                    pe.wait_ge(S("qz_ready"), 2 * hd + 2)
                if past(n - 1):
                    pe.wait_ge(S("p_ready"), n - 1)
                for m in range(2):
                    o_ = bank[:, 2 * (i % 2) + m, :]
                    pe.matmul(o_[:, i * P:(i + 1) * P], ident, causal, start=True, stop=False)
                    ins = pe.matmul(o_[:, i * P:(i + 1) * P], slot(X_QZ + m)[:, i * P:(i + 1) * P],
                                    arena[:, bass.ds(A_KT + hd * T + i * P, P)], start=False, stop=True)
                    if i:
                        ins = pe.matmul(o_[:, 0:i * P], slot(X_QZ + m)[:, i * P:(i + 1) * P],
                                        arena[:, bass.ds(A_KT + hd * T, i * P)], start=True, stop=True)
                ins.then_inc(S("sc_done"), 1)

            def turn(e, i):
                n = 4 * e + i
                pe.wait_ge(S("pc_ready"), n + 1)
                if past(n - 1):
                    pe.wait_ge(S("pt_ready"), n - 1)
                for j in range(i + 1):
                    ins = pe.transpose(bank[:, 4 + i % 2, j * P:(j + 1) * P], slot(X_P + 2 * (i % 2))[:, j * P:(j + 1) * P],
                                       ident)
                ins.then_inc(S("ptr_done"), 1)

            def weigh(e, i):
                n = 4 * e + i
                pe.wait_ge(S("pt_ready"), n + 1)
                if past(n):
                    pe.wait_ge(S("ob_ready"), n)
                for j in range(i + 1):
                    ins = pe.matmul(bank[:, 6, i * P:(i + 1) * P], slot(X_PT + i % 2)[:, j * P:(j + 1) * P],
                                    arena[:, bass.ds(A_V + j * D + e * P, P)], start=j == 0, stop=j == i)
                ins.then_inc(S("pv_done"), 1)

            for i in range(4):
                if hd is not None:
                    scores(i)
                if i < 2:
                    if g is not None:
                        turn(g, i + 2)
                elif hd is not None:
                    turn(hd, i - 2)
                if hd is None and g is not None:
                    for n in range(4 * i, 4 * i + 4):
                        early_product(pe, ATTN_EARLY, n, BASE["attn_out"], AU["attn"])
                if i == 3 and o is not None:
                    pe.wait_ge(S("aon_ready"), o + 1)
                    if past(o):
                        pe.wait_ge(S("ay_ready"), o)
                    turned(pe, 7, xn[:, 1, :]).then_inc(S("aotr_done"), 1)
                if i < 3:
                    if g is not None:
                        weigh(g, i + 1)
                elif hd is not None:
                    weigh(hd, 0)

        def attn_act(act, hd, g, o, nxt):
            def soft(i):
                n = 4 * hd + i
                act.wait_ge(S("mx_ready"), n + 1)
                if past(n - 1):
                    act.wait_ge(S("ptr_done"), n - 1)
                for m in range(2):
                    ins = act.activation(slot(X_P + 2 * (i % 2) + m)[:, 0:(i + 1) * P],
                                         bank[:, 2 * (i % 2) + m, 0:(i + 1) * P], ACT.Exp,
                                         bias=negmax[:, 2 * (i % 2) + m:2 * (i % 2) + m + 1],
                                         accum_out=rowsum[:, 2 * (i % 2) + m:2 * (i % 2) + m + 1])
                ins.then_inc(S("p_ready"), 1)

            def keep(e, i):
                n = 4 * e + i
                act.wait_ge(S("ptr_done"), n + 1)
                if past(n - 1):
                    act.wait_ge(S("pv_done"), n - 1)
                act.activation(slot(X_PT + i % 2)[:, 0:(i + 1) * P], bank[:, 4 + i % 2, 0:(i + 1) * P], ACT.Copy)\
                   .then_inc(S("pt_ready"), 1)

            def out_block(e, i):
                act.wait_ge(S("pv_done"), 4 * e + i + 1)
                if i == 0 and past(e):
                    act.wait_ge(S("aovar"), e)
                act.activation(sq[:, 0, i * P:(i + 1) * P], bank[:, 6, i * P:(i + 1) * P], ACT.Square,
                               scale=rr[:, 2 * i:2 * i + 1], accum_out=st[:, 52 + i:53 + i])
                act.activation(arena[:, bass.ds(e * T + i * P, P)], bank[:, 6, i * P:(i + 1) * P], ACT.Copy,
                               scale=rr[:, 2 * i:2 * i + 1]).then_inc(S("ob_ready"), 1)

            for i in range(4):
                if i == 3 and nxt is not None:
                    act.wait_ge(S("sc_done"), 4 * nxt)
                    if g is None:
                        act.wait_ge(S("rope_ready"), 8)
                    queries(act, nxt)
                if hd is not None:
                    soft(i)
                if i < 2:
                    if g is not None:
                        keep(g, i + 2)
                elif hd is not None:
                    keep(hd, i - 2)
                if i < 3:
                    if g is not None:
                        out_block(g, i + 1)
                elif hd is not None:
                    out_block(hd, 0)

        negmax, rowsum = st[:, 0:4], st[:, 4:8]
        rr = st[:, 84:92]
        mixer = st[:, 92:96]

        def queries(act, hd):
            for m in range(2):
                rows = slice(64 * m, 64 * m + 64)
                act.activation(slot(X_QZ + m)[rows, :], arena[rows, bass.ds((X_Q + hd) * T, T)], ACT.Copy)\
                   .then_inc(S("qz_ready"), 1)

        def attn_dve(dve, hd, g, o, nxt):
            def top(i):
                n = 4 * hd + i
                two = 2 * (i % 2)
                dve.wait_ge(S("sc_done"), n + 1)
                if past(n - 1):
                    dve.wait_ge(S("p_ready"), n - 1)
                dve.tensor_reduce(negmax[:, two:two + 2], bank[:, two:two + 2, 0:(i + 1) * P], AX.X, ALU.max,
                                  negate=True).then_inc(S("mx_ready"), 1)

            def mix(e, i):
                n = 4 * e + i
                two = 2 * (i % 2)
                p0, p1 = (slot(X_P + two + m)[:, 0:(i + 1) * P] for m in range(2))
                dve.wait_ge(S("p_ready"), n + 1)
                if past(n - 3):
                    dve.wait_ge(S("ob_ready"), n - 3)
                steps = Steps(dve, "p_step", 2 * n)
                steps.link(dve.reciprocal(rr[:, 2 * i:2 * i + 2], rowsum[:, two:two + 2]))
                steps.link(dve.scalar_tensor_tensor(mixer[:, i:i + 1], rr[:, 2 * i + 1:2 * i + 2], neglam[:, 0:1],
                                                    rowsum[:, two:two + 1], ALU.mult, ALU.mult))
                dve.scalar_tensor_tensor(p0, p1, mixer[:, i:i + 1], p0, ALU.mult, ALU.add)\
                   .then_inc(S("pc_ready"), 1)

            steps = Steps(dve, "ao_step", (RSQRT - 1) * o if o is not None else 0)
            norm = rsqrt(dve, steps, st[:, 56:60], st[:, 76:80], st[:, 80:84], "ao_rn")

            def norm_steps(count):
                if o is not None:
                    for _ in range(count):
                        next(norm)

            for i in range(4):
                if hd is not None:
                    top(i)
                if i == 0 and o is not None:
                    raw_out = arena[:, bass.ds(o * T, T)]
                    dve.wait_ge(S("aovar"), o + 1)
                if i == 0:
                    if g is not None:
                        mix(g, 3)
                elif hd is not None:
                    mix(hd, i - 1)
                if i == 0:
                    norm_steps(3)
                if i == 1:
                    norm_steps(3)
                if i == 2 and o is not None:
                    norm_steps(4)
                    dve.wait_ge(S("ao_rn"), o + 1)
                    if past(o):
                        dve.wait_ge(S("aotr_done"), o)
                    dve.tensor_tensor(c4(xn[:, 1, :]), c4(raw_out), over_t(st[:, 80:84]), ALU.mult)\
                       .then_inc(S("aon_ready"), 1)
            if g is not None:
                dve.wait_ge(S("ob_ready"), 4 * g + 4)
                dve.tensor_scalar(st[:, 56:60], st[:, 52:56], 1.0 / P, EPS, ALU.mult, ALU.add).then_inc(S("aovar"), 1)
            if o is not None:
                dve.wait_ge(S("aotr_done"), o + 1)
                dve.tensor_scalar(arena[:, bass.ds(o * T, T)], bank[:, 7, :], neglam[:, 1:2], None, ALU.mult)\
                   .then_inc(S("ay_ready"), 1)

        def lambda_dve(dve):
            dve.wait_ge(S("tables_landed"), 32)
            steps = Steps(dve, "lam_step")
            lp = arena[:, A_EARLY:A_EARLY + 256].rearrange("p (a b c) -> p a b c", a=2, b=2)
            pr = arena[:, A_EARLY + 512:A_EARLY + 640].rearrange("p (a c) -> p a c", a=2)
            steps.link(dve.tensor_tensor(pr, lp[:, :, 0, :], lp[:, :, 1, :], ALU.mult))
            dve.tensor_reduce(neglam[:, 2:4], pr, AX.X, ALU.add).then_inc(S("lam_sum"), 1)
            dve.wait_ge(S("lam_exp"), 1)
            dve.scalar_tensor_tensor(neglam[:, 0:1], neglam[:, 3:4], -LAM_INIT, neglam[:, 2:3], ALU.add, ALU.subtract)\
               .then_inc(S("lam_ready"), 1)
            dve.tensor_scalar(neglam[:, 1:2], cst[:, C_SUBLN:C_SUBLN + 1], 1.0 - LAM_INIT, None, ALU.mult)\
               .then_inc(S("lam_ready"), 1)

        AU = {"ffn0": 0, "gdn": FJ, "ffn1": FJ + U_OUT, "ffn2": 2 * FJ + U_OUT, "attn": 3 * FJ + U_OUT,
              "ffn3": 3 * FJ + 2 * U_OUT}

        DOWN_END = [BASE["ffn0"] + U_FFN, BASE["gdn_out"] + U_OUT, BASE["ffn1"] + U_FFN, BASE["ffn2"] + U_FFN,
                    BASE["attn_out"] + U_OUT, BASE["ffn3"] + U_FFN]

        @block.sync
        def _(sp):
            sp.dma_start(cst[:, :], cst_in).then_inc(S("cst_landed"), 16)
            sp.dma_start(raw[0][:, :], weights[0, :, :]).then_inc(S("raw_landed0"), 16)
            sp.dma_start(h[:, 0:2, :], xT_in[:, 0:2, :]).then_inc(S("x_landed0"), 16)
            sp.dma_start(h[:, 2:KD, :], xT_in[:, 2:KD, :]).then_inc(S("x_landed1"), 16)
            sp.dma_start(raw[1][:, :], weights[1, :, :]).then_inc(S("raw_landed1"), 16)
            sp.dma_start(arena[:, A_EARLY:A_EARLY + 384], early_in).then_inc(S("tables_landed"), 16)
            sp.dma_start(arena[:, A_GMASK:A_GMASK + 5 * P], masks_in).then_inc(S("tables_landed"), 16)
            with sp.Fori(1, N_UNITS // 2) as i:
                for n in range(2):
                    sp.wait_ge(S("w_lo"), 2 * i + n - 1)
                    sp.dma_start(raw[n][:, :], weights[bass.ds(2 * i + n, 1), :, :].rearrange("a p c -> (a p) c"))\
                      .then_inc(S(f"raw_landed{n}"), 16)
            for k in range(KD):
                sp.wait_ge(S("out_ready"), k + 1)
                sp.dma_start(out[k, :, :], slot(k)).then_inc(S("out_landed"), 16)
            sp.wait_ge(S("out_landed"), 16 * KD)

        def attention(eng, one, supply):
            one(eng, 0, None, None, 1)
            if supply is not None:
                supply(eng, BASE["q"] + 5, (BASE["q"] + 5) % 2)
            one(eng, 1, 0, None, 2)
            one(eng, 2, 1, 0, 3)
            with eng.Fori(3, H - 1) as i:
                one(eng, i, i - 1, i - 2, i + 1)
            one(eng, H - 1, H - 2, H - 3, None)

        def attention_last(eng, one):
            one(eng, None, H - 1, H - 2, None)

        def attention_end(eng, one):
            one(eng, None, None, H - 1, None)

        @block.tensor
        def _(pe):
            def ffn(f, r, b, t):
                U = BASE[f"ffn{f}"]
                ffn_pe(pe, f, t, r, b, U)
                if b == 4:
                    pe.wait_ge(S("v_kept"), 2)
                down_pe(pe, t, FJ, U + 2 * FJ, AU[f"ffn{f}"], ffn_free(f))

            pe.wait_ge(S("cst_landed"), 16)
            ffn(0, 0, 0, 0)
            gdn(pe, gdn_pe)
            gdn_last(pe, gdn_pe)
            down_pe(pe, 1, U_OUT, BASE["gdn_out"], AU["gdn"], {1: ("oc_ready", H), 2: ("y_ready", H)},
                    lambda: gdn_end(pe, gdn_pe), 2)
            ffn(1, 2, 2, 2)
            kv_pe(pe)
            pe.wait_ge(S("v_kept"), 1)
            ffn(2, 3, 4, 3)
            q_pe(pe)
            pe.wait_ge(S("rope_raw"), 8)
            attention(pe, attn_pe, None)
            attention_last(pe, attn_pe)
            down_pe(pe, 4, U_OUT, BASE["attn_out"], AU["attn"], {2: ("ob_ready", 4 * H), 3: ("ay_ready", H)},
                    lambda: attention_end(pe, attn_pe), 3)
            ffn(3, 5, 6, 5)
            norm_sums(pe, 6)
            norm_spread(pe, 6)

        @block.scalar
        def _(act):
            def ffn(f, t):
                U = BASE[f"ffn{f}"]
                ffn_act(act, f, U)
                split_a_hi(act, 0, 0, 0)
                split_a_hi(act, 1, 1, 0)
                supply_hi(act, U + 2 * FJ + 1, (U + 1) % 2)
                down_act(act, t, FJ, U + 2 * FJ, AU[f"ffn{f}"])

            act.wait_ge(S("cst_landed"), 16)
            supply_hi(act, 0, 0)
            enter_act(act, 0, 0, 0)
            act.wait_ge(S("tables_landed"), 32)
            act.activation(bahi[:, :, :].rearrange("p a b -> p (a b)"), arena[:, A_EARLY + 256:A_EARLY + 384], ACT.Copy)\
               .then_inc(S("ba_split"), 1)
            act.wait_ge(S("lam_sum"), 1)
            act.activation(neglam[:, 2:4], neglam[:, 2:4], ACT.Exp).then_inc(S("lam_exp"), 1)
            ffn(0, 0)
            enter_act(act, 1, 1, BASE["gdn_in"])
            gdn(act, gdn_act)
            act.wait_ge(S("y_ready"), 4)
            split_a_hi(act, 0, 0, 0)
            split_a_hi(act, 1, 1, 0)
            gdn_last(act, gdn_act)
            act.wait_ge(S("y_ready"), H)
            down_act(act, 1, U_OUT, BASE["gdn_out"], AU["gdn"])
            enter_act(act, 2, 2, BASE["ffn1"])
            ffn(1, 2)
            enter_act(act, 3, 3, BASE["kv"])
            kv_act(act)
            enter_act(act, 3, 4, BASE["ffn2"])
            v_keep_act(act, BASE["kv"] + 4, 1)
            ffn(2, 3)
            enter_act(act, 4, 5, BASE["q"])
            q_act(act)
            act.wait_ge(S("qz_zero"), 1)
            act.wait_ge(S("rope_ready"), 5)
            queries(act, 0)
            attention(act, attn_act, supply_hi)
            act.wait_ge(S("ay_ready"), 4)
            split_a_hi(act, 0, 0, 0)
            split_a_hi(act, 1, 1, 0)
            attention_last(act, attn_act)
            act.wait_ge(S("ay_ready"), H)
            down_act(act, 4, U_OUT, BASE["attn_out"], AU["attn"])
            enter_act(act, 5, 6, BASE["ffn3"])
            ffn(3, 5)
            for d in range(KD):
                square(act, 6, d)

        @block.gpsimd
        def _(pool):
            norm_pool(pool, 0)
            norm_pool(pool, 1)
            pool.wait_ge(S("tables_landed"), 32)
            gdn(pool, gdn_pool)
            gdn_last(pool, gdn_pool)
            norm_pool(pool, 2)
            trig_pool(pool, 0, AU["ffn1"])
            norm_pool(pool, 3)
            trig_pool(pool, 1, AU["ffn2"])
            for r in range(4, 7):
                norm_pool(pool, r)

        @block.vector
        def _(dve):
            def ffn(f, t):
                U = BASE[f"ffn{f}"]
                ffn_dve(dve, f, U, AU[f"ffn{f}"])
                down_dve(dve, FJ, U + 2 * FJ, AU[f"ffn{f}"])

            dve.wait_ge(S("cst_landed"), 16)
            enter_dve(dve, None, None, 0, 0, 0)
            dve.wait_ge(S("ba_split"), 1)
            dve.tensor_tensor(balo[:, :, :].rearrange("p a b -> p (a b)"), arena[:, A_EARLY + 256:A_EARLY + 384],
                              bahi[:, :, :].rearrange("p a b -> p (a b)").bitcast(F32), ALU.subtract)\
               .then_inc(S("ba_split"), 1)
            lambda_dve(dve)
            ffn(0, 0)
            enter_dve(dve, 0, 0.5, 1, 1, BASE["gdn_in"])
            dve.memset(pre_pad, 0.0).then_inc(S("pad_ready"), 1)
            dve.wait_ge(S("ba_done"), 1)
            dve.tensor_tensor(ba_rows[0:16, :], bank[0:16, 6, :], acc[0:16, :], ALU.mult).then_inc(S("ba_scaled"), 1)
            dve.wait_ge(S("tables_landed"), 32)
            gdn(dve, gdn_dve)
            split_a_lo(dve, 0, 0, AU["gdn"])
            split_a_lo(dve, 1, 1, AU["gdn"])
            gdn_last(dve, gdn_dve)
            gdn_end(dve, gdn_dve)
            dve.wait_ge(S("w_lo"), BASE["gdn_out"] + 2)
            down_dve(dve, U_OUT, BASE["gdn_out"], AU["gdn"])
            enter_dve(dve, 1, 1.0, 2, 2, BASE["ffn1"])
            ffn(1, 2)
            enter_dve(dve, 2, 0.5, 3, 3, BASE["kv"])
            kv_dve(dve)
            enter_dve(dve, None, None, 3, 4, BASE["ffn2"])
            ffn(2, 3)
            enter_dve(dve, 3, 0.5, 4, 5, BASE["q"])
            q_dve(dve)
            dve.wait_ge(S("lam_ready"), 2)
            attention(dve, attn_dve, supply_lo)
            split_a_lo(dve, 0, 0, AU["attn"])
            split_a_lo(dve, 1, 1, AU["attn"])
            attention_last(dve, attn_dve)
            attention_end(dve, attn_dve)
            down_dve(dve, U_OUT, BASE["attn_out"], AU["attn"])
            enter_dve(dve, 4, 1.0, 5, 6, BASE["ffn3"])
            ffn(3, 5)
            for d in range(KD):
                residual(dve, 5, d, 0.5)
            norm_dve(dve, 6)
            dve.wait_ge(S("rbc_done"), 7)
            for k in range(KD):
                dve.scalar_tensor_tensor(slot(k), h[:, k, :], cst[:, C_GAIN + 7 * KD + k:C_GAIN + 7 * KD + k + 1],
                                         bank[:, 5, :], ALU.mult, ALU.mult).then_inc(S("out_ready"), 1)


def _constants():
    import numpy as np
    p = np.arange(P)
    ident = np.eye(P)
    upper = p[:, None] <= p[None, :]
    lower = p[:, None] > p[None, :]
    diag = p[:, None] // 16 == p[None, :] // 16
    levels = []
    for w in (16, 32, 64):
        levels.append((p[:, None] // (2 * w) == p[None, :] // (2 * w)) & (p[:, None] % (2 * w) < w)
                      & (p[None, :] % (2 * w) >= w))
    half = ROPE_DIM // 2
    rot = np.zeros((P, P))
    freq = np.zeros(P, np.float32)
    inv = (np.float32(1.0) / (np.float32(ROPE_THETA) ** (np.arange(half, dtype=np.float32) / np.float32(half))))
    for m in range(P):
        f = m % 64
        if f < half:
            rot[m + half, m] = -1.0
        elif f < ROPE_DIM:
            rot[m - half, m] = 1.0
        if f < ROPE_DIM:
            freq[m] = inv[f % half]
    causal = np.where(p[None, :] <= p[:, None], 0.0, -1.0e30)
    cst = np.concatenate([ident, np.ones((P, P)), upper, rot, causal], 1).astype(np.float32)
    masks = np.concatenate([lower, diag, *levels], 1).astype(np.float32)
    return cst, masks, freq


def kernel(**inputs):
    import numpy as np
    import concourse.bacc as bacc
    from concourse.bass_utils import run_bass_kernel_spmd

    a = {k: np.asarray(v) for k, v in inputs.items()}

    def cols(w):
        return w.reshape(KD, P, -1, 256).transpose(2, 1, 0, 3).reshape(-1, P, UNIT)

    def rows(w):
        return w.reshape(-1, 2, P, D).transpose(0, 2, 1, 3).reshape(-1, P, UNIT)

    def ffn(gu, dn):
        both = np.stack([cols(gu[:, :FF]), cols(gu[:, FF:])], 1).reshape(-1, P, UNIT)
        return [both, rows(dn)]

    w_in = a["gdn_w_in"][0]
    q, k, v, z = (w_in[:, n * D:(n + 1) * D].reshape(D, H, P) for n in range(4))
    per_head = np.stack([q, k, v, z], 2).reshape(D, H * 4 * P)
    kv = a["kv_w"]
    v_units = kv[:, D:].reshape(2, 4, P, 2, 512).transpose(3, 0, 2, 1, 4).reshape(4, P, UNIT)
    f1u, f1d, f2u, f2d = (a[n] for n in ("ffn1_w_gate_up", "ffn1_w_down", "ffn2_w_gate_up", "ffn2_w_down"))
    units = [*ffn(f1u[0], f1d[0]), cols(per_head), rows(a["gdn_w_out"][0]), *ffn(f2u[0], f2d[0]),
             cols(kv[:, :D]), v_units, *ffn(f1u[1], f1d[1]), cols(a["diff_w_q"][0]), rows(a["diff_w_out"][0]),
             *ffn(f2u[1], f2d[1])]
    weights = np.concatenate(units, 0)
    assert weights.shape[0] == N_UNITS

    cst, masks, freq = _constants()
    gains = np.stack([a["ffn1_norm"][0], a["mix_norm"][0], a["ffn2_norm"][0], a["kv_norm"], a["ffn1_norm"][1],
                      a["mix_norm"][1], a["ffn2_norm"][1], a["final_norm"]])
    gains = gains.reshape(8, KD, P).transpose(2, 0, 1).reshape(P, 8 * KD)
    conv = a["gdn_conv"][0].reshape(4, 3, H, P).transpose(3, 2, 1, 0).reshape(P, H * 12)

    def on_all(v):
        return np.broadcast_to(v.reshape(1, -1), (P, v.size))

    cst = np.concatenate([cst, gains, conv, on_all(a["gdn_a_log"]), on_all(a["gdn_dt_bias"]),
                          a["gdn_out_norm"].reshape(P, 1), a["diff_subln"].reshape(P, 1), freq.reshape(P, 1)], 1)
    w_ba = w_in[:, 4 * D:].reshape(KD, P, 16).transpose(1, 0, 2).reshape(P, KD * 16)
    early = np.concatenate([on_all(a["diff_lambda"]), w_ba], 1)
    xT = a["x"][0].T.reshape(KD, P, T).transpose(1, 0, 2)
    pos = on_all(a["positions"])

    nc = bacc.Bacc("TRN2", target_bir_lowering=False, num_devices=1)
    arrays, aps = {}, []
    for name, arr in (("weights", weights), ("cst_in", cst), ("masks_in", masks), ("early_in", early),
                      ("xT_in", xT), ("pos_in", pos)):
        arr = np.ascontiguousarray(arr)
        arrays[name] = arr
        aps.append(nc.dram_tensor(name, arr.shape, mybir.dt.from_np(arr.dtype), kind="ExternalInput").ap())
    out = nc.dram_tensor("outT", (KD, P, T), F32, kind="ExternalOutput").ap()
    trunk_kernel(nc, *aps, out)
    r = run_bass_kernel_spmd(nc, [arrays], core_ids=[0])
    return np.ascontiguousarray(r.results[0]["outT"].reshape(D, T).T).reshape(1, T, D)
```
